# Optimizing a Trainium2 kernel written in Bass

```python
import jax, jax.numpy as jnp
from jax import lax
import numpy as np

D_MODEL = 1024
BATCH = 1
SEQ = 1024
DEPTH = 1

A_W = D_MODEL // 2
CONV_A = 31
B_W = D_MODEL // 2
CONV_B = 3
C_HEADS = 8
C_HEAD_DIM = 64
C_W = C_HEADS * C_HEAD_DIM
Q_BLOCK = 128
M_HEADS = 4
M_HEAD_DIM = 64
M_W = M_HEADS * M_HEAD_DIM
MEM_LEN = 256
N_BRANCH = 4
ALPHA = (2.0 * DEPTH) ** 0.25
BETA = (8.0 * DEPTH) ** -0.25
LN_EPS = 1e-5

SPLITS = (
    2 * A_W, A_W,
    B_W, B_W, B_W, B_W,
    C_W, C_W, C_W, C_HEADS, C_W,
    M_W, M_W,
    N_BRANCH * D_MODEL,
)
IN_COLS = sum(SPLITS)
SPLIT_CUTS = tuple(int(c) for c in np.cumsum(SPLITS)[:-1])

kernel_name = 'hybrid_gated_conformer_shortconv_fox_memxattn'

def _layer_norm(x, g, b):
    xf = x.astype(jnp.float32)
    mu = jnp.mean(xf, axis=-1, keepdims=True)
    var = jnp.mean(jnp.square(xf - mu), axis=-1, keepdims=True)
    y = ((xf - mu) * lax.rsqrt(var + LN_EPS)).astype(x.dtype)
    return y * g + b

def _causal_dwconv(x, w):
    k_width, ch = w.shape
    return lax.conv_general_dilated(
        x, w[:, None, :].astype(x.dtype), window_strides=(1,),
        padding=[(k_width - 1, 0)],
        dimension_numbers=('NWC', 'WIO', 'NWC'),
        feature_group_count=ch)

def _forgetting_attention(q, k, v, logf):
    bsz, seq, heads, dh = q.shape
    scale = dh ** -0.5
    cum = jnp.cumsum(logf, axis=1).transpose(0, 2, 1)
    outs = []
    for i in range(seq // Q_BLOCK):
        q0, end = i * Q_BLOCK, (i + 1) * Q_BLOCK
        s = jnp.einsum('bqhd,bkhd->bhqk', q[:, q0:end], k[:, :end]).astype(jnp.float32) * scale
        decay = cum[:, :, q0:end, None] - cum[:, :, None, :end]
        q_pos = q0 + jnp.arange(Q_BLOCK)
        k_pos = jnp.arange(end)
        causal = q_pos[:, None] >= k_pos[None, :]
        s = jnp.where(causal, s + decay, -jnp.inf)
        p = jax.nn.softmax(s, axis=-1).astype(v.dtype)
        outs.append(jnp.einsum('bhqk,bkhd->bqhd', p, v[:, :end]))
    return jnp.concatenate(outs, axis=1)

def _cross_attention(q, k, v):
    dh = q.shape[-1]
    s = jnp.einsum('bshd,bmhd->bhsm', q, k).astype(jnp.float32) * (dh ** -0.5)
    p = jax.nn.softmax(s, axis=-1).astype(v.dtype)
    return jnp.einsum('bhsm,bmhd->bshd', p, v)

def setup_inputs(seed: int = 0) -> dict:
    key = jax.random.key(seed)
    ks = jax.random.split(key, 20)
    f32 = jnp.float32
    nrm = lambda k, shape, scale: jax.random.normal(k, shape, f32) * scale
    return {
        'x': nrm(ks[0], (BATCH, SEQ, D_MODEL), 1.0),
        'mem': nrm(ks[1], (BATCH, MEM_LEN, D_MODEL), 1.0),
        'w_in': nrm(ks[2], (DEPTH, D_MODEL, IN_COLS), D_MODEL ** -0.5),
        'b_forget': jax.random.uniform(ks[3], (DEPTH, C_HEADS), f32, 1.0, 5.0),
        'conv_a_w': nrm(ks[4], (DEPTH, CONV_A, A_W), CONV_A ** -0.5),
        'conv_a_b': nrm(ks[5], (DEPTH, A_W), 0.02),
        'ln_a_g': 1.0 + nrm(ks[6], (DEPTH, A_W), 0.05),
        'ln_a_b': nrm(ks[7], (DEPTH, A_W), 0.02),
        'conv_b_w': nrm(ks[8], (DEPTH, CONV_B, B_W), CONV_B ** -0.5),
        'w_kv_mem': nrm(ks[9], (DEPTH, D_MODEL, 2 * M_W), D_MODEL ** -0.5),
        'mem_ln_g': 1.0 + nrm(ks[10], (D_MODEL,), 0.05),
        'mem_ln_b': nrm(ks[11], (D_MODEL,), 0.02),
        'p_a': nrm(ks[12], (DEPTH, A_W, D_MODEL), BETA * A_W ** -0.5),
        'p_b': nrm(ks[13], (DEPTH, B_W, D_MODEL), BETA * B_W ** -0.5),
        'p_c': nrm(ks[14], (DEPTH, C_W, D_MODEL), BETA * C_W ** -0.5),
        'p_m': nrm(ks[15], (DEPTH, M_W, D_MODEL), BETA * M_W ** -0.5),
        'w_out': nrm(ks[16], (DEPTH, D_MODEL, D_MODEL), BETA * D_MODEL ** -0.5),
        'ln_g': 1.0 + nrm(ks[17], (DEPTH, D_MODEL), 0.05),
        'ln_b': nrm(ks[18], (DEPTH, D_MODEL), 0.02),
    }

def reference(x, mem, w_in, b_forget, conv_a_w, conv_a_b, ln_a_g, ln_a_b, conv_b_w,
              w_kv_mem, mem_ln_g, mem_ln_b, p_a, p_b, p_c, p_m, w_out, ln_g, ln_b):
    bsz, seq, _ = x.shape
    mem_n = _layer_norm(mem, mem_ln_g, mem_ln_b)
    for l in range(DEPTH):
        proj = x @ w_in[l]
        (a_glu, a_gate, b_h, b_b, b_c, b_gate, c_q, c_k, c_v, c_f, c_gate,
         m_q, m_gate, g) = jnp.split(proj, SPLIT_CUTS, axis=-1)

        a_u, a_v = jnp.split(a_glu, 2, axis=-1)
        a = _causal_dwconv(a_u * jax.nn.sigmoid(a_v), conv_a_w[l]) + conv_a_b[l]
        a = jax.nn.silu(_layer_norm(a, ln_a_g[l], ln_a_b[l]))
        y_a = (a * jax.nn.silu(a_gate)) @ p_a[l]

        hb = b_b * _causal_dwconv(b_c * b_h, conv_b_w[l])
        y_b = (hb * jax.nn.silu(b_gate)) @ p_b[l]

        q = c_q.reshape(bsz, seq, C_HEADS, C_HEAD_DIM)
        k = c_k.reshape(bsz, seq, C_HEADS, C_HEAD_DIM)
        v = c_v.reshape(bsz, seq, C_HEADS, C_HEAD_DIM)
        logf = jax.nn.log_sigmoid((c_f + b_forget[l]).astype(jnp.float32))
        o_c = _forgetting_attention(q, k, v, logf).reshape(bsz, seq, C_W)
        y_c = (o_c * jax.nn.silu(c_gate)) @ p_c[l]

        mk, mv = jnp.split(mem_n @ w_kv_mem[l], 2, axis=-1)
        o_m = _cross_attention(
            m_q.reshape(bsz, seq, M_HEADS, M_HEAD_DIM),
            mk.reshape(bsz, MEM_LEN, M_HEADS, M_HEAD_DIM),
            mv.reshape(bsz, MEM_LEN, M_HEADS, M_HEAD_DIM)).reshape(bsz, seq, M_W)
        y_m = (o_m * jax.nn.silu(m_gate)) @ p_m[l]

        gates = jax.nn.sigmoid(g.reshape(bsz, seq, N_BRANCH, D_MODEL))
        merged = (gates[:, :, 0] * y_a + gates[:, :, 1] * y_b
                  + gates[:, :, 2] * y_c + gates[:, :, 3] * y_m)
        out = merged @ w_out[l]

        x = _layer_norm(ALPHA * x + out, ln_g[l], ln_b[l])
    return x


_drawn_inputs = setup_inputs


def setup_inputs(seed=0):
    import zlib

    import numpy as np

    out = dict(_drawn_inputs(seed))
    spreads = {}
    factors = {'mem': 5.878,
     'b_forget': 188.16,
     'conv_a_b': 64.0,
     'ln_a_g': 200.0,
     'ln_a_b': 200.0,
     'w_kv_mem': 5.636,
     'mem_ln_g': 8.0,
     'mem_ln_b': 22.44,
     'p_m': 5.514,
     'ln_b': 2.909,
     'conv_a_w': 2.865,
     'conv_b_w': 8.0,
     'p_b': 8.0,
     'p_c': 64.0}
    for name, (base, spread) in spreads.items():
        noise = np.random.default_rng([zlib.crc32(name.encode()), seed]).standard_normal(out[name].shape)
        drawn = base * np.exp(spread * noise) if base else spread * noise
        out[name] = __import__('jax').numpy.asarray(drawn.astype(out[name].dtype))
    for name, factor in factors.items():
        out[name] = (out[name] * factor).astype(out[name].dtype)
    return out
```

```python
from contextlib import ExitStack

import concourse.bass as bass
from concourse import mybir

F32 = mybir.dt.float32
F32R = mybir.dt.float32r
ACT = mybir.ActivationFunctionType
ALU = mybir.AluOpType
AX = mybir.AxisListType

P = 128
BIG = 1.0e30


def hybrid_mixer(nc, xT, x, mem, w_in, b_forget, conv_a_wT, conv_a_b, ln_a_g, ln_a_b, conv_b_wT,
                 w_kv_mem, mem_ln_g, mem_ln_b, p_a, p_b, p_c, p_m, w_out, ln_g, ln_b, out):
    D, T = xT.shape
    KT = D // P
    HALF = T // 2
    NT = T // P
    DT = D // P
    CONV_A, A_W = conv_a_wT.shape[1], conv_a_wT.shape[0]
    CONV_B, B_W = conv_b_wT.shape[1], conv_b_wT.shape[0]
    PAD_A, PAD_B = CONV_A - 1, CONV_B - 1
    HEADS = b_forget.shape[0]
    DH = 64
    C_W = HEADS * DH
    MEM = mem.shape[0]
    MT = MEM // P
    M_W = w_kv_mem.shape[1] // 2
    M_HEADS = M_W // DH
    CT = A_W // P
    MP = M_W // P
    QSCALE = DH ** -0.5
    ALPHA = 2.0 ** 0.25
    EPS = 1e-5
    assert A_W == B_W == C_W == CT * P and CT == 4 and NT == 8 and MT == 2 and MP == 2

    col, at = {}, 0
    for name, width in (("a_u", A_W), ("a_v", A_W), ("a_gate", A_W), ("b_h", B_W), ("b_b", B_W), ("b_c", B_W),
                        ("b_gate", B_W), ("q", C_W), ("k", C_W), ("v", C_W), ("f", HEADS), ("c_gate", C_W),
                        ("m_q", M_W), ("m_gate", M_W), ("g", 4 * D)):
        col[name] = at
        at += width
    assert at == w_in.shape[1]

    S_C = 0
    S_M = S_C + 4 * CT
    S_A = S_M + 2 * MP
    S_GC = S_A + 2 * CT
    S_GM = S_GC + 2 * DT
    S_B = S_GM + 2 * DT
    S_GB = S_B + 4 * CT
    S_AG = S_GB + 2 * DT
    S_GA = S_AG + CT
    S_END = S_GA + 2 * DT

    BASE = (nc.sbuf_base + 63) // 64 * 64
    KB = 1024

    def at_(name, shape, dt, off):
        return nc.alloc_sbuf_tensor_at(name, shape, dt, offset=BASE + off)

    xT_hi = at_("xT_hi", [P, KT, T], F32R, 0)
    xT_lo = at_("xT_lo", [P, KT, T], F32R, 32 * KB)
    w_raw = at_("w_raw", [P, 2, KT, P], F32, 64 * KB)
    w_hi = at_("w_hi", [P, 2, KT, P], F32R, 72 * KB)
    w_lo = at_("w_lo", [P, 2, KT, P], F32R, 80 * KB)
    z_hi = at_("z_hi", [P, CT, T], F32R, 88 * KB)
    z_lo = at_("z_lo", [P, CT, T], F32R, 104 * KB)
    x_raw = at_("x_raw", [P, KT, T], F32, 88 * KB)
    wkv = at_("wkv", [P, KT, 2 * M_W], F32, 120 * KB)
    memT = at_("memT", [P, KT, MEM], F32, 136 * KB)
    mem_sb = at_("mem_sb", [P, MT, D], F32, 144 * KB)
    wf_stack = at_("wf_stack", [P, KT, P], F32R, 152 * KB)
    negcum = at_("negcum", [HEADS, T], F32, 156 * KB)
    f_z = at_("f_z", [HEADS, T], F32, 160 * KB)
    f_abs = at_("f_abs", [HEADS, T], F32, 164 * KB)
    f_e = at_("f_e", [HEADS, T], F32, 168 * KB)
    f_u = at_("f_u", [HEADS, T], F32, 172 * KB)
    f_r = at_("f_r", [HEADS, T], F32, 176 * KB)
    f_l = at_("f_l", [HEADS, T], F32, 180 * KB)
    q_stack = at_("q_stack", [P, 2, T], F32R, 120 * KB)
    k_stack_hi = at_("k_stack_hi", [P, 2, T], F32R, 128 * KB)
    k_stack_lo = at_("k_stack_lo", [P, 2, T], F32R, 136 * KB)
    v_stack = at_("v_stack", [P, 2, NT, 2, DH], F32R, 144 * KB)
    bias = at_("bias", [P, 2, T], F32, 152 * KB)
    probs = at_("probs", [P, 2, T], F32, 160 * KB)
    v_raw = at_("v_raw", [P, T], F32, 160 * KB)
    k_raw = at_("k_raw", [P, T], F32, 164 * KB)
    pT_hi = at_("pT_hi", [P, NT, 2 * P], F32R, 168 * KB)
    pT_lo = at_("pT_lo", [P, NT, 2 * P], F32R, 176 * KB)
    q_raw = at_("q_raw", [P, T], F32, 172 * KB)
    km_hi = at_("km_hi", [P, M_HEADS, MEM], F32R, 184 * KB)
    km_lo = at_("km_lo", [P, M_HEADS, MEM], F32R, 188 * KB)
    vm_stack = at_("vm_stack", [P, MT, M_HEADS, 2, DH], F32R, 192 * KB)
    xt = at_("xt", [P, T], F32, 196 * KB)
    sg = at_("sg", [P, T], F32, 200 * KB)
    zm_hi = at_("zm_hi", [P, MP, T], F32R, 128 * KB)
    zm_lo = at_("zm_lo", [P, MP, T], F32R, 136 * KB)
    WA = PAD_A + T
    glu = at_("glu", [P, CT, WA], F32, 144 * KB)
    merged = at_("merged", [P, DT, T], F32, 162 * KB)
    ytmp = at_("ytmp", [P, 2, T], F32, 120 * KB)
    prod = at_("prod", [P, PAD_B + T], F32, 128 * KB)
    cv = at_("cv", [P, T], F32, 133 * KB)
    bz = at_("bz", [P, T], F32, 137 * KB)
    wout_hi = at_("wout_hi", [P, KT, D], F32R, 128 * KB)
    wout_lo = at_("wout_lo", [P, KT, D], F32R, 88 * KB)
    lng_b = at_("lng_b", [P, D], F32, 120 * KB)
    lnb_b = at_("lnb_b", [P, D], F32, 124 * KB)
    x_tok = at_("x_tok", [P, 2, D], F32, 162 * KB)
    y_tok = at_("y_tok", [P, 2, D], F32, 170 * KB)
    off = [204 * KB]

    def small(name, shape, dt=F32):
        n = 4
        for d in shape[1:]:
            n *= d
        t = nc.alloc_sbuf_tensor_at(name, shape, dt, offset=BASE + off[0], align_bytes=8)
        off[0] += (n + 7) // 8 * 8
        return t

    ident = small("ident", [P, P])
    otmp = small("otmp", [P, 2 * P])
    maskc = small("maskc", [P, P])
    bdiag = small("bdiag", [P, 2, P])
    cwk = small("cwk", [P, CONV_A + 1])
    cwa = small("cwa", [P, CT, CONV_A])
    cwb = small("cwb", [P, CT, CONV_B])
    cab = small("cab", [P, CT])
    lag = small("lag", [P, CT])
    lab = small("lab", [P, CT])
    eps = small("eps", [P, 1])
    rmin = small("rmin", [P, 2, 2])
    rsum = small("rsum", [P, 2, 2])
    rinv = small("rinv", [P, 2, 2])
    mv = small("mv", [P, 2, 2])
    rstd = small("rstd", [P, 2])
    wf_raw = at_("wf_raw", [P, KT, HEADS], F32, 184 * KB)
    memg = at_("memg", [P, KT], F32, 188 * KB)
    memb = at_("memb", [P, KT], F32, 188 * KB + 32)
    bf = at_("bf", [HEADS, 1], F32, 188 * KB + 64)
    stats = at_("stats", [P, 2, 2, 6], F32, 195 * KB)
    ones_ln = at_("ones_ln", [P, P], F32, 132 * KB + 512)
    assert BASE + off[0] <= nc.sbuf_usable_end, (BASE + off[0], nc.sbuf_usable_end)

    cum_dram = nc.dram_tensor("cum_scratch", [HEADS, T], F32, kind="Internal").ap()

    ctx = ExitStack()
    with ctx:
        pj = ctx.enter_context(nc.psum_tensor("pj", [P, 4, HALF], F32))
        pt = ctx.enter_context(nc.psum_tensor("pt", [P, 2, HALF], F32))
        po = ctx.enter_context(nc.psum_tensor("po", [P, 2, HALF], F32))

        def sem(name):
            return ctx.enter_context(nc.semaphore(name))

        s_passed = [sem("vector_passed"), sem("sync_passed")]
        s_x = [sem(f"x_loaded{i}") for i in range(4)]
        s_par = sem("params_loaded")
        s_wf = sem("wf_loaded")
        s_mem = sem("mem_loaded")
        s_wkv = sem("wkv_loaded")
        s_cst = sem("constants_made")
        s_fix = sem("small_setup_done")
        s_xhi = sem("x_hi_made")
        s_xlo = sem("x_lo_made")
        s_wld = [sem(f"w_raw_loaded{i}") for i in range(2)]
        s_whi = sem("w_hi_made")
        s_wlo = sem("w_lo_made")
        s_pj = sem("half_accumulated")
        s_pjfree = sem("half_evacuated")
        s_xt = sem("xt_written")
        s_wfs = sem("wf_stack_made")
        s_f = sem("f_accumulated")
        s_fa = sem("f_scalar_steps")
        s_fv = sem("f_vector_steps")
        s_cumst = sem("cum_stored")
        s_ms = sem("mem_stats")
        s_mr = sem("mem_std")
        s_mn = sem("mem_normalised")
        s_mt = sem("mem_transposed")
        s_mte = sem("memT_written")
        s_kv = sem("mem_kv_accumulated")
        s_kvh = sem("mem_kv_hi_made")
        s_kvl = sem("mem_kv_lo_made")
        s_bias = [sem(f"bias_loaded{a}") for a in range(2)]
        s_stkh = sem("stack_hi_made")
        s_stkl = sem("stack_lo_made")
        s_s = sem("scores_ready")
        s_bd = sem("diag_bias_made")
        s_dm = sem("diag_min")
        s_sp = sem("scores_biased")
        s_e = sem("probs_exp")
        s_ri = sem("row_sum_inverted")
        s_pn = sem("probs_normalised")
        s_tb = sem("transposed")
        s_thi = sem("pT_hi_made")
        s_tlo = sem("pT_lo_made")
        s_pv = sem("pv_accumulated")
        s_osh = sem("o_half_shifted")
        s_oadd = sem("o_halves_added")
        s_og = sem("o_gated")
        s_zpre = sem("z_product_made")
        s_zhi = sem("z_hi_made")
        s_zlo = sem("z_lo_made")
        s_cw = sem("conv_weights_ready")
        s_ca = sem("conv_steps")
        s_cb = sem("convb_steps")
        s_bt = sem("b_times_conv")
        s_yt = sem("gated_y_made")
        s_add = sem("branch_added")
        s_lnm = sem("ln_mean_accumulated")
        s_lnc = sem("ln_centred")
        s_sq = sem("ln_squared")
        s_lnv = sem("ln_var_accumulated")
        s_sd = sem("ln_std")
        s_rs = sem("ln_rstd")
        s_an = sem("a_scaled")
        s_ag = sem("a_affine")
        s_at = sem("a_tanh")
        s_as = sem("a_silu_made")
        s_woh = sem("wout_hi_made")
        s_wol = sem("wout_lo_made")
        s_gh = sem("merged_hi_made")
        s_gl = sem("merged_lo_made")
        s_lnp = sem("ln_params_loaded")
        s_xtk = [sem(f"x_tok_loaded{i}") for i in range(2)]
        s_out_pj = sem("out_half_accumulated")
        s_yk = sem("residual_added")
        s_st = sem("out_stats")
        s_mvr = sem("out_mean_var")
        s_osd = sem("out_std")
        s_ors = sem("out_rstd")
        s_t1 = sem("out_centred")
        s_yo = sem("out_ready")
        s_store = [sem(f"out_stored{i}") for i in range(2)]

        block = ctx.enter_context(nc.Block())

        F_STEPS = 10
        STK_PAIR = 6
        CONV_STEPS = 1 + 2 * CT * CONV_A
        X_M = 2 * CT
        X_A = X_M + 2 * MP
        X_GC = X_A + 2 * CT
        X_GM = X_GC + 2 * DT
        X_B = X_GM + 2 * DT
        X_GB = X_B + 4 * CT
        X_AG = X_GB + 2 * DT
        X_GA = X_AG + 2 * CT
        UNITS = 2 * NT

        def batches(i):
            first, last = 1 - i % 2, 2 * (i // 2) + 1
            slots = list(range(first, last + 1))
            return [slots[n:n + 4] for n in range(0, len(slots), 4)]

        TB_HEAD = sum(len(batches(i)) for i in range(NT))
        TB_PAIR = 2 + 2 * TB_HEAD

        def tb_before(u):
            return 2 + (u // NT) * TB_HEAD + sum(len(batches(i)) for i in range(u % NT))

        PV_PAIR = 2 * (NT // 2)
        assert TB_PAIR % 2 == 0

        def raw_count(s_half, j):
            return 16 * (s_half + j // 2 + 1)

        @block.sync
        def _(sp):
            def load_w(s, j, src, nk):
                sp.wait_ge(s_wlo, s - 1)
                sp.sem_inc(s_passed[1], 1)
                sp.dma_start(w_raw[:, j % 2, 0:nk, :], src).then_inc(s_wld[j % 2], 16)

            def wcols(c0):
                if not isinstance(c0, int):
                    c0 = sp.snap(c0)
                return w_in[:, bass.ds(c0, P)].rearrange("(k p) c -> p k c", p=P)

            def pcols(w, dt):
                return w[:, bass.ds(sp.snap(dt * P), P)].rearrange("(k p) c -> p k c", p=P)

            xv = xT.rearrange("(k p) t -> p k t", p=P)
            sp.dma_start(wf_raw[:, :, :], w_in[:, col["f"]:col["f"] + HEADS].rearrange("(k p) c -> p k c", p=P)
                         ).then_inc(s_wf, 16)
            for i in range(4):
                sp.dma_start(x_raw[:, 2 * i:2 * i + 2, :], xv[:, 2 * i:2 * i + 2, :]).then_inc(s_x[i], 16)
            sp.dma_start(mem_sb[:, :, :], mem.rearrange("(m p) d -> p m d", p=P)).then_inc(s_mem, 16)
            sp.dma_start(w_raw[:, 0, :, :], wcols(col["q"])).then_inc(s_wld[0], 16)
            sp.dma_start(wkv[:, :, :], w_kv_mem.rearrange("(k p) c -> p k c", p=P)).then_inc(s_wkv, 16)
            sp.dma_start(w_raw[:, 1, :, :], wcols(col["k"])).then_inc(s_wld[1], 16)
            for t, src in ((cwa[:, :, :], conv_a_wT.rearrange("(c p) k -> p c k", p=P)),
                           (cwb[:, :, :], conv_b_wT.rearrange("(c p) k -> p c k", p=P)),
                           (cab[:, :], conv_a_b),
                           (lag[:, :], ln_a_g),
                           (lab[:, :], ln_a_b),
                           (memg[:, :], mem_ln_g),
                           (memb[:, :], mem_ln_b),
                           (bf[:, :], b_forget.rearrange("(h o) -> h o", o=1))):
                sp.dma_start(t, src).then_inc(s_par, 16)
            sp.wait_ge(s_fv, F_STEPS)
            sp.dma_start(cum_dram[:, :], negcum[:, :]).then_inc(s_cumst, 16)
            sp.wait_ge(s_cumst, 16)
            for a in range(2):
                sp.dma_start(bias[:, a, :], cum_dram[a, :].partition_broadcast(P)).then_inc(s_bias[a], 16)

            def pair_loads(c, last):
                s = 4 * c
                load_w(s + 2, 2, wcols(col["v"] + c * P), KT)
                load_w(s + 3, 3, wcols(col["c_gate"] + c * P), KT)
                if last:
                    return
                load_w(s + 4, 4, wcols(col["q"] + (c + 1) * P), KT)
                load_w(s + 5, 5, wcols(col["k"] + (c + 1) * P), KT)
                for a in range(2):
                    sp.wait_ge(s_sp, UNITS * c + NT * (a + 1))
                    sp.sem_inc(s_passed[1], 1)
                    sp.dma_start(bias[:, a, :], cum_dram[2 * c + 2 + a, :].partition_broadcast(P)
                                 ).then_inc(s_bias[a], 16)

            with sp.Fori(0, CT - 1) as c:
                pair_loads(c, False)
            pair_loads(CT - 1, True)
            for m in range(MP):
                load_w(S_M + 2 * m, 0, wcols(col["m_q"] + m * P), KT)
                load_w(S_M + 2 * m + 1, 1, wcols(col["m_gate"] + m * P), KT)
            with sp.Fori(0, CT) as ct:
                load_w(S_A + 2 * ct, 0, wcols(col["a_v"] + ct * P), KT)
                load_w(S_A + 2 * ct + 1, 1, wcols(col["a_u"] + ct * P), KT)

            def merge_loads(s0, branch, w, nk):
                with sp.Fori(0, DT) as dt:
                    load_w(s0 + 2 * dt, 0, wcols(col["g"] + branch * D + dt * P), KT)
                    load_w(s0 + 2 * dt + 1, 1, pcols(w, dt), nk)

            merge_loads(S_GC, 2, p_c, CT)
            merge_loads(S_GM, 3, p_m, MP)
            with sp.Fori(0, CT) as ct:
                for j, name in enumerate(("b_c", "b_h", "b_gate", "b_b")):
                    load_w(S_B + 4 * ct + j, j, wcols(col[name] + ct * P), KT)
            merge_loads(S_GB, 1, p_b, CT)
            with sp.Fori(0, CT // 2) as i:
                for j in range(2):
                    load_w(S_AG + 2 * i + j, j, wcols(col["a_gate"] + (2 * i + j) * P), KT)
            merge_loads(S_GA, 0, p_a, CT)
            wo_v = w_out.rearrange("(k p) c -> k p c", p=P)
            for k in range(KT):
                s = S_END + k
                if k < 2:
                    sp.wait_ge(s_wlo, s - 1)
                else:
                    sp.wait_ge(s_wol, k - 1)
                sp.dma_start(w_raw[:, k % 2, :, :].rearrange("p a b -> p (a b)"), wo_v[k]).then_inc(s_wld[k % 2], 16)
            sp.wait_ge(s_add, 3 * DT)
            sp.dma_start(lng_b[:, :], ln_g.partition_broadcast(P)).then_inc(s_lnp, 16)
            sp.dma_start(lnb_b[:, :], ln_b.partition_broadcast(P)).then_inc(s_lnp, 16)
            sp.wait_ge(s_gl, DT)
            for t in range(NT):
                if t >= 2:
                    sp.wait_ge(s_yk, 2 * (t - 1))
                sp.dma_start(x_tok[:, t % 2, :], x[t * P:(t + 1) * P, :]).then_inc(s_xtk[t % 2], 16)
                if t >= 1:
                    sp.wait_ge(s_yo, t)
                    sp.dma_start(out[(t - 1) * P:t * P, :], y_tok[:, (t - 1) % 2, :]).then_inc(s_store[(t - 1) % 2], 16)
            sp.wait_ge(s_yo, NT)
            sp.dma_start(out[(NT - 1) * P:NT * P, :], y_tok[:, (NT - 1) % 2, :]).then_inc(s_store[(NT - 1) % 2], 16)
            for i in range(2):
                sp.wait_ge(s_store[i], 16 * (NT // 2))

        @block.tensor
        def _(pe):
            def stream_tile(s, j, nk=KT, r_hi=xT_hi, r_lo=xT_lo, free=True):
                pe.wait_ge(s_wlo, s + 1)
                for h in range(2):
                    if free:
                        pe.wait_ge(s_pjfree, 2 * s + h - 3)
                    b = 2 * (j % 2) + h
                    t = slice(h * HALF, (h + 1) * HALF)
                    for k in range(nk):
                        nc.tensor.matmul(pj[:, b, :], w_hi[:, j % 2, k, :], r_hi[:, k, t], start=k == 0, stop=False)
                        nc.tensor.matmul(pj[:, b, :], w_hi[:, j % 2, k, :], r_lo[:, k, t], start=False, stop=False)
                        mm = nc.tensor.matmul(pj[:, b, :], w_lo[:, j % 2, k, :], r_hi[:, k, t],
                                              start=False, stop=k == nk - 1)
                    mm.then_inc(s_pj, 1)

            pe.wait_ge(s_wfs, 2)
            for h in range(2):
                for k in range(KT):
                    if h == 0:
                        pe.wait_ge(s_xlo, k + 1)
                    for n, r in enumerate((xT_hi, xT_lo)):
                        mm = nc.tensor.matmul(po[:, h, :], wf_stack[:, k, :], r[:, k, h * HALF:(h + 1) * HALF],
                                              start=k == 0 and n == 0, stop=k == KT - 1 and n == 1)
                mm.then_inc(s_f, 1)
            pe.wait_ge(s_cst, 2)
            n = 0
            for m in range(MT):
                pe.wait_ge(s_mn, m + 1)
                for kb in range(KT // 4):
                    if n >= 2:
                        pe.wait_ge(s_mte, n - 1)
                    for k in range(4):
                        mm = nc.tensor.transpose(pt[:, n % 2, k * P:(k + 1) * P],
                                                 mem_sb[:, m, (4 * kb + k) * P:(4 * kb + k + 1) * P], ident[:, :])
                    mm.then_inc(s_mt, 1)
                    n += 1
            pe.wait_ge(s_mte, n)
            pe.wait_ge(s_wkv, 16)
            pe.wait_ge(s_fv, 1)
            for c in range(MP):
                for k in range(KT):
                    mm = nc.tensor.matmul(po[:, c, 0:MEM], wkv[:, k, c * P:(c + 1) * P], memT[:, k, :],
                                          start=k == 0, stop=k == KT - 1)
                mm.then_inc(s_kv, 1)
            for m in range(MT):
                for k in range(KT):
                    mm = nc.tensor.matmul(pt[:, m, 0:M_W], memT[:, k, m * P:(m + 1) * P], wkv[:, k, M_W:2 * M_W],
                                          start=k == 0, stop=k == KT - 1)
                mm.then_inc(s_kv, 1)

            def pair(c):
                for j in range(4):
                    stream_tile(4 * c + j, j, free=j >= 2)
                tb, pv, un = TB_PAIR * c, PV_PAIR * c, UNITS * c
                pe.wait_ge(s_kvl, 2 * MP + MT)
                pe.wait_ge(s_pjfree, 8 * c + 6)
                for b in range(2):
                    for k in range(4):
                        mm = nc.tensor.transpose(pt[:, b, k * P:(k + 1) * P],
                                                 v_raw[:, (4 * b + k) * P:(4 * b + k + 1) * P], ident[:, :])
                    mm.then_inc(s_tb, 1)
                pe.wait_ge(s_pjfree, 8 * c + 8)
                pe.wait_ge(s_stkl, STK_PAIR * c + 6)

                def scores(u):
                    a, i = u // NT, u % NT
                    if u >= 2:
                        pe.wait_ge(s_sp, un + u - 1)
                    L = max(i + 1, 2) * P
                    sc = pj[:, 2 * (u % 2):2 * (u % 2) + 2, :].rearrange("p a b -> p (a b)")
                    parts = [(0, min(L, HALF))] + ([(HALF, max(L, HALF + 2 * P))] if L > HALF else [])
                    for k0, k1 in parts:
                        nc.tensor.matmul(sc[:, k0:k1], q_stack[:, a, i * P:(i + 1) * P],
                                         k_stack_hi[:, a, k0:k1], start=True, stop=False)
                        mm = nc.tensor.matmul(sc[:, k0:k1], q_stack[:, a, i * P:(i + 1) * P],
                                              k_stack_lo[:, a, k0:k1], start=False, stop=True)
                    mm.then_inc(s_s, 1)

                scores(0)
                scores(1)
                for u in range(UNITS):
                    a, i = u // NT, u % NT
                    top = 2 * (i // 2) + 1
                    pe.wait_ge(s_pn, un + u + 1)
                    for n, slots in enumerate(batches(i)):
                        x_ = tb_before(u) + n
                        pe.wait_ge(s_tlo, tb + x_ - 1)
                        for q, slot in enumerate(slots):
                            kt = top - slot
                            mm = nc.tensor.transpose(pt[:, x_ % 2, q * P:(q + 1) * P],
                                                     probs[:, u % 2, kt * P:(kt + 1) * P], ident[:, :])
                        mm.then_inc(s_tb, 1)
                    if u + 2 < UNITS:
                        scores(u + 2)
                    if i % 2 == 1:
                        n = u // 2
                        pe.wait_ge(s_tlo, tb + tb_before(u) + len(batches(i)))
                        if n >= 2:
                            pe.wait_ge(s_oadd, pv + n - 1)
                        for slot in range(top + 1):
                            for r in (pT_hi, pT_lo):
                                mm = nc.tensor.matmul(po[:, n % 2, 0:2 * P],
                                                      v_stack[:, a, top - slot, :, :].rearrange("p a b -> p (a b)"),
                                                      r[:, slot, :], start=slot == 0 and r is pT_hi,
                                                      stop=slot == top and r is pT_lo)
                        mm.then_inc(s_pv, 1)

            with pe.Fori(0, CT) as c:
                pair(c)

            TB, PV, UN = TB_PAIR * CT, PV_PAIR * CT, UNITS * CT
            for m in range(MP):
                for j in range(2):
                    stream_tile(S_M + 2 * m + j, j)
                pe.wait_ge(s_pjfree, 2 * (S_M + 2 * m + 2))
                pe.wait_ge(s_stkl, STK_PAIR * CT + 2 * (m + 1))
                un, tb, pv = UN + NT * m, TB + NT * m, PV + NT * m

                def mscores(i):
                    if i >= 2:
                        pe.wait_ge(s_sp, un + i - 1)
                        pe.wait_ge(s_e, un + i - 1)
                    for a in range(2):
                        h = 2 * m + a
                        nc.tensor.matmul(pj[:, 2 * (i % 2), a * MEM:(a + 1) * MEM], q_stack[:, a, i * P:(i + 1) * P],
                                         km_hi[:, h, :], start=True, stop=False)
                        mm = nc.tensor.matmul(pj[:, 2 * (i % 2), a * MEM:(a + 1) * MEM],
                                              q_stack[:, a, i * P:(i + 1) * P], km_lo[:, h, :], start=False, stop=True)
                    mm.then_inc(s_s, 1)

                mscores(0)
                mscores(1)
                for i in range(NT):
                    pe.wait_ge(s_pn, un + i + 1)
                    pe.wait_ge(s_tlo, tb + i - 1)
                    for q in range(2 * MT):
                        mm = nc.tensor.transpose(pt[:, i % 2, q * P:(q + 1) * P],
                                                 probs[:, i % 2, q * P:(q + 1) * P], ident[:, :])
                    mm.then_inc(s_tb, 1)
                    if i + 2 < NT:
                        mscores(i + 2)
                    if i % 2 == 1:
                        pe.wait_ge(s_tlo, tb + i + 1)
                        for a in range(2):
                            n = 2 * (i // 2) + a
                            pe.wait_ge(s_oadd, pv + n - 1)
                            for t in range(MT):
                                for r in (pT_hi, pT_lo):
                                    mm = nc.tensor.matmul(
                                        po[:, a, 0:2 * P],
                                        vm_stack[:, t, 2 * m + a, :, :].rearrange("p a b -> p (a b)"),
                                        r[:, MT * a + t, :], start=t == 0 and r is pT_hi,
                                        stop=t == MT - 1 and r is pT_lo)
                            mm.then_inc(s_pv, 1)

            with pe.Fori(0, CT) as ct:
                for j in range(2):
                    stream_tile(S_A + 2 * ct + j, j)

            def merge(s0, nk, r_hi, r_lo):
                with pe.Fori(0, DT) as dt:
                    stream_tile(s0 + 2 * dt, 0)
                    stream_tile(s0 + 2 * dt + 1, 1, nk, r_hi, r_lo)

            pe.wait_ge(s_zlo, CT)
            merge(S_GC, CT, z_hi, z_lo)
            pe.wait_ge(s_zlo, CT + MP)
            merge(S_GM, MP, zm_hi, zm_lo)
            with pe.Fori(0, CT) as ct:
                for j in range(4):
                    stream_tile(S_B + 4 * ct + j, j)
            pe.wait_ge(s_zlo, CT + MP + CT)
            merge(S_GB, CT, z_hi, z_lo)
            pe.wait_ge(s_cst, 3)
            pe.wait_ge(s_ca, CONV_STEPS)
            for h in range(2):
                for ct in range(CT):
                    mm = nc.tensor.matmul(pt[:, h, :], ones_ln[:, :], glu[:, ct, PAD_A + h * HALF:PAD_A + (h + 1) * HALF],
                                          start=ct == 0, stop=ct == CT - 1)
                mm.then_inc(s_lnm, 1)
            for ct in range(CT):
                pe.wait_ge(s_sq, ct + 1)
                for h in range(2):
                    mm = nc.tensor.matmul(po[:, h, :], ones_ln[:, :], ytmp[:, ct % 2, h * HALF:(h + 1) * HALF],
                                          start=ct == 0, stop=ct == CT - 1)
                mm.then_inc(s_lnv, 1)
            with pe.Fori(0, CT // 2) as i:
                for j in range(2):
                    stream_tile(S_AG + 2 * i + j, j)
            pe.wait_ge(s_zlo, CT + MP + 2 * CT)
            merge(S_GA, CT, z_hi, z_lo)

            for t in range(NT):
                for h in range(2):
                    n = 2 * t + h
                    if n < 4:
                        pe.wait_ge(s_pjfree, 2 * S_END)
                    else:
                        pe.wait_ge(s_yk, n - 3)
                    for k in range(KT):
                        if t == 0 and h == 0:
                            pe.wait_ge(s_gl, k + 1)
                            pe.wait_ge(s_wol, k + 1)
                        tk, c = slice(t * P, (t + 1) * P), slice(h * HALF, (h + 1) * HALF)
                        nc.tensor.matmul(pj[:, n % 4, :], xT_hi[:, k, tk], wout_hi[:, k, c], start=k == 0, stop=False)
                        nc.tensor.matmul(pj[:, n % 4, :], xT_hi[:, k, tk], wout_lo[:, k, c], start=False, stop=False)
                        mm = nc.tensor.matmul(pj[:, n % 4, :], xT_lo[:, k, tk], wout_hi[:, k, c],
                                              start=False, stop=k == KT - 1)
                    mm.then_inc(s_out_pj, 1)

        @block.scalar
        def _(act):
            def split_w(sh, j, nk=KT, free=True):
                act.wait_ge(s_wld[j % 2], raw_count(sh, j))
                if free:
                    act.wait_ge(s_pj, 4 * sh + 2 * j - 2)
                nc.scalar.activation(w_hi[:, j % 2, 0:nk, :], w_raw[:, j % 2, 0:nk, :], ACT.Copy).then_inc(s_whi, 1)

            def evac(s, j, func, scale):
                for h in range(2):
                    act.wait_ge(s_pj, 2 * s + h + 1)
                    if h == 0:
                        act.wait_ge(s_pjfree, 2 * s)
                    nc.scalar.activation(xt[:, h * HALF:(h + 1) * HALF], pj[:, 2 * (j % 2) + h, :], func,
                                         scale=scale).then_inc(s_xt, 1)

            act.wait_ge(s_wf, 16)
            act.wait_ge(s_wfs, 1)
            nc.scalar.activation(wf_stack[:, :, 0:HEADS], wf_raw[:, :, :], ACT.Copy).then_inc(s_fa, 1)
            for k in range(KT):
                act.wait_ge(s_x[k // 2], 16)
                nc.scalar.activation(xT_hi[:, k, :], x_raw[:, k, :], ACT.Copy).then_inc(s_xhi, 1)
            split_w(0, 0, free=False)
            act.wait_ge(s_ms, MT)
            act.wait_ge(s_fix, 1)
            nc.scalar.activation(rstd[:, 0:MT], mv[:, :, 1], ACT.Sqrt, bias=eps[:, 0:1]).then_inc(s_mr, 1)
            for h in range(2):
                act.wait_ge(s_f, h + 1)
                nc.scalar.activation(f_l[:, h * HALF:(h + 1) * HALF], po[32:32 + HEADS, h, :],
                                     ACT.Copy).then_inc(s_fa, 1)
            act.wait_ge(s_fv, 1)
            nc.scalar.activation(f_abs[:, :], f_z[:, :], ACT.Abs).then_inc(s_fa, 1)
            act.wait_ge(s_fa, 4)
            nc.scalar.activation(f_e[:, :], f_abs[:, :], ACT.Exp, scale=-1.0).then_inc(s_fa, 1)
            act.wait_ge(s_fv, 2)
            nc.scalar.activation(f_l[:, :], f_u[:, :], ACT.Ln).then_inc(s_fa, 1)
            for c in range(MP):
                act.wait_ge(s_kv, c + 1)
                for a in range(2):
                    b, o = DH * a, DH * (1 - a)
                    for r in (b, o):
                        op = nc.scalar.activation(km_hi[r:r + DH, 2 * c + a, :], po[b:b + DH, c, 0:MEM], ACT.Copy)
                    op.then_inc(s_kvh, 1)
            for m in range(MT):
                act.wait_ge(s_kv, MP + m + 1)
                nc.scalar.activation(vm_stack[:, m, :, 0, :],
                                     pt[:, m, 0:M_W].rearrange("p (h d) -> p h d", d=DH), ACT.Copy).then_inc(s_kvh, 1)

            def out_shift(a, n, count, first=False):
                b, o = DH * a, DH * (1 - a)
                act.wait_ge(s_pv, count + 1)
                if not first:
                    act.wait_ge(s_og, count)
                nc.scalar.activation(otmp[b:b + DH, :], po[o:o + DH, n % 2, 0:2 * P], ACT.Copy).then_inc(s_osh, 1)

            def pair(c, last):
                sh = 2 * c
                stk = STK_PAIR * c
                split_w(sh, 1, free=False)
                split_w(sh, 2)
                act.wait_ge(s_pjfree, 8 * c + 2)
                for a in range(2):
                    b = DH * a
                    nc.scalar.activation(q_stack[b:b + DH, a, :], q_raw[b:b + DH, :], ACT.Copy).then_inc(s_stkh, 1)
                split_w(sh, 3)
                act.wait_ge(s_pjfree, 8 * c + 4)
                for a in range(2):
                    b = DH * a
                    for r in (b, DH - b):
                        nc.scalar.activation(k_stack_hi[r:r + DH, a, :], k_raw[b:b + DH, :],
                                             ACT.Copy).then_inc(s_stkh, 1)
                evac(4 * c + 3, 3, ACT.Tanh, 0.5)
                split_w(sh, 4)
                tb, pv, un = TB_PAIR * c, PV_PAIR * c, UNITS * c
                for b in range(2):
                    act.wait_ge(s_tb, tb + b + 1)
                    nc.scalar.activation(v_stack[:, :, 4 * b:4 * b + 4, 0, :].rearrange("p a k d -> p k a d"),
                                         pt[:, b, :].rearrange("p (k a d) -> p k a d", k=4, a=2),
                                         ACT.Copy).then_inc(s_thi, 1)

                def exp(u):
                    i = u % NT
                    act.wait_ge(s_sp, un + u + 1)
                    nc.scalar.activation(probs[:, u % 2, 0:(i + 1) * P], probs[:, u % 2, 0:(i + 1) * P], ACT.Exp,
                                         scale=-1.0, bias=rmin[:, u % 2, 1:2],
                                         accum_out=rsum[:, u % 2, 0:1]).then_inc(s_e, 1)

                exp(0)
                for u in range(UNITS):
                    a, i = u // NT, u % NT
                    if u + 1 < UNITS:
                        exp(u + 1)
                    for n, slots in enumerate(batches(i)):
                        act.wait_ge(s_tb, tb + tb_before(u) + n + 1)
                        if i % 2 == 0 and n == 0 and u > 0:
                            act.wait_ge(s_pv, pv + u // 2)
                        nc.scalar.activation(
                            pT_hi[:, slots[0]:slots[-1] + 1, (i % 2) * P:(i % 2 + 1) * P],
                            pt[:, (tb_before(u) + n) % 2, 0:len(slots) * P].rearrange("p (k q) -> p k q", q=P),
                            ACT.Copy).then_inc(s_thi, 1)
                    if i % 2 == 1:
                        out_shift(a, u // 2, pv + u // 2, first=u == 1)
                act.wait_ge(s_og, pv + PV_PAIR)
                nc.scalar.activation(z_hi[:, bass.ds(c, 1), :].rearrange("p o t -> p (o t)"), sg[:, :],
                                     ACT.Copy).then_inc(s_zhi, 1)

            with act.Fori(0, CT) as c:
                pair(c, False)

            for m in range(MP):
                s = S_M + 2 * m
                split_w(s // 2, 1)
                act.wait_ge(s_pjfree, 2 * s + 2)
                for a in range(2):
                    b = DH * a
                    nc.scalar.activation(q_stack[b:b + DH, a, :], q_raw[b:b + DH, :], ACT.Copy).then_inc(s_stkh, 1)
                evac(s + 1, 1, ACT.Tanh, 0.5)
                split_w(s // 2, 2)
                un, tb, pv = UNITS * CT + NT * m, TB_PAIR * CT + NT * m, PV_PAIR * CT + NT * m

                def mexp(i):
                    act.wait_ge(s_sp, un + i + 1)
                    if i >= 2:
                        act.wait_ge(s_tb, tb + i - 1)
                    for a in range(2):
                        op = nc.scalar.activation(probs[:, i % 2, a * MEM:(a + 1) * MEM],
                                                  pj[:, 2 * (i % 2), a * MEM:(a + 1) * MEM], ACT.Exp,
                                                  bias=rmin[:, i % 2, a:a + 1], accum_out=rsum[:, i % 2, a:a + 1])
                    op.then_inc(s_e, 1)

                mexp(0)
                for i in range(NT):
                    if i + 1 < NT:
                        mexp(i + 1)
                    act.wait_ge(s_tb, tb + i + 1)
                    if i % 2 == 0:
                        act.wait_ge(s_pv, pv + i)
                    nc.scalar.activation(pT_hi[:, 0:2 * MT, (i % 2) * P:(i % 2 + 1) * P],
                                         pt[:, i % 2, :].rearrange("p (k q) -> p k q", q=P),
                                         ACT.Copy).then_inc(s_thi, 1)
                    if i % 2 == 1:
                        for a in range(2):
                            out_shift(a, a, pv + 2 * (i // 2) + a)
                act.wait_ge(s_og, pv + NT)
                nc.scalar.activation(zm_hi[:, m, :], sg[:, :], ACT.Copy).then_inc(s_zhi, 1)

            with act.Fori(0, CT) as ct:
                sh = S_A // 2 + ct
                split_w(sh, 1)
                evac(S_A + 2 * ct, 0, ACT.Tanh, 0.5)
                split_w(sh, 2)

            def merge_step(s0, dt, nk, last=False):
                sh = s0 // 2 + dt
                split_w(sh, 1, nk)
                evac(s0 + 2 * dt, 0, ACT.Tanh, 0.5)
                if not last:
                    split_w(sh, 2)

            with act.Fori(0, DT) as dt:
                merge_step(S_GC, dt, CT)
            with act.Fori(0, DT) as dt:
                merge_step(S_GM, dt, MP)
            with act.Fori(0, CT) as ct:
                s = S_B + 4 * ct
                sh = S_B // 2 + 2 * ct
                split_w(sh, 1)
                evac(s, 0, ACT.Copy, 1.0)
                split_w(sh, 2)
                split_w(sh, 3)
                evac(s + 2, 2, ACT.Tanh, 0.5)
                split_w(sh, 4)
                act.wait_ge(s_zpre, ct + 1)
                nc.scalar.activation(z_hi[:, bass.ds(ct, 1), :].rearrange("p o t -> p (o t)"), bz[:, :],
                                     ACT.Copy).then_inc(s_zhi, 1)
            with act.Fori(0, DT) as dt:
                merge_step(S_GB, dt, CT)
            for ct in range(CT):
                act.wait_ge(s_lnc, ct + 1)
                if ct == 0:
                    act.wait_ge(s_add, 2 * DT)
                if ct >= 2:
                    act.wait_ge(s_lnv, ct - 1)
                nc.scalar.activation(ytmp[:, ct % 2, :], glu[:, ct, PAD_A:WA], ACT.Square).then_inc(s_sq, 1)
            act.wait_ge(s_lnv, CT)
            act.wait_ge(s_pjfree, 2 * S_AG)
            for h in range(2):
                op = nc.scalar.activation(xt[:, h * HALF:(h + 1) * HALF], po[:, h, :], ACT.Sqrt, bias=eps[:, 0:1])
            op.then_inc(s_sd, 1)
            for ct in range(CT):
                act.wait_ge(s_an, ct + 1)
                nc.scalar.activation(glu[:, ct, PAD_A:WA], glu[:, ct, PAD_A:WA], ACT.Identity,
                                     scale=lag[:, ct:ct + 1], bias=lab[:, ct:ct + 1]).then_inc(s_ag, 1)
                act.wait_ge(s_ag, ct + 1)
                act.wait_ge(s_rs, 1)
                if ct >= 1:
                    act.wait_ge(s_as, ct)
                nc.scalar.activation(xt[:, :], glu[:, ct, PAD_A:WA], ACT.Tanh, scale=0.5).then_inc(s_at, 1)
            act.wait_ge(s_as, CT)
            with act.Fori(0, CT // 2) as i:
                sh = S_AG // 2 + i
                for j in range(2):
                    split_w(sh, j + 1)
                    evac(S_AG + 2 * i + j, j, ACT.Tanh, 0.5)
                    act.wait_ge(s_zpre, CT + 2 * i + j + 1)
                    nc.scalar.activation(z_hi[:, bass.ds(2 * i + j, 1), :].rearrange("p o t -> p (o t)"), sg[:, :],
                                         ACT.Copy).then_inc(s_zhi, 1)
            with act.Fori(0, DT - 1) as dt:
                merge_step(S_GA, dt, CT)
            merge_step(S_GA, DT - 1, CT, last=True)
            for k in range(KT):
                act.wait_ge(s_wld[k % 2], raw_count(S_END // 2, k))
                if k == 0:
                    act.wait_ge(s_pj, 2 * S_END)
                nc.scalar.activation(wout_hi[:, k, :], w_raw[:, k % 2, :, :].rearrange("p a b -> p (a b)"),
                                     ACT.Copy).then_inc(s_woh, 1)
                act.wait_ge(s_add, 3 * DT if k == KT - 1 else 2 * DT + k + 1)
                nc.scalar.activation(xT_hi[:, k, :], merged[:, k, :], ACT.Copy, scale=0.5).then_inc(s_gh, 1)
            for t in range(NT):
                act.wait_ge(s_mvr, t + 1)
                nc.scalar.activation(rstd[:, t % 2:t % 2 + 1], mv[:, t % 2, 1:2], ACT.Sqrt,
                                     bias=eps[:, 0:1]).then_inc(s_osd, 1)

        @block.gpsimd
        def _(pool):
            def split_w(s, j, nk=KT):
                pool.wait_ge(s_whi, s + 1)
                nc.gpsimd.tensor_tensor(w_lo[:, j % 2, 0:nk, :], w_raw[:, j % 2, 0:nk, :], w_hi[:, j % 2, 0:nk, :],
                                        ALU.subtract).then_inc(s_wlo, 1)

            nc.gpsimd.memset(ident[:, :], 0.0).then_inc(s_cst, 1)
            pool.wait_ge(s_cst, 1)
            nc.gpsimd.affine_select(out=ident[:, :], in_=ident[:, :], compare_op=ALU.not_equal, fill=1.0, base=0,
                                    pattern=[[-1, P]], channel_multiplier=1).then_inc(s_cst, 1)
            nc.gpsimd.memset(maskc[:, :], 0.0).then_inc(s_bd, 1)
            pool.wait_ge(s_bd, 1)
            nc.gpsimd.affine_select(out=maskc[:, :], in_=maskc[:, :], compare_op=ALU.is_ge, fill=-BIG, base=0,
                                    pattern=[[-1, P]], channel_multiplier=1).then_inc(s_bd, 1)
            split_w(0, 0)
            pool.wait_ge(s_bd, 2)

            with pool.Fori(0, CT) as c:
                for j in range(1, 5):
                    split_w(4 * c + j, j)
                un = UNITS * c
                for u in range(UNITS):
                    a, i = u // NT, u % NT
                    if i == 0:
                        pool.wait_ge(s_bias[a], 16 * (c + 1))
                    if u >= 2:
                        pool.wait_ge(s_dm, un + u - 1)
                    nc.gpsimd.tensor_tensor(bdiag[:, u % 2, :], bias[:, a, i * P:(i + 1) * P], maskc[:, :],
                                            ALU.add).then_inc(s_bd, 1)
            for m in range(MP):
                for j in range(1, 3):
                    split_w(S_M + 2 * m + j, j)
            with pool.Fori(0, CT) as ct:
                for j in range(1, 3):
                    split_w(S_A + 2 * ct + j, j)
            with pool.Fori(0, DT) as dt:
                split_w(S_GC + 2 * dt + 1, 1, CT)
                split_w(S_GC + 2 * dt + 2, 2)

            def merge_step(s0, nk, d2, last=False):
                for e in range(2):
                    dt = 2 * d2 + e
                    split_w(s0 + 2 * dt + 1, 1, nk)
                    if not (last and e == 1):
                        split_w(s0 + 2 * dt + 2, 2)
                    pool.wait_ge(s_pjfree, 2 * (s0 + 2 * dt + 2))
                    md = merged[:, bass.ds(dt, 1), :].rearrange("p o t -> p (o t)")
                    nc.gpsimd.tensor_tensor(md, md, ytmp[:, e, :], ALU.add).then_inc(s_add, 1)

            with pool.Fori(0, DT // 2) as d2:
                merge_step(S_GM, MP, d2)
            nc.gpsimd.memset(ones_ln[:, :], 1.0 / A_W).then_inc(s_cst, 1)
            with pool.Fori(0, CT) as ct:
                for j in range(1, 5):
                    split_w(S_B + 4 * ct + j, j)
            with pool.Fori(0, DT // 2) as d2:
                merge_step(S_GB, CT, d2)
            with pool.Fori(0, CT // 2) as i:
                for j in range(1, 3):
                    split_w(S_AG + 2 * i + j, j)
            with pool.Fori(0, DT // 2 - 1) as d2:
                merge_step(S_GA, CT, d2)
            merge_step(S_GA, CT, DT // 2 - 1, last=True)

        @block.vector
        def _(dve):
            def hs(h):
                return slice(h * HALF, (h + 1) * HALF)

            def raw_evac(s, j, dst, scale=None):
                for h in range(2):
                    dve.wait_ge(s_pj, 2 * s + h + 1)
                    if scale is None:
                        nc.vector.tensor_copy(dst[:, hs(h)], pj[:, 2 * (j % 2) + h, :]).then_inc(s_pjfree, 1)
                    else:
                        nc.vector.tensor_scalar(dst[:, hs(h)], pj[:, 2 * (j % 2) + h, :], scale, None,
                                                ALU.mult).then_inc(s_pjfree, 1)

            def gate_evac(s, j, xt_count):
                for h in range(2):
                    dve.wait_ge(s_xt, xt_count + h + 1)
                    nc.vector.scalar_tensor_tensor(out=sg[:, hs(h)], in0=xt[:, hs(h)], scalar=1.0,
                                                   in1=pj[:, 2 * (j % 2) + h, :], op0=ALU.add,
                                                   op1=ALU.mult).then_inc(s_pjfree, 1)

            nc.vector.memset(wf_stack[:, :, :].bitcast(mybir.dt.uint32), 0).then_inc(s_wfs, 1)
            nc.vector.memset(eps[:, :], EPS).then_inc(s_fix, 1)
            dve.wait_ge(s_fa, 1)
            nc.vector.tensor_tensor(wf_stack[:, :, 32:32 + HEADS], wf_raw[:, :, :], wf_stack[:, :, 0:HEADS],
                                    ALU.subtract).then_inc(s_wfs, 1)
            for k in range(KT):
                dve.wait_ge(s_xhi, k + 1)
                nc.vector.tensor_tensor(xT_lo[:, k, :], x_raw[:, k, :], xT_hi[:, k, :], ALU.subtract).then_inc(s_xlo, 1)
            dve.wait_ge(s_mem, 16)
            for m in range(MT):
                for h in range(2):
                    op = nc.vector.bn_stats(stats[:, m, h, :], mem_sb[:, m, hs(h)])
            op.then_inc(s_st, 1)
            dve.wait_ge(s_st, 1)
            for m in range(MT):
                nc.vector.bn_aggr(mv[:, m, :], stats[:, m, :, :]).then_inc(s_ms, 1)
            dve.wait_ge(s_mr, 1)
            nc.vector.reciprocal(rinv[:, 0, :], rstd[:, 0:MT]).then_inc(s_mr, 1)
            dve.wait_ge(s_mr, 2)
            for m in range(MT):
                nc.vector.tensor_scalar(mem_sb[:, m, :], mem_sb[:, m, :], mv[:, m, 0:1], rinv[:, 0, m:m + 1],
                                        ALU.subtract, ALU.mult).then_inc(s_mn, 1)
            dve.wait_ge(s_par, 16 * 8)
            dve.wait_ge(s_fa, 3)
            for h in range(2):
                op = nc.vector.scalar_tensor_tensor(out=f_z[:, hs(h)], in0=po[0:HEADS, h, :], scalar=bf[:, 0:1],
                                                    in1=f_l[:, hs(h)], op0=ALU.add, op1=ALU.add)
            op.then_inc(s_fv, 1)
            n = 0
            for m in range(MT):
                for kb in range(KT // 4):
                    dve.wait_ge(s_mt, n + 1)
                    for k in range(4):
                        kk = 4 * kb + k
                        op = nc.vector.tensor_scalar(memT[:, kk, m * P:(m + 1) * P], pt[:, n % 2, k * P:(k + 1) * P],
                                                     memg[:, kk:kk + 1], memb[:, kk:kk + 1], ALU.mult, ALU.add)
                    op.then_inc(s_mte, 1)
                    n += 1
            dve.wait_ge(s_fa, 5)
            nc.vector.tensor_scalar(f_u[:, :], f_e[:, :], 1.0, None, ALU.add).then_inc(s_fv, 1)
            dve.wait_ge(s_fv, 2)
            nc.vector.scalar_tensor_tensor(out=f_e[:, :], in0=f_u[:, :], scalar=1.0, in1=f_e[:, :],
                                           op0=ALU.subtract, op1=ALU.subtract).then_inc(s_fv, 1)
            nc.vector.reciprocal(f_r[:, :], f_u[:, :]).then_inc(s_fv, 1)
            dve.wait_ge(s_fv, 4)
            nc.vector.scalar_tensor_tensor(out=f_e[:, :], in0=f_e[:, :], scalar=-1.0, in1=f_r[:, :],
                                           op0=ALU.mult, op1=ALU.mult).then_inc(s_fv, 1)
            dve.wait_ge(s_fa, 6)
            dve.wait_ge(s_fv, 5)
            nc.vector.tensor_tensor(f_l[:, :], f_l[:, :], f_e[:, :], ALU.add).then_inc(s_fv, 1)
            nc.vector.tensor_scalar(f_z[:, :], f_z[:, :], -1.0, 0.0, ALU.mult, ALU.max).then_inc(s_fv, 1)
            dve.wait_ge(s_fv, 7)
            nc.vector.tensor_tensor(f_l[:, :], f_l[:, :], f_z[:, :], ALU.add).then_inc(s_fv, 1)
            nc.vector.memset(f_abs[:, :], 1.0).then_inc(s_fv, 1)
            dve.wait_ge(s_fv, 9)
            nc.vector.tensor_tensor_scan(negcum[:, :], f_abs[:, :], f_l[:, :], 0.0, ALU.mult,
                                         ALU.add).then_inc(s_fv, 1)
            for c in range(MP):
                for a in range(2):
                    b, o = DH * a, DH * (1 - a)
                    dve.wait_ge(s_kvh, 2 * c + a + 1)
                    for r in (b, o):
                        op = nc.vector.tensor_tensor(km_lo[r:r + DH, 2 * c + a, :], po[b:b + DH, c, 0:MEM],
                                                     km_hi[b:b + DH, 2 * c + a, :], ALU.subtract)
                    op.then_inc(s_kvl, 1)
            for m in range(MT):
                dve.wait_ge(s_kvh, 2 * MP + m + 1)
                nc.vector.tensor_tensor(vm_stack[:, m, :, 1, :], pt[:, m, 0:M_W].rearrange("p (h d) -> p h d", d=DH),
                                        vm_stack[:, m, :, 0, :], ALU.subtract).then_inc(s_kvl, 1)
            dve.wait_ge(s_fv, F_STEPS)
            for t in (pT_hi, pT_lo):
                nc.vector.memset(t[:, 0, 0:P].bitcast(mybir.dt.uint32), 0)

            def out_gate(a, n, g, count):
                b = DH * a
                dve.wait_ge(s_osh, count + 1)
                nc.vector.tensor_tensor(otmp[b:b + DH, :], po[b:b + DH, n % 2, 0:2 * P], otmp[b:b + DH, :],
                                        ALU.add).then_inc(s_oadd, 1)
                dve.wait_ge(s_oadd, count + 1)
                t = slice(g * 2 * P, (g + 1) * 2 * P)
                nc.vector.scalar_tensor_tensor(out=sg[b:b + DH, t], in0=otmp[b:b + DH, :], scalar=0.5,
                                               in1=sg[b:b + DH, t], op0=ALU.mult, op1=ALU.mult).then_inc(s_og, 1)

            def pair(c):
                raw_evac(4 * c, 0, q_raw, QSCALE)
                stk = STK_PAIR * c
                raw_evac(4 * c + 1, 1, k_raw)
                for a in range(2):
                    b, o = DH * a, DH * (1 - a)
                    dve.wait_ge(s_stkh, stk + a + 1)
                    nc.vector.tensor_tensor(q_stack[o:o + DH, a, :], q_raw[b:b + DH, :], q_stack[b:b + DH, a, :],
                                            ALU.subtract).then_inc(s_stkl, 1)
                raw_evac(4 * c + 2, 2, v_raw)
                for a in range(2):
                    b, o = DH * a, DH * (1 - a)
                    dve.wait_ge(s_stkh, stk + 2 + 2 * a + 2)
                    for r in (b, o):
                        nc.vector.tensor_tensor(k_stack_lo[r:r + DH, a, :], k_raw[b:b + DH, :],
                                                k_stack_hi[b:b + DH, a, :], ALU.subtract).then_inc(s_stkl, 1)
                gate_evac(4 * c + 3, 3, 2 * c)
                tb, pv, un = TB_PAIR * c, PV_PAIR * c, UNITS * c
                for b in range(2):
                    dve.wait_ge(s_thi, tb + b + 1)
                    nc.vector.tensor_tensor(v_stack[:, :, 4 * b:4 * b + 4, 1, :].rearrange("p a k d -> p k a d"),
                                            pt[:, b, :].rearrange("p (k a d) -> p k a d", k=4, a=2),
                                            v_stack[:, :, 4 * b:4 * b + 4, 0, :].rearrange("p a k d -> p k a d"),
                                            ALU.subtract).then_inc(s_tlo, 1)

                def biased(u):
                    a, i = u // NT, u % NT
                    dve.wait_ge(s_s, un + u + 1)
                    dve.wait_ge(s_bd, 2 + un + u + 1)
                    if i == 0:
                        dve.wait_ge(s_bias[a], 16 * (c + 1))
                    if u >= 2:
                        dve.wait_ge(s_tb, tb + tb_before(u - 1))
                    else:
                        dve.wait_ge(s_tb, tb + 2)
                    sc = pj[:, 2 * (u % 2):2 * (u % 2) + 2, :].rearrange("p a b -> p (a b)")
                    d = slice(i * P, (i + 1) * P)
                    mn = rmin[:, u % 2, 0:1] if i else rmin[:, u % 2, 1:2]
                    dve.sem_inc(s_passed[0], 1)
                    op = nc.vector.tensor_tensor_reduce(probs[:, u % 2, d], sc[:, d], bdiag[:, u % 2, :], -1.0, BIG,
                                                        ALU.add, ALU.min, mn)
                    op.then_inc(s_dm, 1)
                    dve.wait_ge(s_dm, un + u + 1)
                    if i:
                        dve.sem_inc(s_passed[0], 1)
                        nc.vector.tensor_tensor_reduce(probs[:, u % 2, 0:i * P], sc[:, 0:i * P], bias[:, a, 0:i * P],
                                                       -1.0, rmin[:, u % 2, 0:1], ALU.add, ALU.min,
                                                       rmin[:, u % 2, 1:2]).then_inc(s_sp, 1)
                    else:
                        nc.vector.tensor_copy(rmin[:, u % 2, 0:1], rmin[:, u % 2, 1:2]).then_inc(s_sp, 1)

                biased(0)
                for u in range(UNITS):
                    a, i = u // NT, u % NT
                    if u + 1 < UNITS:
                        biased(u + 1)
                    dve.wait_ge(s_e, un + u + 1)
                    nc.vector.reciprocal(rinv[:, u % 2, 0:1], rsum[:, u % 2, 0:1]).then_inc(s_ri, 1)
                    dve.wait_ge(s_ri, un + u + 1)
                    nc.vector.tensor_scalar(probs[:, u % 2, 0:(i + 1) * P], probs[:, u % 2, 0:(i + 1) * P],
                                            rinv[:, u % 2, 0:1], None, ALU.mult).then_inc(s_pn, 1)
                    for n, slots in enumerate(batches(i)):
                        dve.wait_ge(s_thi, tb + tb_before(u) + n + 1)
                        q = slice((i % 2) * P, (i % 2 + 1) * P)
                        nc.vector.tensor_tensor(
                            pT_lo[:, slots[0]:slots[-1] + 1, q],
                            pt[:, (tb_before(u) + n) % 2, 0:len(slots) * P].rearrange("p (k q) -> p k q", q=P),
                            pT_hi[:, slots[0]:slots[-1] + 1, q], ALU.subtract).then_inc(s_tlo, 1)
                    if i % 2 == 1:
                        out_gate(a, u // 2, i // 2, pv + u // 2)
                dve.wait_ge(s_zhi, c + 1)
                nc.vector.tensor_tensor(z_lo[:, bass.ds(c, 1), :].rearrange("p o t -> p (o t)"), sg[:, :],
                                        z_hi[:, bass.ds(c, 1), :].rearrange("p o t -> p (o t)"),
                                        ALU.subtract).then_inc(s_zlo, 1)

            with dve.Fori(0, CT) as c:
                pair(c)

            for m in range(MP):
                s = S_M + 2 * m
                raw_evac(s, 0, q_raw, QSCALE)
                for a in range(2):
                    b, o = DH * a, DH * (1 - a)
                    dve.wait_ge(s_stkh, STK_PAIR * CT + 2 * m + a + 1)
                    nc.vector.tensor_tensor(q_stack[o:o + DH, a, :], q_raw[b:b + DH, :], q_stack[b:b + DH, a, :],
                                            ALU.subtract).then_inc(s_stkl, 1)
                gate_evac(s + 1, 1, X_M + 2 * m)
                un, tb, pv = UNITS * CT + NT * m, TB_PAIR * CT + NT * m, PV_PAIR * CT + NT * m

                def mmax(i):
                    dve.wait_ge(s_s, un + i + 1)
                    nc.vector.tensor_reduce(rmin[:, i % 2, :], pj[:, 2 * (i % 2), :].rearrange("p (a k) -> p a k", a=2),
                                            AX.X, ALU.max).then_inc(s_dm, 1)
                    dve.wait_ge(s_dm, un + i + 1)
                    nc.vector.tensor_scalar(rmin[:, i % 2, :], rmin[:, i % 2, :], -1.0, None, ALU.mult).then_inc(s_sp, 1)

                mmax(0)
                for i in range(NT):
                    if i + 1 < NT:
                        mmax(i + 1)
                    dve.wait_ge(s_e, un + i + 1)
                    nc.vector.reciprocal(rinv[:, i % 2, :], rsum[:, i % 2, :]).then_inc(s_ri, 1)
                    dve.wait_ge(s_ri, un + i + 1)
                    for a in range(2):
                        op = nc.vector.tensor_scalar(probs[:, i % 2, a * MEM:(a + 1) * MEM],
                                                     probs[:, i % 2, a * MEM:(a + 1) * MEM],
                                                     rinv[:, i % 2, a:a + 1], None, ALU.mult)
                    op.then_inc(s_pn, 1)
                    dve.wait_ge(s_thi, tb + i + 1)
                    q = slice((i % 2) * P, (i % 2 + 1) * P)
                    nc.vector.tensor_tensor(pT_lo[:, 0:2 * MT, q], pt[:, i % 2, :].rearrange("p (k q) -> p k q", q=P),
                                            pT_hi[:, 0:2 * MT, q], ALU.subtract).then_inc(s_tlo, 1)
                    if i % 2 == 1:
                        for a in range(2):
                            out_gate(a, a, i // 2, pv + 2 * (i // 2) + a)
                dve.wait_ge(s_zhi, CT + m + 1)
                nc.vector.tensor_tensor(zm_lo[:, m, :], sg[:, :], zm_hi[:, m, :], ALU.subtract).then_inc(s_zlo, 1)

            for ct in range(CT):
                op = nc.vector.memset(glu[:, ct, 0:PAD_A], 0.0)
            op.then_inc(s_ca, 1)
            nc.vector.tensor_scalar(cwa[:, :, :], cwa[:, :, :], 0.5, None, ALU.mult).then_inc(s_cw, 1)
            with dve.Fori(0, CT) as ct:
                for h in range(2):
                    dve.wait_ge(s_pj, 2 * (S_A + 2 * ct + 1) + h + 1)
                    if h == 0:
                        dve.wait_ge(s_xt, X_A + 2 * ct + 2)
                    nc.vector.scalar_tensor_tensor(
                        out=glu[:, bass.ds(ct, 1), PAD_A + h * HALF:PAD_A + (h + 1) * HALF].rearrange("p o t -> p (o t)"),
                        in0=xt[:, hs(h)], scalar=1.0, in1=pj[:, 2 + h, :], op0=ALU.add, op1=ALU.mult).then_inc(s_pjfree, 2)

            def conv_taps(ct, h, taps, unit):
                for n in taps:
                    src = glu[:, bass.ds(ct, 1), h * HALF + n:(h + 1) * HALF + n].rearrange("p o t -> p (o t)")
                    dve.wait_ge(s_ca, 1 + CONV_A * unit + n)
                    if n == 0:
                        dve.wait_ge(s_cw, 1 + 2 * unit)
                        nc.vector.tensor_copy(cwk[:, 0:CONV_A], cwa[:, bass.ds(ct, 1), :].rearrange("p o t -> p (o t)")
                                              ).then_inc(s_cw, 1)
                        nc.vector.tensor_copy(cwk[:, CONV_A:CONV_A + 1], cab[:, bass.ds(ct, 1)]).then_inc(s_cw, 1)
                        dve.wait_ge(s_cw, 1 + 2 * unit + 2)
                        op = nc.vector.tensor_scalar(sg[:, 0:HALF], src, cwk[:, 0:1], cwk[:, CONV_A:CONV_A + 1],
                                                     ALU.mult, ALU.add)
                    else:
                        op = nc.vector.scalar_tensor_tensor(out=src if n == CONV_A - 1 else sg[:, 0:HALF], in0=src,
                                                            scalar=cwk[:, n:n + 1], in1=sg[:, 0:HALF],
                                                            op0=ALU.mult, op1=ALU.add)
                    op.then_inc(s_ca, 1)

            def merge_step(s0, x0, d2, first=False, fresh=False, adds=0, conv=None):
                cuts = [range(0, 8), range(8, 16), range(16, 24), range(24, CONV_A)]
                for e in range(2):
                    dt = 2 * d2 + e
                    for h in range(2):
                        if conv is not None:
                            conv_taps(d2, conv[0], cuts[2 * e + h], conv[1] + d2)
                        if h == 0:
                            dve.wait_ge(s_xt, x0 + 2 * dt + 2)
                            if not first and not fresh:
                                dve.wait_ge(s_add, adds + dt - 1)
                        dve.wait_ge(s_pj, 2 * (s0 + 2 * dt + 1) + h + 1)
                        dst = merged[:, bass.ds(dt, 1), hs(h)].rearrange("p o t -> p (o t)") if first else ytmp[:, e, hs(h)]
                        nc.vector.scalar_tensor_tensor(out=dst, in0=xt[:, hs(h)], scalar=1.0, in1=pj[:, 2 + h, :],
                                                       op0=ALU.add, op1=ALU.mult).then_inc(s_pjfree, 2)

            dve.wait_ge(s_pjfree, 2 * S_GC)
            with dve.Fori(0, DT // 2) as d2:
                merge_step(S_GC, X_GC, d2, first=True, conv=(1, 0))
            merge_step(S_GM, X_GM, 0, fresh=True, conv=(0, CT))
            with dve.Fori(1, DT // 2) as d2:
                merge_step(S_GM, X_GM, d2, conv=(0, CT))

            nc.vector.memset(prod[:, 0:PAD_B], 0.0).then_inc(s_cb, 1)
            with dve.Fori(0, CT) as ct:
                s = S_B + 4 * ct
                x0 = X_B + 4 * ct
                dve.wait_ge(s_xt, x0 + 2)
                for h in range(2):
                    dve.wait_ge(s_pj, 2 * (s + 1) + h + 1)
                    nc.vector.tensor_tensor(prod[:, PAD_B + h * HALF:PAD_B + (h + 1) * HALF], pj[:, 2 + h, :],
                                            xt[:, hs(h)], ALU.mult).then_inc(s_pjfree, 2)
                nc.vector.tensor_copy(cwk[:, 0:CONV_B], cwb[:, bass.ds(ct, 1), :].rearrange("p o t -> p (o t)")
                                      ).then_inc(s_cb, 1)
                dve.wait_ge(s_pjfree, 2 * s + 4)
                for n in range(CONV_B):
                    dve.wait_ge(s_cb, 1 + (CONV_B + 1) * ct + 1 + n)
                    if n == 0:
                        op = nc.vector.tensor_scalar(cv[:, :], prod[:, 0:T], cwk[:, 0:1], None, ALU.mult)
                    else:
                        op = nc.vector.scalar_tensor_tensor(out=cv[:, :], in0=prod[:, n:n + T], scalar=cwk[:, n:n + 1],
                                                            in1=cv[:, :], op0=ALU.mult, op1=ALU.add)
                    op.then_inc(s_cb, 1)
                gate_evac(s + 2, 2, x0 + 2)
                dve.wait_ge(s_cb, 1 + (CONV_B + 1) * (ct + 1))
                for h in range(2):
                    dve.wait_ge(s_pj, 2 * (s + 3) + h + 1)
                    nc.vector.tensor_tensor(bz[:, hs(h)], pj[:, 2 + h, :], cv[:, hs(h)], ALU.mult).then_inc(s_pjfree, 1)
                dve.wait_ge(s_pjfree, 2 * s + 8)
                nc.vector.scalar_tensor_tensor(out=bz[:, :], in0=bz[:, :], scalar=0.5, in1=sg[:, :],
                                               op0=ALU.mult, op1=ALU.mult).then_inc(s_zpre, 1)
                dve.wait_ge(s_zhi, CT + MP + ct + 1)
                nc.vector.tensor_tensor(z_lo[:, bass.ds(ct, 1), :].rearrange("p o t -> p (o t)"), bz[:, :],
                                        z_hi[:, bass.ds(ct, 1), :].rearrange("p o t -> p (o t)"),
                                        ALU.subtract).then_inc(s_zlo, 1)
            with dve.Fori(0, DT // 2) as d2:
                merge_step(S_GB, X_GB, d2, adds=DT)

            dve.wait_ge(s_lnm, 2)
            for ct in range(CT):
                for h in range(2):
                    v = glu[:, ct, PAD_A + h * HALF:PAD_A + (h + 1) * HALF]
                    op = nc.vector.tensor_tensor(v, v, pt[:, h, :], ALU.subtract)
                op.then_inc(s_lnc, 1)
            dve.wait_ge(s_sd, 1)
            nc.vector.reciprocal(ytmp[:, 0, :], xt[:, :]).then_inc(s_rs, 1)
            dve.wait_ge(s_rs, 1)
            dve.wait_ge(s_lnc, CT)
            for ct in range(CT):
                v = glu[:, ct, PAD_A:WA]
                nc.vector.tensor_tensor(v, v, ytmp[:, 0, :], ALU.mult).then_inc(s_an, 1)
            for ct in range(CT):
                v = glu[:, ct, PAD_A:WA]
                dve.wait_ge(s_at, ct + 1)
                nc.vector.scalar_tensor_tensor(out=v, in0=xt[:, :], scalar=1.0, in1=v, op0=ALU.add,
                                               op1=ALU.mult).then_inc(s_as, 1)
            dve.wait_ge(s_as, CT)
            with dve.Fori(0, CT // 2) as i:
                for j in range(2):
                    ct = 2 * i + j
                    dve.wait_ge(s_zlo, 2 * CT + MP + ct)
                    gate_evac(S_AG + ct, j, X_AG + 2 * ct)
                    dve.wait_ge(s_pjfree, 2 * (S_AG + ct + 1))
                    v = glu[:, bass.ds(ct, 1), PAD_A:WA].rearrange("p o t -> p (o t)")
                    nc.vector.scalar_tensor_tensor(out=sg[:, :], in0=sg[:, :], scalar=0.25, in1=v,
                                                   op0=ALU.mult, op1=ALU.mult).then_inc(s_zpre, 1)
                    dve.wait_ge(s_zhi, 2 * CT + MP + ct + 1)
                    nc.vector.tensor_tensor(z_lo[:, bass.ds(ct, 1), :].rearrange("p o t -> p (o t)"), sg[:, :],
                                            z_hi[:, bass.ds(ct, 1), :].rearrange("p o t -> p (o t)"),
                                            ALU.subtract).then_inc(s_zlo, 1)
            with dve.Fori(0, DT // 2) as d2:
                merge_step(S_GA, X_GA, d2, adds=2 * DT)

            for k in range(KT):
                dve.wait_ge(s_woh, k + 1)
                nc.vector.tensor_tensor(wout_lo[:, k, :], w_raw[:, k % 2, :, :].rearrange("p a b -> p (a b)"),
                                        wout_hi[:, k, :], ALU.subtract).then_inc(s_wol, 1)
                dve.wait_ge(s_gh, k + 1)
                nc.vector.scalar_tensor_tensor(out=xT_lo[:, k, :], in0=merged[:, k, :], scalar=0.5, in1=xT_hi[:, k, :],
                                               op0=ALU.mult, op1=ALU.subtract).then_inc(s_gl, 1)
            dve.wait_ge(s_lnp, 32)
            for t in range(NT):
                q = t % 2
                if t >= 2:
                    dve.wait_ge(s_store[q], 16 * (t // 2))
                dve.wait_ge(s_xtk[q], 16 * (t // 2 + 1))
                for h in range(2):
                    dve.wait_ge(s_out_pj, 2 * t + h + 1)
                    nc.vector.scalar_tensor_tensor(out=y_tok[:, q, hs(h)], in0=x_tok[:, q, hs(h)], scalar=ALPHA,
                                                   in1=pj[:, (2 * t + h) % 4, :], op0=ALU.mult,
                                                   op1=ALU.add).then_inc(s_yk, 1)
                dve.wait_ge(s_yk, 2 * t + 2)
                for h in range(2):
                    op = nc.vector.bn_stats(stats[:, q, h, :], y_tok[:, q, hs(h)])
                op.then_inc(s_st, 1)
                dve.wait_ge(s_st, 1 + t + 1)
                nc.vector.bn_aggr(mv[:, q, :], stats[:, q, :, :]).then_inc(s_mvr, 1)
                dve.wait_ge(s_osd, t + 1)
                nc.vector.reciprocal(rinv[:, q, 0:1], rstd[:, q:q + 1]).then_inc(s_ors, 1)
                nc.vector.scalar_tensor_tensor(out=y_tok[:, q, :], in0=y_tok[:, q, :], scalar=mv[:, q, 0:1],
                                               in1=lng_b[:, :], op0=ALU.subtract, op1=ALU.mult).then_inc(s_t1, 1)
                dve.wait_ge(s_ors, t + 1)
                dve.wait_ge(s_t1, t + 1)
                nc.vector.scalar_tensor_tensor(out=y_tok[:, q, :], in0=y_tok[:, q, :], scalar=rinv[:, q, 0:1],
                                               in1=lnb_b[:, :], op0=ALU.mult, op1=ALU.add).then_inc(s_yo, 1)


def kernel(**inputs):
    import numpy as np
    import concourse.bacc as bacc
    from concourse.bass_utils import run_bass_kernel_spmd

    def one(name):
        return np.ascontiguousarray(np.asarray(inputs[name])[0])

    def columns(v):
        return np.ascontiguousarray(v.reshape(-1, P).T)

    x = one("x")
    arrays = {
        "xT": np.ascontiguousarray(x.T), "x": x, "mem": one("mem"), "w_in": one("w_in"),
        "b_forget": one("b_forget"), "conv_a_wT": np.ascontiguousarray(one("conv_a_w").T),
        "conv_a_b": columns(one("conv_a_b")), "ln_a_g": columns(one("ln_a_g")), "ln_a_b": columns(one("ln_a_b")),
        "conv_b_wT": np.ascontiguousarray(one("conv_b_w").T), "w_kv_mem": one("w_kv_mem"),
        "mem_ln_g": columns(np.asarray(inputs["mem_ln_g"])), "mem_ln_b": columns(np.asarray(inputs["mem_ln_b"])),
        "p_a": one("p_a"), "p_b": one("p_b"), "p_c": one("p_c"), "p_m": one("p_m"), "w_out": one("w_out"),
        "ln_g": one("ln_g"), "ln_b": one("ln_b"),
    }
    nc = bacc.Bacc("TRN2", target_bir_lowering=False, num_devices=1)
    args = {name: nc.dram_tensor(f"in_{name}", a.shape, F32, kind="ExternalInput").ap() for name, a in arrays.items()}
    out = nc.dram_tensor("out_y", x.shape, F32, kind="ExternalOutput").ap()
    hybrid_mixer(nc, out=out, **args)
    r = run_bass_kernel_spmd(nc, [{f"in_{name}": a for name, a in arrays.items()}], core_ids=[0])
    return r.results[0]["out_y"].reshape(inputs["x"].shape)
```

```python
from contextlib import ExitStack

import concourse.bass as bass
from concourse import mybir

F32 = mybir.dt.float32
F32R = mybir.dt.float32r
ACT = mybir.ActivationFunctionType
ALU = mybir.AluOpType
AX = mybir.AxisListType

P = 128
BIG = 1.0e30


def hybrid_mixer(nc, xT, x, mem, w_in, b_forget, conv_a_wT, conv_a_b, ln_a_g, ln_a_b, conv_b_wT,
                 w_kv_mem, mem_ln_g, mem_ln_b, p_a, p_b, p_c, p_m, w_out, ln_g, ln_b, out):
    D, T = xT.shape
    KT = D // P
    HALF = T // 2
    NT = T // P
    DT = D // P
    CONV_A, A_W = conv_a_wT.shape[1], conv_a_wT.shape[0]
    CONV_B, B_W = conv_b_wT.shape[1], conv_b_wT.shape[0]
    PAD_A, PAD_B = CONV_A - 1, CONV_B - 1
    HEADS = b_forget.shape[0]
    DH = 64
    C_W = HEADS * DH
    MEM = mem.shape[0]
    MT = MEM // P
    M_W = w_kv_mem.shape[1] // 2
    M_HEADS = M_W // DH
    CT = A_W // P
    MP = M_W // P
    QSCALE = DH ** -0.5
    ALPHA = 2.0 ** 0.25
    EPS = 1e-5
    assert A_W == B_W == C_W == CT * P and CT == 4 and NT == 8 and MT == 2 and MP == 2

    col, at = {}, 0
    for name, width in (("a_u", A_W), ("a_v", A_W), ("a_gate", A_W), ("b_h", B_W), ("b_b", B_W), ("b_c", B_W),
                        ("b_gate", B_W), ("q", C_W), ("k", C_W), ("v", C_W), ("f", HEADS), ("c_gate", C_W),
                        ("m_q", M_W), ("m_gate", M_W), ("g", 4 * D)):
        col[name] = at
        at += width
    assert at == w_in.shape[1]

    S_C = 3
    S_M = S_C + 4 * CT
    S_A = S_M + 1
    S_GC = S_A + 2 * CT
    S_GM = S_GC + 2 * DT
    S_B = S_GM + 2 * DT
    S_GB = S_B + 4 * CT
    S_AG = S_GB + 2 * DT
    S_GA = S_AG + CT
    S_END = S_GA + 2 * DT

    BASE = (nc.sbuf_base + 63) // 64 * 64
    KB = 1024

    def at_(name, shape, dt, off):
        return nc.alloc_sbuf_tensor_at(name, shape, dt, offset=BASE + off)

    xT_hi = at_("xT_hi", [P, KT, T], F32R, 0)
    xT_lo = at_("xT_lo", [P, KT, T], F32R, 32 * KB)
    w_raw = at_("w_raw", [P, 2, KT, P], F32, 64 * KB)
    w_hi = at_("w_hi", [P, 2, KT, P], F32R, 72 * KB)
    w_lo = at_("w_lo", [P, 2, KT, P], F32R, 80 * KB)
    z_hi = at_("z_hi", [P, CT, T], F32R, 104 * KB)
    z_lo = at_("z_lo", [P, CT, T], F32R, 88 * KB)
    z_raw = at_("z_raw", [P, CT, T], F32, 88 * KB)
    x_raw = at_("x_raw", [P, KT, T], F32, 88 * KB)
    wkv = at_("wkv", [P, KT, 2 * M_W], F32, 120 * KB)
    memT = at_("memT", [P, KT, MEM], F32, 136 * KB)
    mem_sb = at_("mem_sb", [P, MT, D], F32, 144 * KB)
    wf_stack = at_("wf_stack", [P, KT, P], F32R, 152 * KB)
    negcum = at_("negcum", [HEADS, T], F32, 156 * KB)
    f_z = at_("f_z", [HEADS, T], F32, 160 * KB)
    f_abs = at_("f_abs", [HEADS, T], F32, 164 * KB)
    f_e = at_("f_e", [HEADS, T], F32, 168 * KB)
    f_u = at_("f_u", [HEADS, T], F32, 172 * KB)
    f_r = at_("f_r", [HEADS, T], F32, 176 * KB)
    f_l = at_("f_l", [HEADS, T], F32, 180 * KB)
    q_stack = at_("q_stack", [P, 2, T], F32R, 120 * KB)
    k_stack_hi = at_("k_stack_hi", [P, 2, T], F32R, 128 * KB)
    k_stack_lo = at_("k_stack_lo", [P, 2, T], F32R, 136 * KB)
    v_stack = at_("v_stack", [P, 2, NT, 2, DH], F32R, 144 * KB)
    bias = at_("bias", [P, 2, T], F32, 152 * KB)
    probs = at_("probs", [P, 2, T], F32, 160 * KB)
    v_raw = at_("v_raw", [P, T], F32, 112 * KB)
    k_raw = at_("k_raw", [P, T], F32, 108 * KB)
    g_raw = at_("g_raw", [P, T], F32, 116 * KB)
    pT_hi = at_("pT_hi", [P, NT, 2 * P], F32R, 168 * KB)
    pT_lo = at_("pT_lo", [P, NT, 2 * P], F32R, 176 * KB)
    q_raw = at_("q_raw", [P, T], F32, 104 * KB)
    km_hi = at_("km_hi", [P, M_HEADS, MEM], F32R, 184 * KB)
    km_lo = at_("km_lo", [P, M_HEADS, MEM], F32R, 188 * KB)
    vm_stack = at_("vm_stack", [P, MT, M_HEADS, 2, DH], F32R, 192 * KB)
    xt = at_("xt", [P, T], F32, 196 * KB)
    sg = at_("sg", [P, T], F32, 200 * KB)
    q_stack1 = at_("q_stack1", [P, 2, T], F32R, 152 * KB)
    WA = PAD_A + T
    glu = at_("glu", [P, CT, WA], F32, 128 * KB)
    zm_raw = at_("zm_raw", [P, MP, T], F32, 144 * KB + 512)
    zm_lo = at_("zm_lo", [P, MP, T], F32R, 144 * KB + 512)
    zm_hi = at_("zm_hi", [P, MP, T], F32R, 152 * KB + 512)
    merged = at_("merged", [P, DT, T], F32, 164 * KB)
    ytmp = at_("ytmp", [P, 2, T], F32, 120 * KB)
    prod = at_("prod", [P, PAD_B + T], F32, 144 * KB + 512)
    cv = at_("cv", [P, T], F32, 149 * KB)
    bz = at_("bz", [P, T], F32, 153 * KB)
    ones_ln = at_("ones_ln", [P, P], F32, 157 * KB)
    an_rstd = at_("an_rstd", [P, T], F32, 149 * KB)
    wout_hi = at_("wout_hi", [P, KT, D], F32R, 128 * KB)
    wout_lo = at_("wout_lo", [P, KT, D], F32R, 88 * KB)
    lng_b = at_("lng_b", [P, D], F32, 120 * KB)
    lnb_b = at_("lnb_b", [P, D], F32, 124 * KB)
    x_tok = at_("x_tok", [P, 2, D], F32, 164 * KB)
    y_tok = at_("y_tok", [P, 2, D], F32, 172 * KB)
    off = [204 * KB]

    def small(name, shape, dt=F32):
        n = 4
        for d in shape[1:]:
            n *= d
        t = nc.alloc_sbuf_tensor_at(name, shape, dt, offset=BASE + off[0], align_bytes=8)
        off[0] += (n + 7) // 8 * 8
        return t

    ident = small("ident", [P, P])
    otmp = small("otmp", [P, 2 * P])
    maskc = small("maskc", [P, P])
    bdiag = small("bdiag", [P, 2, P])
    cwk = small("cwk", [P, CONV_A + 1])
    cwa = small("cwa", [P, CT, CONV_A])
    cwb = small("cwb", [P, CT, CONV_B])
    cab = small("cab", [P, CT])
    lag = small("lag", [P, CT])
    lab = small("lab", [P, CT])
    eps = small("eps", [P, 1])
    rmin = small("rmin", [P, 2, 2])
    rsum = small("rsum", [P, 2, 2])
    rinv = small("rinv", [P, 2, 2])
    mv = small("mv", [P, 2, 2])
    rstd = small("rstd", [P, 2])
    wf_raw = at_("wf_raw", [P, KT, HEADS], F32, 184 * KB)
    memg = at_("memg", [P, KT], F32, 188 * KB)
    memb = at_("memb", [P, KT], F32, 188 * KB + 32)
    bf = at_("bf", [HEADS, 1], F32, 188 * KB + 64)
    stats = at_("stats", [P, 2, 2, 6], F32, 195 * KB)
    assert BASE + off[0] <= nc.sbuf_usable_end, (BASE + off[0], nc.sbuf_usable_end)

    cum_dram = nc.dram_tensor("cum_scratch", [HEADS, T], F32, kind="Internal").ap()

    ctx = ExitStack()
    with ctx:
        pj = ctx.enter_context(nc.psum_tensor("pj", [P, 4, HALF], F32))
        pt = ctx.enter_context(nc.psum_tensor("pt", [P, 2, HALF], F32))
        po = ctx.enter_context(nc.psum_tensor("po", [P, 2, HALF], F32))

        def sem(name):
            return ctx.enter_context(nc.semaphore(name))

        s_passed = [sem("vector_passed"), sem("sync_passed")]
        s_x = [sem(f"x_loaded{i}") for i in range(4)]
        s_par = sem("params_loaded")
        s_wf = sem("wf_loaded")
        s_mem = sem("mem_loaded")
        s_wkv = sem("wkv_loaded")
        s_cst = sem("constants_made")
        s_fix = sem("small_setup_done")
        s_xhi = sem("x_hi_made")
        s_xlo = sem("x_lo_made")
        s_wld = [sem(f"w_raw_loaded{i}") for i in range(2)]
        s_whi = sem("w_hi_made")
        s_wlo = sem("w_lo_made")
        s_pj = sem("half_accumulated")
        s_pjfree = sem("half_evacuated")
        s_xt = sem("xt_written")
        s_wfs = sem("wf_stack_made")
        s_f = sem("f_accumulated")
        s_fa = sem("f_scalar_steps")
        s_fv = sem("f_vector_steps")
        s_cumst = sem("cum_stored")
        s_ms = sem("mem_stats")
        s_mr = sem("mem_std")
        s_mn = sem("mem_normalised")
        s_mt = sem("mem_transposed")
        s_mte = sem("memT_written")
        s_kv = sem("mem_kv_accumulated")
        s_kvh = sem("mem_kv_hi_made")
        s_kvl = sem("mem_kv_lo_made")
        s_bias = [sem(f"bias_loaded{a}") for a in range(2)]
        s_stkh = sem("stack_hi_made")
        s_stkl = sem("stack_lo_made")
        s_s = sem("scores_ready")
        s_bd = sem("diag_bias_made")
        s_dm = sem("diag_min")
        s_sp = sem("scores_biased")
        s_e = sem("probs_exp")
        s_ri = sem("row_sum_inverted")
        s_pn = sem("probs_normalised")
        s_tb = sem("transposed")
        s_thi = sem("pT_hi_made")
        s_tlo = sem("pT_lo_made")
        s_pv = sem("pv_accumulated")
        s_osh = sem("o_half_shifted")
        s_oadd = sem("o_halves_added")
        s_og = sem("o_gated")
        s_zpre = sem("z_product_made")
        s_zhi = sem("z_hi_made")
        s_zlo = sem("z_lo_made")
        s_cw = sem("conv_weights_ready")
        s_ca = sem("conv_steps")
        s_cb = sem("convb_steps")
        s_bt = sem("b_times_conv")
        s_yt = sem("gated_y_made")
        s_add = sem("branch_added")
        s_lnm = sem("ln_mean_accumulated")
        s_lnc = sem("ln_centred")
        s_sq = sem("ln_squared")
        s_lnv = sem("ln_var_accumulated")
        s_sd = sem("ln_std")
        s_rs = sem("ln_rstd")
        s_an = sem("a_scaled")
        s_ag = sem("a_affine")
        s_at = sem("a_tanh")
        s_as = sem("a_silu_made")
        s_woh = sem("wout_hi_made")
        s_wol = sem("wout_lo_made")
        s_gh = sem("merged_hi_made")
        s_gl = sem("merged_lo_made")
        s_lnp = sem("ln_params_loaded")
        s_xtk = [sem(f"x_tok_loaded{i}") for i in range(2)]
        s_out_pj = sem("out_half_accumulated")
        s_yk = sem("residual_added")
        s_st = sem("out_stats")
        s_mvr = sem("out_mean_var")
        s_osd = sem("out_std")
        s_ors = sem("out_rstd")
        s_t1 = sem("out_centred")
        s_yo = sem("out_ready")
        s_store = [sem(f"out_stored{i}") for i in range(2)]

        block = ctx.enter_context(nc.Block())

        F_STEPS = 10
        STK_HEAD = 3
        STK_PAIR = 2 * STK_HEAD
        CONV_STEPS = 1 + 2 * CT * CONV_A
        X_M = 2 * CT + 2
        X_A = X_M + 2
        X_GC = X_A + 2 * CT
        X_GM = X_GC + 2 * DT
        X_B = X_GM + 2 * DT
        X_GB = X_B + 4 * CT
        X_AG = X_GB + 2 * DT
        X_GA = X_AG + 2 * CT
        UNITS = 2 * NT

        def batches(i):
            first, last = 1 - i % 2, 2 * (i // 2) + 1
            slots = list(range(first, last + 1))
            return [slots[n:n + 4] for n in range(0, len(slots), 4)]

        TB_HEAD = sum(len(batches(i)) for i in range(NT))
        TB_PAIR = 2 + 2 * TB_HEAD

        def tb_before(u):
            return 2 + (u // NT) * TB_HEAD + sum(len(batches(i)) for i in range(u % NT))

        PV_PAIR = 2 * (NT // 2)
        assert TB_PAIR % 2 == 0

        M_STARTS, M_ENDS = {}, {}
        for n, s in enumerate(range(S_M, S_GC - 2)):
            first, per, w0 = (2 * KT * n, 6, 0) if n < 3 else (2 * KT * (n - 3), 8, NT)
            M_STARTS.setdefault(w0 + first // per, []).append(s)
            for h in range(2):
                M_ENDS.setdefault(w0 + (first + KT * (h + 1) - 1) // per + 1, []).append((s, h))

        def raw_count(s_half, j):
            return 16 * (s_half + j // 2 + 1)

        @block.sync
        def _(sp):
            def load_w(s, j, src, nk):
                sp.wait_ge(s_wlo, 2 * (s - 1))
                sp.sem_inc(s_passed[1], 1)
                sp.dma_start(w_raw[:, j % 2, 0:nk, :], src).then_inc(s_wld[j % 2], 16)

            def wcols(c0):
                if not isinstance(c0, int):
                    c0 = sp.snap(c0)
                return w_in[:, bass.ds(c0, P)].rearrange("(k p) c -> p k c", p=P)

            def pcols(w, dt):
                return w[:, bass.ds(sp.snap(dt * P), P)].rearrange("(k p) c -> p k c", p=P)

            xv = xT.rearrange("(k p) t -> p k t", p=P)
            sp.dma_start(wf_raw[:, :, :], w_in[:, col["f"]:col["f"] + HEADS].rearrange("(k p) c -> p k c", p=P)
                         ).then_inc(s_wf, 16)
            for i in range(4):
                sp.dma_start(x_raw[:, 2 * i:2 * i + 2, :], xv[:, 2 * i:2 * i + 2, :]).then_inc(s_x[i], 16)
            sp.dma_start(mem_sb[:, :, :], mem.rearrange("(m p) d -> p m d", p=P)).then_inc(s_mem, 16)
            sp.dma_start(w_raw[:, 0, :, :], wcols(col["q"])).then_inc(s_wld[0], 16)
            sp.dma_start(wkv[:, :, :], w_kv_mem.rearrange("(k p) c -> p k c", p=P)).then_inc(s_wkv, 16)
            sp.dma_start(w_raw[:, 1, :, :], wcols(col["k"])).then_inc(s_wld[1], 16)
            for t, src in ((cwa[:, :, :], conv_a_wT.rearrange("(c p) k -> p c k", p=P)),
                           (cwb[:, :, :], conv_b_wT.rearrange("(c p) k -> p c k", p=P)),
                           (cab[:, :], conv_a_b),
                           (lag[:, :], ln_a_g),
                           (lab[:, :], ln_a_b),
                           (memg[:, :], mem_ln_g),
                           (memb[:, :], mem_ln_b),
                           (bf[:, :], b_forget.rearrange("(h o) -> h o", o=1))):
                sp.dma_start(t, src).then_inc(s_par, 16)
            load_w(2, 0, wcols(col["v"]), KT)
            load_w(3, 1, wcols(col["q"] + P), KT)
            sp.wait_ge(s_fv, F_STEPS)
            sp.dma_start(cum_dram[:, :], negcum[:, :]).then_inc(s_cumst, 16)
            sp.wait_ge(s_cumst, 16)
            for a in range(2):
                sp.dma_start(bias[:, a, :], cum_dram[a, :].partition_broadcast(P)).then_inc(s_bias[a], 16)
            load_w(4, 0, wcols(col["k"] + P), KT)
            load_w(5, 1, wcols(col["v"] + P), KT)

            def bias_row(c, a):
                sp.wait_ge(s_sp, UNITS * c + NT * (a + 1))
                sp.sem_inc(s_passed[1], 1)
                sp.dma_start(bias[:, a, :], cum_dram[2 * c + 2 + a, :].partition_broadcast(P)).then_inc(s_bias[a], 16)

            with sp.Fori(0, CT - 2) as c:
                load_w(4 * c + 6, 0, wcols(col["c_gate"] + c * P), KT)
                load_w(4 * c + 7, 1, wcols(col["q"] + (c + 2) * P), KT)
                bias_row(c, 0)
                load_w(4 * c + 8, 0, wcols(col["k"] + (c + 2) * P), KT)
                load_w(4 * c + 9, 1, wcols(col["v"] + (c + 2) * P), KT)
                bias_row(c, 1)
            c = CT - 2
            load_w(4 * c + 6, 0, wcols(col["c_gate"] + c * P), KT)
            load_w(4 * c + 7, 1, wcols(col["m_q"]), KT)
            bias_row(c, 0)
            load_w(4 * c + 8, 0, wcols(col["m_q"] + P), KT)
            load_w(4 * c + 9, 1, wcols(col["m_gate"]), KT)
            bias_row(c, 1)
            load_w(4 * c + 10, 0, wcols(col["c_gate"] + (CT - 1) * P), KT)
            load_w(S_M, 1, wcols(col["m_gate"] + P), KT)
            for ct in range(CT):
                load_w(S_A + 2 * ct, 0, wcols(col["a_v"] + ct * P), KT)
                load_w(S_A + 2 * ct + 1, 1, wcols(col["a_u"] + ct * P), KT)

            def merge_loads(s0, branch, w, nk):
                with sp.Fori(0, DT) as dt:
                    load_w(s0 + 2 * dt, 0, wcols(col["g"] + branch * D + dt * P), KT)
                    load_w(s0 + 2 * dt + 1, 1, pcols(w, dt), nk)

            merge_loads(S_GC, 2, p_c, CT)
            merge_loads(S_GM, 3, p_m, MP)
            with sp.Fori(0, CT) as ct:
                for j, name in enumerate(("b_c", "b_h", "b_gate", "b_b")):
                    load_w(S_B + 4 * ct + j, j, wcols(col[name] + ct * P), KT)
            merge_loads(S_GB, 1, p_b, CT)
            with sp.Fori(0, CT // 2) as i:
                for j in range(2):
                    load_w(S_AG + 2 * i + j, j, wcols(col["a_gate"] + (2 * i + j) * P), KT)
            merge_loads(S_GA, 0, p_a, CT)
            wo_v = w_out.rearrange("(k p) c -> k p c", p=P)
            for k in range(KT):
                s = S_END + k
                if k < 2:
                    sp.wait_ge(s_wlo, 2 * (s - 1))
                else:
                    sp.wait_ge(s_wol, k - 1)
                sp.dma_start(w_raw[:, k % 2, :, :].rearrange("p a b -> p (a b)"), wo_v[k]).then_inc(s_wld[k % 2], 16)
            sp.wait_ge(s_add, 3 * DT)
            sp.dma_start(lng_b[:, :], ln_g.partition_broadcast(P)).then_inc(s_lnp, 16)
            sp.dma_start(lnb_b[:, :], ln_b.partition_broadcast(P)).then_inc(s_lnp, 16)
            sp.wait_ge(s_gl, DT)
            for t in range(NT):
                if t >= 2:
                    sp.wait_ge(s_yk, 2 * (t - 1))
                sp.dma_start(x_tok[:, t % 2, :], x[t * P:(t + 1) * P, :]).then_inc(s_xtk[t % 2], 16)
                if t >= 1:
                    sp.wait_ge(s_yo, t)
                    sp.dma_start(out[(t - 1) * P:t * P, :], y_tok[:, (t - 1) % 2, :]).then_inc(s_store[(t - 1) % 2], 16)
            sp.wait_ge(s_yo, NT)
            sp.dma_start(out[(NT - 1) * P:NT * P, :], y_tok[:, (NT - 1) % 2, :]).then_inc(s_store[(NT - 1) % 2], 16)
            for i in range(2):
                sp.wait_ge(s_store[i], 16 * (NT // 2))

        @block.tensor
        def _(pe):
            def k_steps(s, j, h, k0, k1, bank, nk=KT, r_hi=xT_hi, r_lo=xT_lo):
                t = slice(h * HALF, (h + 1) * HALF)
                for k in range(k0, k1):
                    if h == 0 and k % (nk // 2) == 0:
                        pe.wait_ge(s_wlo, 2 * s + 1 + k // (nk // 2))
                    nc.tensor.matmul(pj[:, bank, :], w_hi[:, j % 2, k, :], r_hi[:, k, t], start=k == 0, stop=False)
                    nc.tensor.matmul(pj[:, bank, :], w_hi[:, j % 2, k, :], r_lo[:, k, t], start=False, stop=False)
                    mm = nc.tensor.matmul(pj[:, bank, :], w_lo[:, j % 2, k, :], r_hi[:, k, t],
                                          start=False, stop=k == nk - 1)
                if k1 == nk:
                    mm.then_inc(s_pj, 1)

            def stream_tile(s, j, nk=KT, r_hi=xT_hi, r_lo=xT_lo, back=3):
                for h in range(2):
                    if back == 3:
                        pe.wait_ge(s_pjfree, 2 * s + h - 3)
                    elif back == 0 and h == 0:
                        pe.wait_ge(s_pjfree, 2 * s)
                    k_steps(s, j, h, 0, nk, 2 * (j % 2) + h, nk, r_hi, r_lo)

            def stream_part(s, j, n0, n1):
                for n in range(n0, n1):
                    d, h, k = n // (2 * KT), n // KT % 2, n % KT
                    if k == 0:
                        pe.wait_ge(s_pjfree, 2 * (s + d) + h - 1)
                    k_steps(s + d, j + d, h, k, k + 1, h)

            pe.wait_ge(s_wfs, 2)
            for h in range(2):
                for k in range(KT):
                    if h == 0:
                        pe.wait_ge(s_xlo, k + 1)
                    for n, r in enumerate((xT_hi, xT_lo)):
                        mm = nc.tensor.matmul(po[:, h, :], wf_stack[:, k, :], r[:, k, h * HALF:(h + 1) * HALF],
                                              start=k == 0 and n == 0, stop=k == KT - 1 and n == 1)
                mm.then_inc(s_f, 1)
            pe.wait_ge(s_cst, 2)
            n = 0
            for m in range(MT):
                pe.wait_ge(s_mn, m + 1)
                for kb in range(KT // 4):
                    if n >= 2:
                        pe.wait_ge(s_mte, n - 1)
                    for k in range(4):
                        mm = nc.tensor.transpose(pt[:, n % 2, k * P:(k + 1) * P],
                                                 mem_sb[:, m, (4 * kb + k) * P:(4 * kb + k + 1) * P], ident[:, :])
                    mm.then_inc(s_mt, 1)
                    n += 1
            pe.wait_ge(s_mte, n)
            pe.wait_ge(s_wkv, 16)
            pe.wait_ge(s_fv, 1)
            for c in range(MP):
                for k in range(KT):
                    mm = nc.tensor.matmul(po[:, c, 0:MEM], wkv[:, k, c * P:(c + 1) * P], memT[:, k, :],
                                          start=k == 0, stop=k == KT - 1)
                mm.then_inc(s_kv, 1)
            for m in range(MT):
                for k in range(KT):
                    mm = nc.tensor.matmul(pt[:, m, 0:M_W], memT[:, k, m * P:(m + 1) * P], wkv[:, k, M_W:2 * M_W],
                                          start=k == 0, stop=k == KT - 1)
                mm.then_inc(s_kv, 1)

            scores_ps = pj[:, 2:4, :].rearrange("p a b -> p (a b)")

            def scores(c, u):
                un, a, i = UNITS * c, u // NT % 2, u % NT
                if u % NT == 0:
                    pe.wait_ge(s_stkl, STK_PAIR * c + STK_HEAD * (u // NT + 1))
                if u > 0:
                    pe.wait_ge(s_sp, un + u)
                L = max(i + 1, 2) * P
                parts = [(0, min(L, HALF))] + ([(HALF, max(L, HALF + 2 * P))] if L > HALF else [])
                for k0, k1 in parts:
                    nc.tensor.matmul(scores_ps[:, k0:k1], q_stack[:, a, i * P:(i + 1) * P],
                                     k_stack_hi[:, a, k0:k1], start=True, stop=False)
                    mm = nc.tensor.matmul(scores_ps[:, k0:k1], q_stack[:, a, i * P:(i + 1) * P],
                                          k_stack_lo[:, a, k0:k1], start=False, stop=True)
                mm.then_inc(s_s, 1)

            def turn(c, u):
                i = u % NT
                top = 2 * (i // 2) + 1
                pe.wait_ge(s_pn, UNITS * c + u + 1)
                for n, slots in enumerate(batches(i)):
                    x_ = tb_before(u) + n
                    pe.wait_ge(s_tlo, TB_PAIR * c + x_ - 1)
                    for q, slot in enumerate(slots):
                        kt = top - slot
                        mm = nc.tensor.transpose(pt[:, x_ % 2, q * P:(q + 1) * P],
                                                 probs[:, u % 2, kt * P:(kt + 1) * P], ident[:, :])
                    mm.then_inc(s_tb, 1)

            def weigh(c, n):
                a, top = n // (NT // 2), 2 * (n % (NT // 2)) + 1
                u = 2 * n + 1
                pe.wait_ge(s_tlo, TB_PAIR * c + tb_before(u) + len(batches(u % NT)))
                if n >= 2:
                    pe.wait_ge(s_oadd, PV_PAIR * c + n - 1)
                for slot in range(top + 1):
                    for r in (pT_hi, pT_lo):
                        mm = nc.tensor.matmul(po[:, n % 2, 0:2 * P],
                                              v_stack[:, a, top - slot, :, :].rearrange("p a b -> p (a b)"),
                                              r[:, slot, :], start=slot == 0 and r is pT_hi,
                                              stop=slot == top and r is pT_lo)
                mm.then_inc(s_pv, 1)

            def pair(c, last):
                s = 4 * c
                pe.wait_ge(s_pjfree, 8 * c + 6)
                for b in range(2):
                    for k in range(4):
                        mm = nc.tensor.transpose(pt[:, b, k * P:(k + 1) * P],
                                                 v_raw[:, (4 * b + k) * P:(4 * b + k + 1) * P], ident[:, :])
                    mm.then_inc(s_tb, 1)
                for u in range(UNITS):
                    stream_part(s + S_C, S_C, 4 * u, 4 * u + 2)
                    turn(c, u)
                    stream_part(s + S_C, S_C, 4 * u + 2, 4 * u + 4)
                    if u % 2 == 0 and u:
                        weigh(c, u // 2 - 1)
                    if u + 2 < UNITS or not last:
                        scores(c, u + 2)
                weigh(c, UNITS // 2 - 1)

            pe.wait_ge(s_kvl, 2 * MP + MT)
            for s in range(S_C):
                stream_tile(s, s, back=None if s < 2 else 3)
            scores(0, 0)
            scores(0, 1)
            with pe.Fori(0, CT - 1) as c:
                pair(c, False)
            pair(CT - 1, True)

            TB, PV, UN = TB_PAIR * CT, PV_PAIR * CT, UNITS * CT

            def mscores(w):
                m, i = w // NT, w % NT
                if i == 0:
                    pe.wait_ge(s_stkl, STK_PAIR * CT + 2 * (m + 1))
                if w >= 2:
                    pe.wait_ge(s_e, UN + w - 1)
                for a in range(2):
                    q = (q_stack, q_stack1)[m][:, a, i * P:(i + 1) * P]
                    o = pj[:, 2 + w % 2, a * MEM:(a + 1) * MEM]
                    nc.tensor.matmul(o, q, km_hi[:, 2 * m + a, :], start=True, stop=False)
                    mm = nc.tensor.matmul(o, q, km_lo[:, 2 * m + a, :], start=False, stop=True)
                mm.then_inc(s_s, 1)

            def mweigh(g):
                pe.wait_ge(s_tlo, TB + 2 * g + 2)
                for a in range(2):
                    pe.wait_ge(s_oadd, PV + 2 * g + a - 1)
                    for t in range(MT):
                        for r in (pT_hi, pT_lo):
                            mm = nc.tensor.matmul(
                                po[:, a, 0:2 * P],
                                vm_stack[:, t, 2 * (g // (NT // 2)) + a, :, :].rearrange("p a b -> p (a b)"),
                                r[:, MT * a + t, :], start=t == 0 and r is pT_hi, stop=t == MT - 1 and r is pT_lo)
                    mm.then_inc(s_pv, 1)

            pe.wait_ge(s_sp, UN)
            mscores(0)
            mscores(1)
            for w in range(2 * NT):
                s, n0, d = (S_M, 6 * w, 3) if w < NT else (S_M + 3, 8 * (w - NT), 4)
                stream_part(s, s, n0, n0 + d)
                pe.wait_ge(s_pn, UN + w + 1)
                pe.wait_ge(s_tlo, TB + w - 1)
                for q in range(2 * MT):
                    mm = nc.tensor.transpose(pt[:, w % 2, q * P:(q + 1) * P],
                                             probs[:, w % 2, q * P:(q + 1) * P], ident[:, :])
                mm.then_inc(s_tb, 1)
                stream_part(s, s, n0 + d, n0 + 2 * d)
                if w % 2 == 0 and w:
                    mweigh(w // 2 - 1)
                if w + 2 < 2 * NT:
                    mscores(w + 2)
            mweigh(NT - 1)
            for j in range(2):
                stream_tile(S_GC - 2 + j, j, back=0)

            def merge(s0, nk, r_hi, r_lo):
                with pe.Fori(0, DT) as dt:
                    stream_tile(s0 + 2 * dt, 0)
                    stream_tile(s0 + 2 * dt + 1, 1, nk, r_hi, r_lo)

            pe.wait_ge(s_zlo, CT)
            merge(S_GC, CT, z_hi, z_lo)
            pe.wait_ge(s_zlo, CT + MP)
            merge(S_GM, MP, zm_hi, zm_lo)
            pe.wait_ge(s_cst, 3)
            pe.wait_ge(s_ca, CONV_STEPS)
            for h in range(2):
                for ct in range(CT):
                    mm = nc.tensor.matmul(pt[:, h, :], ones_ln[:, :], glu[:, ct, PAD_A + h * HALF:PAD_A + (h + 1) * HALF],
                                          start=ct == 0, stop=ct == CT - 1)
                mm.then_inc(s_lnm, 1)
            for j in range(2):
                stream_tile(S_B + j, j)
            pe.wait_ge(s_sq, CT)
            for h in range(2):
                for ct in range(CT):
                    mm = nc.tensor.matmul(po[:, h, :], ones_ln[:, :], z_raw[:, ct, h * HALF:(h + 1) * HALF],
                                          start=ct == 0, stop=ct == CT - 1)
                mm.then_inc(s_lnv, 1)
            for j in range(2, 4):
                stream_tile(S_B + j, j)
            with pe.Fori(1, CT) as ct:
                for j in range(4):
                    stream_tile(S_B + 4 * ct + j, j)
            pe.wait_ge(s_zlo, CT + MP + CT)
            merge(S_GB, CT, z_hi, z_lo)
            with pe.Fori(0, CT // 2) as i:
                for j in range(2):
                    stream_tile(S_AG + 2 * i + j, j)
            pe.wait_ge(s_zlo, CT + MP + 2 * CT)
            merge(S_GA, CT, z_hi, z_lo)

            for t in range(NT):
                for h in range(2):
                    n = 2 * t + h
                    if n < 4:
                        pe.wait_ge(s_pjfree, 2 * S_END)
                    else:
                        pe.wait_ge(s_yk, n - 3)
                    for k in range(KT):
                        if t == 0 and h == 0:
                            pe.wait_ge(s_gl, k + 1)
                            pe.wait_ge(s_wol, k + 1)
                        tk, c = slice(t * P, (t + 1) * P), slice(h * HALF, (h + 1) * HALF)
                        nc.tensor.matmul(pj[:, n % 4, :], xT_hi[:, k, tk], wout_hi[:, k, c], start=k == 0, stop=False)
                        nc.tensor.matmul(pj[:, n % 4, :], xT_hi[:, k, tk], wout_lo[:, k, c], start=False, stop=False)
                        mm = nc.tensor.matmul(pj[:, n % 4, :], xT_lo[:, k, tk], wout_hi[:, k, c],
                                              start=False, stop=k == KT - 1)
                    mm.then_inc(s_out_pj, 1)

        @block.scalar
        def _(act):
            def split_w(sh, j, nk=KT, free=True):
                act.wait_ge(s_wld[j % 2], raw_count(sh, j))
                if free:
                    act.wait_ge(s_pj, 4 * sh + 2 * j - 2)
                for e in range(2):
                    k = slice(e * nk // 2, (e + 1) * nk // 2)
                    nc.scalar.activation(w_hi[:, j % 2, k, :], w_raw[:, j % 2, k, :], ACT.Copy).then_inc(s_whi, 1)

            def evac_half(s, bank, h, func, scale):
                act.wait_ge(s_pj, 2 * s + h + 1)
                if h == 0:
                    act.wait_ge(s_pjfree, 2 * s)
                nc.scalar.activation(xt[:, h * HALF:(h + 1) * HALF], pj[:, bank, :], func, scale=scale).then_inc(s_xt, 1)

            def evac(s, j, func, scale):
                for h in range(2):
                    evac_half(s, 2 * (j % 2) + h, h, func, scale)

            act.wait_ge(s_wf, 16)
            act.wait_ge(s_wfs, 1)
            nc.scalar.activation(wf_stack[:, :, 0:HEADS], wf_raw[:, :, :], ACT.Copy).then_inc(s_fa, 1)
            for k in range(KT):
                act.wait_ge(s_x[k // 2], 16)
                nc.scalar.activation(xT_hi[:, k, :], x_raw[:, k, :], ACT.Copy).then_inc(s_xhi, 1)
            split_w(0, 0, free=False)
            split_w(0, 1, free=False)
            act.wait_ge(s_ms, MT)
            act.wait_ge(s_fix, 1)
            nc.scalar.activation(rstd[:, 0:MT], mv[:, :, 1], ACT.Sqrt, bias=eps[:, 0:1]).then_inc(s_mr, 1)
            for h in range(2):
                act.wait_ge(s_f, h + 1)
                nc.scalar.activation(f_l[:, h * HALF:(h + 1) * HALF], po[32:32 + HEADS, h, :],
                                     ACT.Copy).then_inc(s_fa, 1)
            act.wait_ge(s_fv, 1)
            nc.scalar.activation(f_abs[:, :], f_z[:, :], ACT.Abs).then_inc(s_fa, 1)
            act.wait_ge(s_fa, 4)
            nc.scalar.activation(f_e[:, :], f_abs[:, :], ACT.Exp, scale=-1.0).then_inc(s_fa, 1)
            act.wait_ge(s_fv, 2)
            nc.scalar.activation(f_l[:, :], f_u[:, :], ACT.Ln).then_inc(s_fa, 1)
            for c in range(MP):
                act.wait_ge(s_kv, c + 1)
                for a in range(2):
                    b, o = DH * a, DH * (1 - a)
                    for r in (b, o):
                        op = nc.scalar.activation(km_hi[r:r + DH, 2 * c + a, :], po[b:b + DH, c, 0:MEM], ACT.Copy)
                    op.then_inc(s_kvh, 1)
            for m in range(MT):
                act.wait_ge(s_kv, MP + m + 1)
                nc.scalar.activation(vm_stack[:, m, :, 0, :],
                                     pt[:, m, 0:M_W].rearrange("p (h d) -> p h d", d=DH), ACT.Copy).then_inc(s_kvh, 1)

            def out_shift(a, n, count, first=False):
                b, o = DH * a, DH * (1 - a)
                act.wait_ge(s_pv, count + 1)
                if not first:
                    act.wait_ge(s_oadd, count)
                nc.scalar.activation(otmp[b:b + DH, :], po[o:o + DH, n % 2, 0:2 * P], ACT.Copy).then_inc(s_osh, 1)

            def q_hi(a, src, dst):
                b = DH * a
                nc.scalar.activation(dst[b:b + DH, a, :], src[b:b + DH, :], ACT.Copy).then_inc(s_stkh, 1)

            def k_hi(a):
                b = DH * a
                for r in (b, DH - b):
                    nc.scalar.activation(k_stack_hi[r:r + DH, a, :], k_raw[b:b + DH, :], ACT.Copy).then_inc(s_stkh, 1)

            def exp(c, u):
                i = u % NT
                act.wait_ge(s_sp, UNITS * c + u + 1)
                nc.scalar.activation(probs[:, u % 2, 0:(i + 1) * P], probs[:, u % 2, 0:(i + 1) * P], ACT.Exp,
                                     scale=-1.0, bias=rmin[:, u % 2, 1:2],
                                     accum_out=rsum[:, u % 2, 0:1]).then_inc(s_e, 1)

            def turned_hi(c, u):
                i = u % NT
                for n, slots in enumerate(batches(i)):
                    act.wait_ge(s_tb, TB_PAIR * c + tb_before(u) + n + 1)
                    if i % 2 == 0 and n == 0 and u > 0:
                        act.wait_ge(s_pv, PV_PAIR * c + u // 2)
                    nc.scalar.activation(
                        pT_hi[:, slots[0]:slots[-1] + 1, (i % 2) * P:(i % 2 + 1) * P],
                        pt[:, (tb_before(u) + n) % 2, 0:len(slots) * P].rearrange("p (k q) -> p k q", q=P),
                        ACT.Copy).then_inc(s_thi, 1)

            def pair(c, last):
                s = 4 * c
                for b in range(2):
                    act.wait_ge(s_tb, TB_PAIR * c + b + 1)
                    nc.scalar.activation(v_stack[:, :, 4 * b:4 * b + 4, 0, :].rearrange("p a k d -> p k a d"),
                                         pt[:, b, :].rearrange("p (k a d) -> p k a d", k=4, a=2),
                                         ACT.Copy).then_inc(s_thi, 1)
                for k in range(UNITS):
                    if k:
                        turned_hi(c, k - 1)
                    if k + 1 < UNITS or not last:
                        exp(c, k + 1)
                    if k % 2 == 0 and k:
                        out_shift((k // 2 - 1) // (NT // 2), k // 2 - 1, PV_PAIR * c + k // 2 - 1, first=k == 2)
                    if k % 4 == 0:
                        split_w(2 * c, 4 + k // 4)
                    for a, kq, kk in ((0, 9, 10), (1, 14, 15)):
                        if k == kq:
                            act.wait_ge(s_s, UNITS * c + NT * (a + 1))
                            act.wait_ge(s_pjfree, 8 * c + 8)
                            q_hi(a, q_raw, q_stack)
                        if k == kk and not last:
                            act.wait_ge(s_pjfree, 8 * c + 10)
                            k_hi(a)
                    if last and k in (10, 12):
                        evac_half(s + 5, k // 2 - 5, k // 2 - 5, ACT.Tanh, 0.5)
                    if k == 14:
                        evac_half(s + 6, 0, 0, ACT.Tanh, 0.5)
                turned_hi(c, UNITS - 1)
                evac_half(s + 6, 1, 1, ACT.Tanh, 0.5)
                out_shift(1, UNITS // 2 - 1, PV_PAIR * c + UNITS // 2 - 1)

            split_w(1, 0)
            act.wait_ge(s_pjfree, 2)
            q_hi(0, q_raw, q_stack)
            act.wait_ge(s_pjfree, 4)
            k_hi(0)
            q_hi(1, q_raw, q_stack)
            k_hi(1)
            split_w(1, 1)
            exp(0, 0)
            with act.Fori(0, CT - 1) as c:
                pair(c, False)
            pair(CT - 1, True)

            TB, PV, UN = TB_PAIR * CT, PV_PAIR * CT, UNITS * CT

            def mexp(w):
                act.wait_ge(s_sp, UN + w + 1)
                if w >= 2:
                    act.wait_ge(s_tb, TB + w - 1)
                for a in range(2):
                    op = nc.scalar.activation(probs[:, w % 2, a * MEM:(a + 1) * MEM],
                                              pj[:, 2 + w % 2, a * MEM:(a + 1) * MEM], ACT.Exp,
                                              bias=rmin[:, w % 2, a:a + 1], accum_out=rsum[:, w % 2, a:a + 1])
                op.then_inc(s_e, 1)

            def mturned_hi(w):
                act.wait_ge(s_tb, TB + w + 1)
                if w % 2 == 0:
                    act.wait_ge(s_pv, PV + w)
                nc.scalar.activation(pT_hi[:, 0:2 * MT, (w % 2) * P:(w % 2 + 1) * P],
                                     pt[:, w % 2, :].rearrange("p (k q) -> p k q", q=P), ACT.Copy).then_inc(s_thi, 1)

            mexp(0)
            for w in range(2 * NT):
                if w:
                    mturned_hi(w - 1)
                if w + 1 < 2 * NT:
                    mexp(w + 1)
                for s, h in M_ENDS.get(w, ()):
                    if s == S_M or (s - S_A) % 2 == 0:
                        evac_half(s, h, h, ACT.Tanh, 0.5)
                if w % 2 == 0 and w:
                    for a in range(2):
                        out_shift(a, a, PV + w - 2 + a)
                for s in M_STARTS.get(w, ()):
                    split_w((s + 1) // 2, (s + 1) % 2)
                if w in (2, 3):
                    if w == 2:
                        act.wait_ge(s_dm, 1 + UNITS * CT)
                    q_hi(w - 2, k_raw, q_stack1)
            mturned_hi(2 * NT - 1)
            for s, h in M_ENDS[2 * NT]:
                if (s - S_A) % 2 == 0:
                    evac_half(s, h, h, ACT.Tanh, 0.5)
            for a in range(2):
                out_shift(a, a, PV + 2 * NT - 2 + a)
            split_w(S_GC // 2 - 1, 1)
            for ct in range(CT):
                if ct == 0:
                    act.wait_ge(s_zpre, CT + MP)
                nc.scalar.activation(z_hi[:, ct, :], z_raw[:, ct, :], ACT.Copy).then_inc(s_zhi, 1)
            evac(S_GC - 2, 0, ACT.Tanh, 0.5)
            for m in range(MP):
                nc.scalar.activation(zm_hi[:, m, :], zm_raw[:, m, :], ACT.Copy).then_inc(s_zhi, 1)
            split_w(S_GC // 2, 0)

            def merge_step(s0, dt, nk, last=False):
                sh = s0 // 2 + dt
                split_w(sh, 1, nk)
                evac(s0 + 2 * dt, 0, ACT.Tanh, 0.5)
                if not last:
                    split_w(sh, 2)

            with act.Fori(0, DT) as dt:
                merge_step(S_GC, dt, CT)
            with act.Fori(0, DT) as dt:
                merge_step(S_GM, dt, MP)
            for ct in range(CT):
                act.wait_ge(s_lnc, ct + 1)
                nc.scalar.activation(z_raw[:, ct, :], glu[:, ct, PAD_A:WA], ACT.Square).then_inc(s_sq, 1)
            with act.Fori(0, CT) as ct:
                s = S_B + 4 * ct
                sh = S_B // 2 + 2 * ct
                split_w(sh, 1)
                evac(s, 0, ACT.Copy, 1.0)
                split_w(sh, 2)
                split_w(sh, 3)
                evac(s + 2, 2, ACT.Tanh, 0.5)
                split_w(sh, 4)
                act.wait_ge(s_zpre, CT + MP + ct + 1)
                nc.scalar.activation(z_hi[:, bass.ds(ct, 1), :].rearrange("p o t -> p (o t)"), bz[:, :],
                                     ACT.Copy).then_inc(s_zhi, 1)
            act.wait_ge(s_lnv, 2)
            act.wait_ge(s_pjfree, 2 * S_GB)
            for h in range(2):
                op = nc.scalar.activation(xt[:, h * HALF:(h + 1) * HALF], po[:, h, :], ACT.Sqrt, bias=eps[:, 0:1])
            op.then_inc(s_sd, 1)
            act.wait_ge(s_rs, 1)
            for dt in range(2):
                merge_step(S_GB, dt, CT)
            for ct in range(CT):
                act.wait_ge(s_an, ct + 1)
                nc.scalar.activation(glu[:, ct, PAD_A:WA], glu[:, ct, PAD_A:WA], ACT.Identity,
                                     scale=lag[:, ct:ct + 1], bias=lab[:, ct:ct + 1]).then_inc(s_ag, 1)
            for ct in range(CT):
                act.wait_ge(s_ag, ct + 1)
                if ct >= 1:
                    act.wait_ge(s_as, ct)
                nc.scalar.activation(an_rstd[:, :], glu[:, ct, PAD_A:WA], ACT.Tanh, scale=0.5).then_inc(s_at, 1)
            with act.Fori(2, DT) as dt:
                merge_step(S_GB, dt, CT)
            act.wait_ge(s_as, CT)
            with act.Fori(0, CT // 2) as i:
                sh = S_AG // 2 + i
                for j in range(2):
                    split_w(sh, j + 1)
                    evac(S_AG + 2 * i + j, j, ACT.Tanh, 0.5)
                    act.wait_ge(s_zpre, 2 * CT + MP + 2 * i + j + 1)
                    nc.scalar.activation(z_hi[:, bass.ds(2 * i + j, 1), :].rearrange("p o t -> p (o t)"), sg[:, :],
                                         ACT.Copy).then_inc(s_zhi, 1)
            with act.Fori(0, DT - 1) as dt:
                merge_step(S_GA, dt, CT)
            merge_step(S_GA, DT - 1, CT, last=True)
            for k in range(KT):
                act.wait_ge(s_wld[k % 2], raw_count(S_END // 2, k))
                if k == 0:
                    act.wait_ge(s_pj, 2 * S_END)
                nc.scalar.activation(wout_hi[:, k, :], w_raw[:, k % 2, :, :].rearrange("p a b -> p (a b)"),
                                     ACT.Copy).then_inc(s_woh, 1)
                act.wait_ge(s_add, 3 * DT if k == KT - 1 else 2 * DT + k + 1)
                nc.scalar.activation(xT_hi[:, k, :], merged[:, k, :], ACT.Copy, scale=0.5).then_inc(s_gh, 1)
            for t in range(NT):
                act.wait_ge(s_mvr, t + 1)
                nc.scalar.activation(rstd[:, t % 2:t % 2 + 1], mv[:, t % 2, 1:2], ACT.Sqrt,
                                     bias=eps[:, 0:1]).then_inc(s_osd, 1)

        @block.gpsimd
        def _(pool):
            def split_w(s, j, nk=KT):
                for e in range(2):
                    k = slice(e * nk // 2, (e + 1) * nk // 2)
                    pool.wait_ge(s_whi, 2 * s + e + 1)
                    nc.gpsimd.tensor_tensor(w_lo[:, j % 2, k, :], w_raw[:, j % 2, k, :], w_hi[:, j % 2, k, :],
                                            ALU.subtract).then_inc(s_wlo, 1)

            nc.gpsimd.memset(ident[:, :], 0.0).then_inc(s_cst, 1)
            pool.wait_ge(s_cst, 1)
            nc.gpsimd.affine_select(out=ident[:, :], in_=ident[:, :], compare_op=ALU.not_equal, fill=1.0, base=0,
                                    pattern=[[-1, P]], channel_multiplier=1).then_inc(s_cst, 1)
            nc.gpsimd.memset(maskc[:, :], 0.0).then_inc(s_bd, 1)
            pool.wait_ge(s_bd, 1)
            nc.gpsimd.affine_select(out=maskc[:, :], in_=maskc[:, :], compare_op=ALU.is_ge, fill=-BIG, base=0,
                                    pattern=[[-1, P]], channel_multiplier=1).then_inc(s_bd, 1)
            split_w(0, 0)
            split_w(1, 1)
            pool.wait_ge(s_bd, 2)

            def diag_bias(c, u):
                a, i = u // NT % 2, u % NT
                if i == 0:
                    pool.wait_ge(s_bias[a], 16 * (c + 1 + u // UNITS))
                pool.wait_ge(s_dm, UNITS * c + u)
                nc.gpsimd.tensor_tensor(bdiag[:, u % 2, :], bias[:, a, i * P:(i + 1) * P], maskc[:, :],
                                        ALU.add).then_inc(s_bd, 1)

            pool.wait_ge(s_bias[0], 16)
            nc.gpsimd.tensor_tensor(bdiag[:, 0, :], bias[:, 0, 0:P], maskc[:, :], ALU.add).then_inc(s_bd, 1)
            split_w(2, 2)
            split_w(3, 3)

            def pair(c, last):
                for k in range(UNITS):
                    if k + 1 < UNITS or not last:
                        diag_bias(c, k + 1)
                    if k % 4 == 0:
                        split_w(4 * c + 4 + k // 4, 4 + k // 4)

            with pool.Fori(0, CT - 1) as c:
                pair(c, False)
            pair(CT - 1, True)
            for s in range(S_M + 1, S_GC + 1):
                split_w(s, s)
            with pool.Fori(0, DT) as dt:
                split_w(S_GC + 2 * dt + 1, 1, CT)
                split_w(S_GC + 2 * dt + 2, 2)

            def merge_step(s0, nk, d2, last=False):
                for e in range(2):
                    dt = 2 * d2 + e
                    split_w(s0 + 2 * dt + 1, 1, nk)
                    if not (last and e == 1):
                        split_w(s0 + 2 * dt + 2, 2)
                    pool.wait_ge(s_pjfree, 2 * (s0 + 2 * dt + 2))
                    md = merged[:, bass.ds(dt, 1), :].rearrange("p o t -> p (o t)")
                    nc.gpsimd.tensor_tensor(md, md, ytmp[:, e, :], ALU.add).then_inc(s_add, 1)

            with pool.Fori(0, DT // 2) as d2:
                merge_step(S_GM, MP, d2)
            nc.gpsimd.memset(ones_ln[:, :], 1.0 / A_W).then_inc(s_cst, 1)
            with pool.Fori(0, CT) as ct:
                for j in range(1, 5):
                    split_w(S_B + 4 * ct + j, j)
            with pool.Fori(0, DT // 2) as d2:
                merge_step(S_GB, CT, d2)
            with pool.Fori(0, CT // 2) as i:
                for j in range(1, 3):
                    split_w(S_AG + 2 * i + j, j)
            with pool.Fori(0, DT // 2 - 1) as d2:
                merge_step(S_GA, CT, d2)
            merge_step(S_GA, CT, DT // 2 - 1, last=True)

        @block.vector
        def _(dve):
            def hs(h):
                return slice(h * HALF, (h + 1) * HALF)

            def raw_evac(s, j, dst, scale=None):
                for h in range(2):
                    dve.wait_ge(s_pj, 2 * s + h + 1)
                    if scale is None:
                        nc.vector.tensor_copy(dst[:, hs(h)], pj[:, 2 * (j % 2) + h, :]).then_inc(s_pjfree, 1)
                    else:
                        nc.vector.tensor_scalar(dst[:, hs(h)], pj[:, 2 * (j % 2) + h, :], scale, None,
                                                ALU.mult).then_inc(s_pjfree, 1)

            def gate_evac(s, j, xt_count):
                for h in range(2):
                    dve.wait_ge(s_xt, xt_count + h + 1)
                    nc.vector.scalar_tensor_tensor(out=sg[:, hs(h)], in0=xt[:, hs(h)], scalar=1.0,
                                                   in1=pj[:, 2 * (j % 2) + h, :], op0=ALU.add,
                                                   op1=ALU.mult).then_inc(s_pjfree, 1)

            nc.vector.memset(wf_stack[:, :, :].bitcast(mybir.dt.uint32), 0).then_inc(s_wfs, 1)
            nc.vector.memset(eps[:, :], EPS).then_inc(s_fix, 1)
            dve.wait_ge(s_fa, 1)
            nc.vector.tensor_tensor(wf_stack[:, :, 32:32 + HEADS], wf_raw[:, :, :], wf_stack[:, :, 0:HEADS],
                                    ALU.subtract).then_inc(s_wfs, 1)
            for k in range(KT):
                dve.wait_ge(s_xhi, k + 1)
                nc.vector.tensor_tensor(xT_lo[:, k, :], x_raw[:, k, :], xT_hi[:, k, :], ALU.subtract).then_inc(s_xlo, 1)
            dve.wait_ge(s_mem, 16)
            for m in range(MT):
                for h in range(2):
                    op = nc.vector.bn_stats(stats[:, m, h, :], mem_sb[:, m, hs(h)])
            op.then_inc(s_st, 1)
            dve.wait_ge(s_st, 1)
            for m in range(MT):
                nc.vector.bn_aggr(mv[:, m, :], stats[:, m, :, :]).then_inc(s_ms, 1)
            dve.wait_ge(s_mr, 1)
            nc.vector.reciprocal(rinv[:, 0, :], rstd[:, 0:MT]).then_inc(s_mr, 1)
            dve.wait_ge(s_mr, 2)
            for m in range(MT):
                nc.vector.tensor_scalar(mem_sb[:, m, :], mem_sb[:, m, :], mv[:, m, 0:1], rinv[:, 0, m:m + 1],
                                        ALU.subtract, ALU.mult).then_inc(s_mn, 1)
            dve.wait_ge(s_par, 16 * 8)
            dve.wait_ge(s_fa, 3)
            for h in range(2):
                op = nc.vector.scalar_tensor_tensor(out=f_z[:, hs(h)], in0=po[0:HEADS, h, :], scalar=bf[:, 0:1],
                                                    in1=f_l[:, hs(h)], op0=ALU.add, op1=ALU.add)
            op.then_inc(s_fv, 1)
            n = 0
            for m in range(MT):
                for kb in range(KT // 4):
                    dve.wait_ge(s_mt, n + 1)
                    for k in range(4):
                        kk = 4 * kb + k
                        op = nc.vector.tensor_scalar(memT[:, kk, m * P:(m + 1) * P], pt[:, n % 2, k * P:(k + 1) * P],
                                                     memg[:, kk:kk + 1], memb[:, kk:kk + 1], ALU.mult, ALU.add)
                    op.then_inc(s_mte, 1)
                    n += 1
            dve.wait_ge(s_fa, 5)
            nc.vector.tensor_scalar(f_u[:, :], f_e[:, :], 1.0, None, ALU.add).then_inc(s_fv, 1)
            dve.wait_ge(s_fv, 2)
            nc.vector.scalar_tensor_tensor(out=f_e[:, :], in0=f_u[:, :], scalar=1.0, in1=f_e[:, :],
                                           op0=ALU.subtract, op1=ALU.subtract).then_inc(s_fv, 1)
            nc.vector.reciprocal(f_r[:, :], f_u[:, :]).then_inc(s_fv, 1)
            dve.wait_ge(s_fv, 4)
            nc.vector.scalar_tensor_tensor(out=f_e[:, :], in0=f_e[:, :], scalar=-1.0, in1=f_r[:, :],
                                           op0=ALU.mult, op1=ALU.mult).then_inc(s_fv, 1)
            dve.wait_ge(s_fa, 6)
            dve.wait_ge(s_fv, 5)
            nc.vector.tensor_tensor(f_l[:, :], f_l[:, :], f_e[:, :], ALU.add).then_inc(s_fv, 1)
            nc.vector.tensor_scalar(f_z[:, :], f_z[:, :], -1.0, 0.0, ALU.mult, ALU.max).then_inc(s_fv, 1)
            dve.wait_ge(s_fv, 7)
            nc.vector.tensor_tensor(f_l[:, :], f_l[:, :], f_z[:, :], ALU.add).then_inc(s_fv, 1)
            nc.vector.memset(f_abs[:, :], 1.0).then_inc(s_fv, 1)
            dve.wait_ge(s_fv, 9)
            nc.vector.tensor_tensor_scan(negcum[:, :], f_abs[:, :], f_l[:, :], 0.0, ALU.mult,
                                         ALU.add).then_inc(s_fv, 1)
            for c in range(MP):
                for a in range(2):
                    b, o = DH * a, DH * (1 - a)
                    dve.wait_ge(s_kvh, 2 * c + a + 1)
                    for r in (b, o):
                        op = nc.vector.tensor_tensor(km_lo[r:r + DH, 2 * c + a, :], po[b:b + DH, c, 0:MEM],
                                                     km_hi[b:b + DH, 2 * c + a, :], ALU.subtract)
                    op.then_inc(s_kvl, 1)
            for m in range(MT):
                dve.wait_ge(s_kvh, 2 * MP + m + 1)
                nc.vector.tensor_tensor(vm_stack[:, m, :, 1, :], pt[:, m, 0:M_W].rearrange("p (h d) -> p h d", d=DH),
                                        vm_stack[:, m, :, 0, :], ALU.subtract).then_inc(s_kvl, 1)
            dve.wait_ge(s_fv, F_STEPS)
            for t in (pT_hi, pT_lo):
                op = nc.vector.memset(t[:, 0, 0:P].bitcast(mybir.dt.uint32), 0)
            op.then_inc(s_dm, 1)

            def out_add(a, n, dst, count):
                b = DH * a
                dve.wait_ge(s_osh, count + 1)
                nc.vector.tensor_tensor(dst[b:b + DH], po[b:b + DH, n % 2, 0:2 * P], otmp[b:b + DH, :],
                                        ALU.add).then_inc(s_oadd, 1)

            def raw_half(s, h, dst, scale=None):
                dve.wait_ge(s_pj, 2 * s + h + 1)
                if scale is None:
                    nc.vector.tensor_copy(dst[:, hs(h)], pj[:, h, :]).then_inc(s_pjfree, 1)
                else:
                    nc.vector.tensor_scalar(dst[:, hs(h)], pj[:, h, :], scale, None, ALU.mult).then_inc(s_pjfree, 1)

            def gate_half(h, dst, xt_count):
                dve.wait_ge(s_xt, xt_count + h + 1)
                nc.vector.scalar_tensor_tensor(out=dst[:, hs(h)], in0=xt[:, hs(h)], scalar=1.0, in1=pj[:, h, :],
                                               op0=ALU.add, op1=ALU.mult).then_inc(s_pjfree, 1)

            def q_lo(a, src, dst, count):
                b, o = DH * a, DH * (1 - a)
                dve.wait_ge(s_stkh, count)
                nc.vector.tensor_tensor(dst[o:o + DH, a, :], src[b:b + DH, :], dst[b:b + DH, a, :],
                                        ALU.subtract).then_inc(s_stkl, 1)

            def k_lo(a, count):
                b, o = DH * a, DH * (1 - a)
                dve.wait_ge(s_stkh, count)
                for r in (b, o):
                    nc.vector.tensor_tensor(k_stack_lo[r:r + DH, a, :], k_raw[b:b + DH, :],
                                            k_stack_hi[b:b + DH, a, :], ALU.subtract).then_inc(s_stkl, 1)

            def biased(c, u):
                a, i = u // NT % 2, u % NT
                un, tb = UNITS * c, TB_PAIR * c
                dve.wait_ge(s_s, un + u + 1)
                dve.wait_ge(s_bd, 2 + un + u + 1)
                if i == 0:
                    dve.wait_ge(s_bias[a], 16 * (c + 1 + u // UNITS))
                if u == 1:
                    dve.wait_ge(s_tb, tb + 2)
                elif u:
                    dve.wait_ge(s_tb, tb + tb_before(u - 1))
                sc = pj[:, 2:4, :].rearrange("p a b -> p (a b)")
                d = slice(i * P, (i + 1) * P)
                mn = rmin[:, u % 2, 0:1] if i else rmin[:, u % 2, 1:2]
                dve.sem_inc(s_passed[0], 1)
                nc.vector.tensor_tensor_reduce(probs[:, u % 2, d], sc[:, d], bdiag[:, u % 2, :], -1.0, BIG,
                                               ALU.add, ALU.min, mn).then_inc(s_dm, 1)
                dve.wait_ge(s_dm, 1 + un + u + 1)
                if i:
                    dve.sem_inc(s_passed[0], 1)
                    nc.vector.tensor_tensor_reduce(probs[:, u % 2, 0:i * P], sc[:, 0:i * P], bias[:, a, 0:i * P],
                                                   -1.0, rmin[:, u % 2, 0:1], ALU.add, ALU.min,
                                                   rmin[:, u % 2, 1:2]).then_inc(s_sp, 1)
                else:
                    nc.vector.tensor_copy(rmin[:, u % 2, 0:1], rmin[:, u % 2, 1:2]).then_inc(s_sp, 1)

            def normalise(c, u):
                un, i = UNITS * c, u % NT
                dve.wait_ge(s_e, un + u + 1)
                nc.vector.reciprocal(rinv[:, u % 2, 0:1], rsum[:, u % 2, 0:1]).then_inc(s_ri, 1)
                dve.wait_ge(s_ri, un + u + 1)
                nc.vector.tensor_scalar(probs[:, u % 2, 0:(i + 1) * P], probs[:, u % 2, 0:(i + 1) * P],
                                        rinv[:, u % 2, 0:1], None, ALU.mult).then_inc(s_pn, 1)

            def turned_lo(c, u):
                i = u % NT
                for n, slots in enumerate(batches(i)):
                    dve.wait_ge(s_thi, TB_PAIR * c + tb_before(u) + n + 1)
                    q = slice((i % 2) * P, (i % 2 + 1) * P)
                    nc.vector.tensor_tensor(
                        pT_lo[:, slots[0]:slots[-1] + 1, q],
                        pt[:, (tb_before(u) + n) % 2, 0:len(slots) * P].rearrange("p (k q) -> p k q", q=P),
                        pT_hi[:, slots[0]:slots[-1] + 1, q], ALU.subtract).then_inc(s_tlo, 1)

            def pair(c, last):
                s, stk = 4 * c, STK_PAIR * (c + 1)
                for b in range(2):
                    dve.wait_ge(s_thi, TB_PAIR * c + b + 1)
                    nc.vector.tensor_tensor(v_stack[:, :, 4 * b:4 * b + 4, 1, :].rearrange("p a k d -> p k a d"),
                                            pt[:, b, :].rearrange("p (k a d) -> p k a d", k=4, a=2),
                                            v_stack[:, :, 4 * b:4 * b + 4, 0, :].rearrange("p a k d -> p k a d"),
                                            ALU.subtract).then_inc(s_tlo, 1)

                def zc(n):
                    g = n % (NT // 2)
                    return z_raw[:, bass.ds(c, 1), g * 2 * P:(g + 1) * 2 * P].rearrange("p o t -> p (o t)")

                for k in range(UNITS):
                    if k + 1 < UNITS or not last:
                        biased(c, k + 1)
                    if k:
                        turned_lo(c, k - 1)
                    if k + 1 < UNITS or not last:
                        normalise(c, k + 1)
                    if k in (2, 4):
                        raw_half(s + 3, k // 2 - 1, q_raw, QSCALE)
                    if k in (6, 8):
                        raw_half(s + 4, k // 2 - 3, k_raw, QSCALE if last else None)
                    if k in (10, 12):
                        if last:
                            gate_half(k // 2 - 5, v_raw, 2 * c)
                        else:
                            raw_half(s + 5, k // 2 - 5, v_raw)
                    if k == 14:
                        gate_half(0, sg, 2 * c + 2 * last)
                    if k % 2 == 0 and k:
                        n = k // 2 - 1
                        out_add(n // (NT // 2), n, zc(n), PV_PAIR * c + n)
                    if k == 10:
                        q_lo(0, q_raw, q_stack, stk + 1)
                    if k == 11 and not last:
                        k_lo(0, stk + 3)
                    if k == 15:
                        q_lo(1, q_raw, q_stack, stk + (2 if last else 4))
                turned_lo(c, UNITS - 1)
                gate_half(1, sg, 2 * c + 2 * last)
                n = UNITS // 2 - 1
                out_add(1, n, zc(n), PV_PAIR * c + n)
                if not last:
                    k_lo(1, stk + 6)
                dve.wait_ge(s_oadd, PV_PAIR * (c + 1))
                dve.wait_ge(s_pjfree, 8 * c + 14)
                z = z_raw[:, bass.ds(c, 1), :].rearrange("p o t -> p (o t)")
                nc.vector.scalar_tensor_tensor(out=z, in0=z, scalar=0.5, in1=sg[:, :], op0=ALU.mult,
                                               op1=ALU.mult).then_inc(s_zpre, 1)

            raw_evac(0, 0, q_raw, QSCALE)
            raw_evac(1, 1, k_raw)
            q_lo(0, q_raw, q_stack, 1)
            k_lo(0, 3)
            q_lo(1, q_raw, q_stack, 4)
            k_lo(1, 6)
            raw_evac(2, 2, v_raw)
            biased(0, 0)
            normalise(0, 0)
            with dve.Fori(0, CT - 1) as c:
                pair(c, False)
            pair(CT - 1, True)

            TB, PV, UN = TB_PAIR * CT, PV_PAIR * CT, UNITS * CT

            def mmax(w):
                dve.wait_ge(s_s, UN + w + 1)
                nc.vector.tensor_reduce(rmin[:, w % 2, :], pj[:, 2 + w % 2, :].rearrange("p (a k) -> p a k", a=2),
                                        AX.X, ALU.max).then_inc(s_dm, 1)
                dve.wait_ge(s_dm, 1 + UN + w + 1)
                nc.vector.tensor_scalar(rmin[:, w % 2, :], rmin[:, w % 2, :], -1.0, None, ALU.mult).then_inc(s_sp, 1)

            def mnormalise(w):
                dve.wait_ge(s_e, UN + w + 1)
                nc.vector.reciprocal(rinv[:, w % 2, :], rsum[:, w % 2, :]).then_inc(s_ri, 1)
                dve.wait_ge(s_ri, UN + w + 1)
                for a in range(2):
                    op = nc.vector.tensor_scalar(probs[:, w % 2, a * MEM:(a + 1) * MEM],
                                                 probs[:, w % 2, a * MEM:(a + 1) * MEM],
                                                 rinv[:, w % 2, a:a + 1], None, ALU.mult)
                op.then_inc(s_pn, 1)

            def mturned_lo(w):
                dve.wait_ge(s_thi, TB + w + 1)
                q = slice((w % 2) * P, (w % 2 + 1) * P)
                nc.vector.tensor_tensor(pT_lo[:, 0:2 * MT, q], pt[:, w % 2, :].rearrange("p (k q) -> p k q", q=P),
                                        pT_hi[:, 0:2 * MT, q], ALU.subtract).then_inc(s_tlo, 1)

            def mout(g):
                m, g2 = g // (NT // 2), g % (NT // 2)
                for a in range(2):
                    out_add(a, a, zm_raw[:, m, g2 * 2 * P:(g2 + 1) * 2 * P], PV + 2 * g + a)

            def mgate(m, gate):
                dve.wait_ge(s_oadd, PV + NT * (m + 1))
                nc.vector.scalar_tensor_tensor(out=zm_raw[:, m, :], in0=zm_raw[:, m, :], scalar=0.5, in1=gate[:, :],
                                               op0=ALU.mult, op1=ALU.mult).then_inc(s_zpre, 1)

            def a_half(ct, h, bank):
                s = S_A + 2 * ct
                dve.wait_ge(s_pj, 2 * s + 2 + h + 1)
                dve.wait_ge(s_xt, X_A + 2 * ct + h + 1)
                nc.vector.scalar_tensor_tensor(out=glu[:, ct, PAD_A + h * HALF:PAD_A + (h + 1) * HALF],
                                               in0=xt[:, hs(h)], scalar=1.0, in1=pj[:, bank, :],
                                               op0=ALU.add, op1=ALU.mult).then_inc(s_pjfree, 1)

            for ct in range(CT):
                op = nc.vector.memset(glu[:, ct, 0:PAD_A], 0.0)
            op.then_inc(s_ca, 1)
            nc.vector.tensor_scalar(cwa[:, :, :], cwa[:, :, :], 0.5, None, ALU.mult).then_inc(s_cw, 1)
            mmax(0)
            mnormalise(0)
            for w in range(2 * NT + 1):
                if w + 1 < 2 * NT:
                    mmax(w + 1)
                if w:
                    mturned_lo(w - 1)
                if w + 1 < 2 * NT:
                    mnormalise(w + 1)
                if w in (4, 5):
                    q_lo(w - 4, k_raw, q_stack1, STK_PAIR * CT + 2 + w - 4 + 1)
                for s, h in M_ENDS.get(w, ()):
                    if s == S_M:
                        gate_half(h, g_raw, X_M)
                    elif (s - S_A) % 2 == 0:
                        dve.wait_ge(s_xt, X_A + (s - S_A) + h + 1)
                        dve.sem_inc(s_pjfree, 1)
                    else:
                        a_half((s - S_A) // 2, h, h)
                if w % 2 == 0 and w:
                    mout(w // 2 - 1)
                if w == NT + 1:
                    mgate(0, v_raw)
            mgate(1, g_raw)
            for ct in range(CT):
                dve.wait_ge(s_zhi, ct + 1)
                nc.vector.tensor_tensor(z_lo[:, ct, :], z_raw[:, ct, :], z_hi[:, ct, :], ALU.subtract).then_inc(s_zlo, 1)
            for h in range(2):
                dve.wait_ge(s_xt, X_A + 2 * (CT - 1) + h + 1)
                dve.sem_inc(s_pjfree, 1)
            for m in range(MP):
                dve.wait_ge(s_zhi, CT + m + 1)
                nc.vector.tensor_tensor(zm_lo[:, m, :], zm_raw[:, m, :], zm_hi[:, m, :], ALU.subtract).then_inc(s_zlo, 1)
            for h in range(2):
                a_half(CT - 1, h, 2 + h)

            def conv_taps(ct, h, taps, unit):
                for n in taps:
                    src = glu[:, bass.ds(ct, 1), h * HALF + n:(h + 1) * HALF + n].rearrange("p o t -> p (o t)")
                    dve.wait_ge(s_ca, 1 + CONV_A * unit + n)
                    if n == 0:
                        dve.wait_ge(s_cw, 1 + 2 * unit)
                        nc.vector.tensor_copy(cwk[:, 0:CONV_A], cwa[:, bass.ds(ct, 1), :].rearrange("p o t -> p (o t)")
                                              ).then_inc(s_cw, 1)
                        nc.vector.tensor_copy(cwk[:, CONV_A:CONV_A + 1], cab[:, bass.ds(ct, 1)]).then_inc(s_cw, 1)
                        dve.wait_ge(s_cw, 1 + 2 * unit + 2)
                        op = nc.vector.tensor_scalar(sg[:, 0:HALF], src, cwk[:, 0:1], cwk[:, CONV_A:CONV_A + 1],
                                                     ALU.mult, ALU.add)
                    else:
                        op = nc.vector.scalar_tensor_tensor(out=src if n == CONV_A - 1 else sg[:, 0:HALF], in0=src,
                                                            scalar=cwk[:, n:n + 1], in1=sg[:, 0:HALF],
                                                            op0=ALU.mult, op1=ALU.add)
                    op.then_inc(s_ca, 1)

            def merge_step(s0, x0, d2, first=False, fresh=False, adds=0, conv=None):
                cuts = [range(0, 8), range(8, 16), range(16, 24), range(24, CONV_A)]
                for e in range(2):
                    dt = 2 * d2 + e
                    for h in range(2):
                        if conv is not None:
                            conv_taps(d2, conv[0], cuts[2 * e + h], conv[1] + d2)
                        if h == 0:
                            dve.wait_ge(s_xt, x0 + 2 * dt + 2)
                            if not first and not fresh:
                                dve.wait_ge(s_add, adds + dt - 1)
                        dve.wait_ge(s_pj, 2 * (s0 + 2 * dt + 1) + h + 1)
                        dst = merged[:, bass.ds(dt, 1), hs(h)].rearrange("p o t -> p (o t)") if first else ytmp[:, e, hs(h)]
                        nc.vector.scalar_tensor_tensor(out=dst, in0=xt[:, hs(h)], scalar=1.0, in1=pj[:, 2 + h, :],
                                                       op0=ALU.add, op1=ALU.mult).then_inc(s_pjfree, 2)

            dve.wait_ge(s_pjfree, 2 * S_GC)
            with dve.Fori(0, DT // 2) as d2:
                merge_step(S_GC, X_GC, d2, first=True, conv=(1, 0))
            merge_step(S_GM, X_GM, 0, fresh=True, conv=(0, CT))
            with dve.Fori(1, DT // 2) as d2:
                merge_step(S_GM, X_GM, d2, conv=(0, CT))

            dve.wait_ge(s_lnm, 2)
            for ct in range(CT):
                for h in range(2):
                    v = glu[:, ct, PAD_A + h * HALF:PAD_A + (h + 1) * HALF]
                    op = nc.vector.tensor_tensor(v, v, pt[:, h, :], ALU.subtract)
                op.then_inc(s_lnc, 1)

            nc.vector.memset(prod[:, 0:PAD_B], 0.0).then_inc(s_cb, 1)
            with dve.Fori(0, CT) as ct:
                s = S_B + 4 * ct
                x0 = X_B + 4 * ct
                dve.wait_ge(s_xt, x0 + 2)
                for h in range(2):
                    dve.wait_ge(s_pj, 2 * (s + 1) + h + 1)
                    nc.vector.tensor_tensor(prod[:, PAD_B + h * HALF:PAD_B + (h + 1) * HALF], pj[:, 2 + h, :],
                                            xt[:, hs(h)], ALU.mult).then_inc(s_pjfree, 2)
                nc.vector.tensor_copy(cwk[:, 0:CONV_B], cwb[:, bass.ds(ct, 1), :].rearrange("p o t -> p (o t)")
                                      ).then_inc(s_cb, 1)
                dve.wait_ge(s_pjfree, 2 * s + 4)
                for n in range(CONV_B):
                    dve.wait_ge(s_cb, 1 + (CONV_B + 1) * ct + 1 + n)
                    if n == 0:
                        op = nc.vector.tensor_scalar(cv[:, :], prod[:, 0:T], cwk[:, 0:1], None, ALU.mult)
                    else:
                        op = nc.vector.scalar_tensor_tensor(out=cv[:, :], in0=prod[:, n:n + T], scalar=cwk[:, n:n + 1],
                                                            in1=cv[:, :], op0=ALU.mult, op1=ALU.add)
                    op.then_inc(s_cb, 1)
                gate_evac(s + 2, 2, x0 + 2)
                dve.wait_ge(s_cb, 1 + (CONV_B + 1) * (ct + 1))
                for h in range(2):
                    dve.wait_ge(s_pj, 2 * (s + 3) + h + 1)
                    nc.vector.tensor_tensor(bz[:, hs(h)], pj[:, 2 + h, :], cv[:, hs(h)], ALU.mult).then_inc(s_pjfree, 1)
                dve.wait_ge(s_pjfree, 2 * s + 8)
                nc.vector.scalar_tensor_tensor(out=bz[:, :], in0=bz[:, :], scalar=0.5, in1=sg[:, :],
                                               op0=ALU.mult, op1=ALU.mult).then_inc(s_zpre, 1)
                dve.wait_ge(s_zhi, CT + MP + ct + 1)
                nc.vector.tensor_tensor(z_lo[:, bass.ds(ct, 1), :].rearrange("p o t -> p (o t)"), bz[:, :],
                                        z_hi[:, bass.ds(ct, 1), :].rearrange("p o t -> p (o t)"),
                                        ALU.subtract).then_inc(s_zlo, 1)
            dve.wait_ge(s_sd, 1)
            nc.vector.reciprocal(an_rstd[:, :], xt[:, :]).then_inc(s_rs, 1)
            dve.wait_ge(s_rs, 1)
            dve.wait_ge(s_lnc, CT)
            for ct in range(CT):
                v = glu[:, ct, PAD_A:WA]
                nc.vector.tensor_tensor(v, v, an_rstd[:, :], ALU.mult).then_inc(s_an, 1)
            merge_step(S_GB, X_GB, 0, adds=DT)
            for ct in range(CT):
                v = glu[:, ct, PAD_A:WA]
                dve.wait_ge(s_at, ct + 1)
                nc.vector.scalar_tensor_tensor(out=v, in0=an_rstd[:, :], scalar=1.0, in1=v, op0=ALU.add,
                                               op1=ALU.mult).then_inc(s_as, 1)
            with dve.Fori(1, DT // 2) as d2:
                merge_step(S_GB, X_GB, d2, adds=DT)

            dve.wait_ge(s_as, CT)
            with dve.Fori(0, CT // 2) as i:
                for j in range(2):
                    ct = 2 * i + j
                    dve.wait_ge(s_zlo, 2 * CT + MP + ct)
                    gate_evac(S_AG + ct, j, X_AG + 2 * ct)
                    dve.wait_ge(s_pjfree, 2 * (S_AG + ct + 1))
                    v = glu[:, bass.ds(ct, 1), PAD_A:WA].rearrange("p o t -> p (o t)")
                    nc.vector.scalar_tensor_tensor(out=sg[:, :], in0=sg[:, :], scalar=0.25, in1=v,
                                                   op0=ALU.mult, op1=ALU.mult).then_inc(s_zpre, 1)
                    dve.wait_ge(s_zhi, 2 * CT + MP + ct + 1)
                    nc.vector.tensor_tensor(z_lo[:, bass.ds(ct, 1), :].rearrange("p o t -> p (o t)"), sg[:, :],
                                            z_hi[:, bass.ds(ct, 1), :].rearrange("p o t -> p (o t)"),
                                            ALU.subtract).then_inc(s_zlo, 1)
            with dve.Fori(0, DT // 2) as d2:
                merge_step(S_GA, X_GA, d2, adds=2 * DT)

            for k in range(KT):
                dve.wait_ge(s_woh, k + 1)
                nc.vector.tensor_tensor(wout_lo[:, k, :], w_raw[:, k % 2, :, :].rearrange("p a b -> p (a b)"),
                                        wout_hi[:, k, :], ALU.subtract).then_inc(s_wol, 1)
                dve.wait_ge(s_gh, k + 1)
                nc.vector.scalar_tensor_tensor(out=xT_lo[:, k, :], in0=merged[:, k, :], scalar=0.5, in1=xT_hi[:, k, :],
                                               op0=ALU.mult, op1=ALU.subtract).then_inc(s_gl, 1)
            dve.wait_ge(s_lnp, 32)
            for t in range(NT):
                q = t % 2
                if t >= 2:
                    dve.wait_ge(s_store[q], 16 * (t // 2))
                dve.wait_ge(s_xtk[q], 16 * (t // 2 + 1))
                for h in range(2):
                    dve.wait_ge(s_out_pj, 2 * t + h + 1)
                    nc.vector.scalar_tensor_tensor(out=y_tok[:, q, hs(h)], in0=x_tok[:, q, hs(h)], scalar=ALPHA,
                                                   in1=pj[:, (2 * t + h) % 4, :], op0=ALU.mult,
                                                   op1=ALU.add).then_inc(s_yk, 1)
                dve.wait_ge(s_yk, 2 * t + 2)
                for h in range(2):
                    op = nc.vector.bn_stats(stats[:, q, h, :], y_tok[:, q, hs(h)])
                op.then_inc(s_st, 1)
                dve.wait_ge(s_st, 1 + t + 1)
                nc.vector.bn_aggr(mv[:, q, :], stats[:, q, :, :]).then_inc(s_mvr, 1)
                dve.wait_ge(s_osd, t + 1)
                nc.vector.reciprocal(rinv[:, q, 0:1], rstd[:, q:q + 1]).then_inc(s_ors, 1)
                nc.vector.scalar_tensor_tensor(out=y_tok[:, q, :], in0=y_tok[:, q, :], scalar=mv[:, q, 0:1],
                                               in1=lng_b[:, :], op0=ALU.subtract, op1=ALU.mult).then_inc(s_t1, 1)
                dve.wait_ge(s_ors, t + 1)
                dve.wait_ge(s_t1, t + 1)
                nc.vector.scalar_tensor_tensor(out=y_tok[:, q, :], in0=y_tok[:, q, :], scalar=rinv[:, q, 0:1],
                                               in1=lnb_b[:, :], op0=ALU.mult, op1=ALU.add).then_inc(s_yo, 1)


def kernel(**inputs):
    import numpy as np
    import concourse.bacc as bacc
    from concourse.bass_utils import run_bass_kernel_spmd

    def one(name):
        return np.ascontiguousarray(np.asarray(inputs[name])[0])

    def columns(v):
        return np.ascontiguousarray(v.reshape(-1, P).T)

    x = one("x")
    arrays = {
        "xT": np.ascontiguousarray(x.T), "x": x, "mem": one("mem"), "w_in": one("w_in"),
        "b_forget": one("b_forget"), "conv_a_wT": np.ascontiguousarray(one("conv_a_w").T),
        "conv_a_b": columns(one("conv_a_b")), "ln_a_g": columns(one("ln_a_g")), "ln_a_b": columns(one("ln_a_b")),
        "conv_b_wT": np.ascontiguousarray(one("conv_b_w").T), "w_kv_mem": one("w_kv_mem"),
        "mem_ln_g": columns(np.asarray(inputs["mem_ln_g"])), "mem_ln_b": columns(np.asarray(inputs["mem_ln_b"])),
        "p_a": one("p_a"), "p_b": one("p_b"), "p_c": one("p_c"), "p_m": one("p_m"), "w_out": one("w_out"),
        "ln_g": one("ln_g"), "ln_b": one("ln_b"),
    }
    nc = bacc.Bacc("TRN2", target_bir_lowering=False, num_devices=1)
    args = {name: nc.dram_tensor(f"in_{name}", a.shape, F32, kind="ExternalInput").ap() for name, a in arrays.items()}
    out = nc.dram_tensor("out_y", x.shape, F32, kind="ExternalOutput").ap()
    hybrid_mixer(nc, out=out, **args)
    r = run_bass_kernel_spmd(nc, [{f"in_{name}": a for name, a in arrays.items()}], core_ids=[0])
    return r.results[0]["out_y"].reshape(inputs["x"].shape)
```

```python
from contextlib import ExitStack

import concourse.bass as bass
from concourse import mybir

F32 = mybir.dt.float32
F32R = mybir.dt.float32r
ACT = mybir.ActivationFunctionType
ALU = mybir.AluOpType
AX = mybir.AxisListType

P = 128
BIG = 1.0e30


def hybrid_mixer(nc, xT, x, mem, w_in, b_forget, conv_a_wT, conv_a_b, ln_a_g, ln_a_b, conv_b_wT,
                 w_kv_mem, mem_ln_g, mem_ln_b, p_a, p_b, p_c, p_m, w_out, ln_g, ln_b, out):
    D, T = xT.shape
    KT = D // P
    HALF = T // 2
    NT = T // P
    DT = D // P
    CONV_A, A_W = conv_a_wT.shape[1], conv_a_wT.shape[0]
    CONV_B, B_W = conv_b_wT.shape[1], conv_b_wT.shape[0]
    PAD_A, PAD_B = CONV_A - 1, CONV_B - 1
    HEADS = b_forget.shape[0]
    DH = 64
    C_W = HEADS * DH
    MEM = mem.shape[0]
    MT = MEM // P
    M_W = w_kv_mem.shape[1] // 2
    M_HEADS = M_W // DH
    CT = A_W // P
    MP = M_W // P
    QSCALE = DH ** -0.5
    ALPHA = 2.0 ** 0.25
    EPS = 1e-5
    assert A_W == B_W == C_W == CT * P and A_W & (A_W - 1) == 0 and CT == 4 and NT == 8 and MT == 2 and MP == 2

    col, at = {}, 0
    for name, width in (("a_u", A_W), ("a_v", A_W), ("a_gate", A_W), ("b_h", B_W), ("b_b", B_W), ("b_c", B_W),
                        ("b_gate", B_W), ("q", C_W), ("k", C_W), ("v", C_W), ("f", HEADS), ("c_gate", C_W),
                        ("m_q", M_W), ("m_gate", M_W), ("g", 4 * D)):
        col[name] = at
        at += width
    assert at == w_in.shape[1]

    S_C = 3
    S_M = S_C + 4 * CT
    S_A = S_M + 1
    S_GC = S_A + 2 * CT
    S_GM = S_GC + 2 * DT
    S_B = S_GM + 2 * DT
    S_GB = S_B + 4 * CT
    S_AG = S_GB + 2 * DT
    S_GA = S_AG + CT
    S_END = S_GA + 2 * DT

    BASE = (nc.sbuf_base + 63) // 64 * 64
    KB = 1024

    def at_(name, shape, dt, off):
        return nc.alloc_sbuf_tensor_at(name, shape, dt, offset=BASE + off)

    xT_hi = at_("xT_hi", [P, KT, T], F32R, 0)
    xT_lo = at_("xT_lo", [P, KT, T], F32R, 32 * KB)
    w_raw = at_("w_raw", [P, 2, KT, P], F32, 64 * KB)
    w_hi = at_("w_hi", [P, 2, KT, P], F32R, 72 * KB)
    w_lo = at_("w_lo", [P, 2, KT, P], F32R, 80 * KB)
    z_hi = at_("z_hi", [P, CT, T], F32R, 104 * KB)
    z_lo = at_("z_lo", [P, CT, T], F32R, 88 * KB)
    z_raw = at_("z_raw", [P, CT, T], F32, 88 * KB)
    x_raw = at_("x_raw", [P, KT, T], F32, 88 * KB)
    wkv = at_("wkv", [P, KT, 2 * M_W], F32, 120 * KB)
    memT = at_("memT", [P, KT, MEM], F32, 136 * KB)
    mem_sb = at_("mem_sb", [P, MT, D], F32, 144 * KB)
    wf_stack = at_("wf_stack", [P, KT, P], F32R, 152 * KB)
    negcum = at_("negcum", [HEADS, T], F32, 156 * KB)
    f_z = at_("f_z", [HEADS, T], F32, 160 * KB)
    f_abs = at_("f_abs", [HEADS, T], F32, 164 * KB)
    f_e = at_("f_e", [HEADS, T], F32, 168 * KB)
    f_u = at_("f_u", [HEADS, T], F32, 172 * KB)
    f_r = at_("f_r", [HEADS, T], F32, 176 * KB)
    f_l = at_("f_l", [HEADS, T], F32, 180 * KB)
    q_stack = at_("q_stack", [P, 2, T], F32R, 120 * KB)
    k_stack_hi = at_("k_stack_hi", [P, 2, T], F32R, 128 * KB)
    k_stack_lo = at_("k_stack_lo", [P, 2, T], F32R, 136 * KB)
    v_stack = at_("v_stack", [P, 2, NT, 2, DH], F32R, 144 * KB)
    bias = at_("bias", [P, 2, T], F32, 152 * KB)
    probs = at_("probs", [P, 2, T], F32, 160 * KB)
    v_raw = at_("v_raw", [P, T], F32, 112 * KB)
    k_raw = at_("k_raw", [P, T], F32, 108 * KB)
    g_raw = at_("g_raw", [P, T], F32, 116 * KB)
    pT_hi = at_("pT_hi", [P, NT, 2 * P], F32R, 168 * KB)
    pT_lo = at_("pT_lo", [P, NT, 2 * P], F32R, 176 * KB)
    q_raw = at_("q_raw", [P, T], F32, 104 * KB)
    km_hi = at_("km_hi", [P, M_HEADS, MEM], F32R, 184 * KB)
    km_lo = at_("km_lo", [P, M_HEADS, MEM], F32R, 188 * KB)
    vm_stack = at_("vm_stack", [P, MT, M_HEADS, 2, DH], F32R, 192 * KB)
    xt = at_("xt", [P, T], F32, 196 * KB)
    sg = at_("sg", [P, T], F32, 200 * KB)
    q_stack1 = at_("q_stack1", [P, 2, T], F32R, 152 * KB)
    WA = PAD_A + T
    glu = at_("glu", [P, CT, WA], F32, 128 * KB)
    zm_raw = at_("zm_raw", [P, MP, T], F32, 144 * KB + 512)
    zm_lo = at_("zm_lo", [P, MP, T], F32R, 144 * KB + 512)
    zm_hi = at_("zm_hi", [P, MP, T], F32R, 152 * KB + 512)
    merged = at_("merged", [P, DT, T], F32, 164 * KB)
    ytmp = at_("ytmp", [P, 2, T], F32, 120 * KB)
    prod = at_("prod", [P, PAD_B + T], F32, 144 * KB + 512)
    cv = at_("cv", [P, T], F32, 149 * KB)
    bz = at_("bz", [P, T], F32, 153 * KB)
    ones_ln = at_("ones_ln", [P, P], F32R, 157 * KB)
    an_rstd = at_("an_rstd", [P, T], F32, 149 * KB)
    wout_raw = at_("wout_raw", [P, KT, D], F32, 128 * KB)
    wout_lo = at_("wout_lo", [P, KT, D], F32R, 128 * KB)
    wout_hi = at_("wout_hi", [P, KT, D], F32R, 88 * KB)
    wout_hi0 = at_("wout_hi0", [P, D], F32R, 160 * KB)
    merged_hi0 = at_("merged_hi0", [P, T], F32R, 200 * KB)
    lng_b = at_("lng_b", [P, D], F32, 120 * KB)
    lnb_b = at_("lnb_b", [P, D], F32, 124 * KB)
    x_tok = at_("x_tok", [P, 2, D], F32, 164 * KB)
    y_tok = at_("y_tok", [P, 2, D], F32, 172 * KB)
    off = [204 * KB]

    def small(name, shape, dt=F32):
        n = 4
        for d in shape[1:]:
            n *= d
        t = nc.alloc_sbuf_tensor_at(name, shape, dt, offset=BASE + off[0], align_bytes=8)
        off[0] += (n + 7) // 8 * 8
        return t

    ident = small("ident", [P, P])
    otmp = small("otmp", [P, 2 * P])
    maskc = small("maskc", [P, P])
    bdiag = small("bdiag", [P, 2, P])
    cwk = small("cwk", [P, CONV_A + 1])
    cwa = small("cwa", [P, CT, CONV_A])
    cwb = small("cwb", [P, CT, CONV_B])
    cab = small("cab", [P, CT])
    lag = small("lag", [P, CT])
    lab = small("lab", [P, CT])
    eps = small("eps", [P, 1])
    rmin = small("rmin", [P, 2, 2])
    rsum = small("rsum", [P, 2, 2])
    rinv = small("rinv", [P, 2, 2])
    mv = small("mv", [P, 2, 2])
    rstd = small("rstd", [P, 2])
    wf_raw = at_("wf_raw", [P, KT, HEADS], F32, 184 * KB)
    memg = at_("memg", [P, KT], F32, 188 * KB)
    memb = at_("memb", [P, KT], F32, 188 * KB + 32)
    bf = at_("bf", [HEADS, 1], F32, 188 * KB + 64)
    stats = at_("stats", [P, 2, 2, 6], F32, 195 * KB)
    assert BASE + off[0] <= nc.sbuf_usable_end, (BASE + off[0], nc.sbuf_usable_end)

    cum_dram = nc.dram_tensor("cum_scratch", [HEADS, T], F32, kind="Internal").ap()

    ctx = ExitStack()
    with ctx:
        pj = ctx.enter_context(nc.psum_tensor("pj", [P, 4, HALF], F32))
        pt = ctx.enter_context(nc.psum_tensor("pt", [P, 2, HALF], F32))
        po = ctx.enter_context(nc.psum_tensor("po", [P, 2, HALF], F32))

        def sem(name):
            return ctx.enter_context(nc.semaphore(name))

        s_passed = [sem("vector_passed"), sem("sync_passed")]
        s_x = [sem(f"x_loaded{k}") for k in range(KT)]
        s_par = sem("params_loaded")
        s_wf = sem("wf_loaded")
        s_mem = sem("mem_loaded")
        s_wkv = sem("wkv_loaded")
        s_cst = sem("constants_made")
        s_fix = sem("small_setup_done")
        s_xhi = sem("x_hi_made")
        s_xlo = sem("x_lo_made")
        s_wld = [sem(f"w_raw_loaded{i}") for i in range(2)]
        s_whi = sem("w_hi_made")
        s_wlo = sem("w_lo_made")
        s_pj = sem("half_accumulated")
        s_pjfree = sem("half_evacuated")
        s_xt = sem("xt_written")
        s_wfs = sem("wf_stack_made")
        s_f = sem("f_accumulated")
        s_fa = sem("f_scalar_steps")
        s_fv = sem("f_vector_steps")
        s_cumst = sem("cum_stored")
        s_ms = sem("mem_stats")
        s_mr = sem("mem_std")
        s_mn = sem("mem_normalised")
        s_mt = sem("mem_transposed")
        s_mte = sem("memT_written")
        s_kv = sem("mem_kv_accumulated")
        s_kvh = sem("mem_kv_hi_made")
        s_kvl = sem("mem_kv_lo_made")
        s_bias = [sem(f"bias_loaded{a}") for a in range(2)]
        s_stkh = sem("stack_hi_made")
        s_stkl = sem("stack_lo_made")
        s_s = sem("scores_ready")
        s_bd = sem("diag_bias_made")
        s_dm = sem("diag_min")
        s_sp = sem("scores_biased")
        s_e = sem("probs_exp")
        s_ri = sem("row_sum_inverted")
        s_pn = sem("probs_normalised")
        s_tb = sem("transposed")
        s_thi = sem("pT_hi_made")
        s_tlo = sem("pT_lo_made")
        s_pv = sem("pv_accumulated")
        s_osh = sem("o_half_shifted")
        s_oadd = sem("o_halves_added")
        s_og = sem("o_gated")
        s_zpre = sem("z_product_made")
        s_zhi = sem("z_hi_made")
        s_zlo = sem("z_lo_made")
        s_cw = sem("conv_weights_ready")
        s_ca = sem("conv_steps")
        s_cb = sem("convb_steps")
        s_bt = sem("b_times_conv")
        s_yt = sem("gated_y_made")
        s_add = sem("branch_added")
        s_lnm = sem("ln_mean_accumulated")
        s_lnc = sem("ln_centred")
        s_sq = sem("ln_squared")
        s_ah = sem("ln_operand_hi_made")
        s_al = sem("ln_operand_lo_made")
        s_lnv = sem("ln_var_accumulated")
        s_sd = sem("ln_std")
        s_rs = sem("ln_rstd")
        s_an = sem("a_scaled")
        s_ag = sem("a_affine")
        s_at = sem("a_tanh")
        s_as = sem("a_silu_made")
        s_wo = [sem(f"wout_loaded{k}") for k in range(KT)]
        s_woh = sem("wout_hi_made")
        s_wol = sem("wout_lo_made")
        s_gh = sem("merged_hi_made")
        s_gl = sem("merged_lo_made")
        s_lnp = sem("ln_params_loaded")
        s_xtk = [sem(f"x_tok_loaded{i}") for i in range(2)]
        s_out_pj = sem("out_half_accumulated")
        s_yk = sem("residual_added")
        s_st = sem("out_stats")
        s_mvr = sem("out_mean_var")
        s_osd = sem("out_std")
        s_ors = sem("out_rstd")
        s_t1 = sem("out_centred")
        s_yo = sem("out_ready")
        s_store = [sem(f"out_stored{i}") for i in range(2)]

        block = ctx.enter_context(nc.Block())

        F_STEPS = 10
        STK_HEAD = 3
        STK_PAIR = 2 * STK_HEAD
        UNIT_STEPS = CONV_A + 1
        CONV_STEPS = 1 + 2 * CT * UNIT_STEPS
        X_M = 2 * CT + 2
        X_A = X_M + 2
        X_GC = X_A + 2 * CT
        X_GM = X_GC + 2 * DT
        X_B = X_GM + 2 * DT
        X_GB = X_B + 4 * CT
        X_AG = X_GB + 2 * DT
        X_GA = X_AG + 2 * CT
        UNITS = 2 * NT

        def batches(i):
            first, last = 1 - i % 2, 2 * (i // 2) + 1
            slots = list(range(first, last + 1))
            return [slots[n:n + 4] for n in range(0, len(slots), 4)]

        TB_HEAD = sum(len(batches(i)) for i in range(NT))
        TB_PAIR = 2 + 2 * TB_HEAD

        def tb_before(u):
            return 2 + (u // NT) * TB_HEAD + sum(len(batches(i)) for i in range(u % NT))

        PV_PAIR = 2 * (NT // 2)
        assert TB_PAIR % 2 == 0

        M_STARTS, M_ENDS = {}, {}
        for n, s in enumerate(range(S_M, S_GC - 2)):
            first, per, w0 = (2 * KT * n, 6, 0) if n < 3 else (2 * KT * (n - 3), 8, NT)
            M_STARTS.setdefault(w0 + first // per, []).append(s)
            for h in range(2):
                M_ENDS.setdefault(w0 + (first + KT * (h + 1) - 1) // per + 1, []).append((s, h))

        def pieces(nk):
            return slice(0, nk // 4 or 1), slice(nk // 4 or 1, nk)

        def raw_count(s_half, j):
            return 16 * (s_half + j // 2 + 1)

        @block.sync
        def _(sp):
            def load_w(s, j, src, nk):
                sp.wait_ge(s_wlo, 2 * (s - 1))
                sp.sem_inc(s_passed[1], 1)
                sp.dma_start(w_raw[:, j % 2, 0:nk, :], src).then_inc(s_wld[j % 2], 16)

            def wcols(c0):
                if not isinstance(c0, int):
                    c0 = sp.snap(c0)
                return w_in[:, bass.ds(c0, P)].rearrange("(k p) c -> p k c", p=P)

            def pcols(w, dt):
                return w[:, bass.ds(sp.snap(dt * P), P)].rearrange("(k p) c -> p k c", p=P)

            xv = xT.rearrange("(k p) t -> p k t", p=P)
            sp.dma_start(wf_raw[:, :, :], w_in[:, col["f"]:col["f"] + HEADS].rearrange("(k p) c -> p k c", p=P)
                         ).then_inc(s_wf, 16)
            for k in range(KT):
                sp.dma_start(x_raw[:, k, :], xv[:, k, :]).then_inc(s_x[k], 16)
                if k == 0:
                    sp.dma_start(w_raw[:, 0, :, :], wcols(col["q"])).then_inc(s_wld[0], 16)
            sp.dma_start(w_raw[:, 1, :, :], wcols(col["k"])).then_inc(s_wld[1], 16)
            sp.dma_start(mem_sb[:, :, :], mem.rearrange("(m p) d -> p m d", p=P)).then_inc(s_mem, 16)
            sp.dma_start(wkv[:, :, :], w_kv_mem.rearrange("(k p) c -> p k c", p=P)).then_inc(s_wkv, 16)
            for t, src in ((cwa[:, :, :], conv_a_wT.rearrange("(c p) k -> p c k", p=P)),
                           (cwb[:, :, :], conv_b_wT.rearrange("(c p) k -> p c k", p=P)),
                           (cab[:, :], conv_a_b),
                           (lag[:, :], ln_a_g),
                           (lab[:, :], ln_a_b),
                           (memg[:, :], mem_ln_g),
                           (memb[:, :], mem_ln_b),
                           (bf[:, :], b_forget.rearrange("(h o) -> h o", o=1))):
                sp.dma_start(t, src).then_inc(s_par, 16)
            load_w(2, 0, wcols(col["v"]), KT)
            load_w(3, 1, wcols(col["q"] + P), KT)
            sp.wait_ge(s_fv, F_STEPS)
            sp.dma_start(cum_dram[:, :], negcum[:, :]).then_inc(s_cumst, 16)
            sp.wait_ge(s_cumst, 16)
            for a in range(2):
                sp.dma_start(bias[:, a, :], cum_dram[a, :].partition_broadcast(P)).then_inc(s_bias[a], 16)
            load_w(4, 0, wcols(col["k"] + P), KT)
            load_w(5, 1, wcols(col["v"] + P), KT)

            def bias_row(c, a):
                sp.wait_ge(s_sp, UNITS * c + NT * (a + 1))
                sp.sem_inc(s_passed[1], 1)
                sp.dma_start(bias[:, a, :], cum_dram[2 * c + 2 + a, :].partition_broadcast(P)).then_inc(s_bias[a], 16)

            with sp.Fori(0, CT - 2) as c:
                load_w(4 * c + 6, 0, wcols(col["c_gate"] + c * P), KT)
                load_w(4 * c + 7, 1, wcols(col["q"] + (c + 2) * P), KT)
                bias_row(c, 0)
                load_w(4 * c + 8, 0, wcols(col["k"] + (c + 2) * P), KT)
                load_w(4 * c + 9, 1, wcols(col["v"] + (c + 2) * P), KT)
                bias_row(c, 1)
            c = CT - 2
            load_w(4 * c + 6, 0, wcols(col["c_gate"] + c * P), KT)
            load_w(4 * c + 7, 1, wcols(col["m_q"]), KT)
            bias_row(c, 0)
            load_w(4 * c + 8, 0, wcols(col["m_q"] + P), KT)
            load_w(4 * c + 9, 1, wcols(col["m_gate"]), KT)
            bias_row(c, 1)
            load_w(4 * c + 10, 0, wcols(col["c_gate"] + (CT - 1) * P), KT)
            load_w(S_M, 1, wcols(col["m_gate"] + P), KT)
            for ct in range(CT):
                load_w(S_A + 2 * ct, 0, wcols(col["a_v"] + ct * P), KT)
                load_w(S_A + 2 * ct + 1, 1, wcols(col["a_u"] + ct * P), KT)

            def merge_loads(s0, branch, w, nk):
                with sp.Fori(0, DT) as dt:
                    load_w(s0 + 2 * dt, 0, wcols(col["g"] + branch * D + dt * P), KT)
                    load_w(s0 + 2 * dt + 1, 1, pcols(w, dt), nk)

            merge_loads(S_GC, 2, p_c, CT)
            merge_loads(S_GM, 3, p_m, MP)
            with sp.Fori(0, CT) as ct:
                for j, name in enumerate(("b_c", "b_h", "b_gate", "b_b")):
                    load_w(S_B + 4 * ct + j, j, wcols(col[name] + ct * P), KT)
            merge_loads(S_GB, 1, p_b, CT)
            with sp.Fori(0, CT // 2) as i:
                for j in range(2):
                    load_w(S_AG + 2 * i + j, j, wcols(col["a_gate"] + (2 * i + j) * P), KT)
            merge_loads(S_GA, 0, p_a, CT)
            sp.wait_ge(s_zlo, 3 * CT + MP)
            for k in range(KT):
                sp.dma_start(wout_raw[:, k, :], w_out[k * P:(k + 1) * P, :]).then_inc(s_wo[k], 16)
            sp.wait_ge(s_add, 3 * DT)
            sp.dma_start(lng_b[:, :], ln_g.partition_broadcast(P)).then_inc(s_lnp, 16)
            sp.dma_start(lnb_b[:, :], ln_b.partition_broadcast(P)).then_inc(s_lnp, 16)
            sp.wait_ge(s_gl, DT)
            for t in range(NT):
                if t >= 2:
                    sp.wait_ge(s_yk, 2 * (t - 1))
                sp.dma_start(x_tok[:, t % 2, :], x[t * P:(t + 1) * P, :]).then_inc(s_xtk[t % 2], 16)
                if t >= 1:
                    sp.wait_ge(s_yo, t)
                    sp.dma_start(out[(t - 1) * P:t * P, :], y_tok[:, (t - 1) % 2, :]).then_inc(s_store[(t - 1) % 2], 16)
            sp.wait_ge(s_yo, NT)
            sp.dma_start(out[(NT - 1) * P:NT * P, :], y_tok[:, (NT - 1) % 2, :]).then_inc(s_store[(NT - 1) % 2], 16)
            for i in range(2):
                sp.wait_ge(s_store[i], 16 * (NT // 2))

        @block.tensor
        def _(pe):
            def k_steps(s, j, h, k0, k1, bank, nk=KT, r_hi=xT_hi, r_lo=xT_lo):
                t = slice(h * HALF, (h + 1) * HALF)
                for k in range(k0, k1):
                    for e, piece in enumerate(pieces(nk)):
                        if h == 0 and k == piece.start:
                            pe.wait_ge(s_wlo, 2 * s + 1 + e)
                    nc.tensor.matmul(pj[:, bank, :], w_hi[:, j % 2, k, :], r_hi[:, k, t], start=k == 0, stop=False)
                    nc.tensor.matmul(pj[:, bank, :], w_hi[:, j % 2, k, :], r_lo[:, k, t], start=False, stop=False)
                    mm = nc.tensor.matmul(pj[:, bank, :], w_lo[:, j % 2, k, :], r_hi[:, k, t],
                                          start=False, stop=k == nk - 1)
                if k1 == nk:
                    mm.then_inc(s_pj, 1)

            def stream_tile(s, j, nk=KT, r_hi=xT_hi, r_lo=xT_lo, back=3, halves=range(2)):
                for h in halves:
                    if back == 3:
                        pe.wait_ge(s_pjfree, 2 * s + h - 3)
                    elif back == 0 and h == 0:
                        pe.wait_ge(s_pjfree, 2 * s)
                    k_steps(s, j, h, 0, nk, 2 * (j % 2) + h, nk, r_hi, r_lo)

            def stream_part(s, j, n0, n1):
                for n in range(n0, n1):
                    d, h, k = n // (2 * KT), n // KT % 2, n % KT
                    if k == 0:
                        pe.wait_ge(s_pjfree, 2 * (s + d) + h - 1)
                    k_steps(s + d, j + d, h, k, k + 1, h)

            pe.wait_ge(s_wfs, 2)
            for k in range(KT):
                pe.wait_ge(s_xlo, k + 1)
                for h in range(2):
                    for r in (xT_hi, xT_lo):
                        mm = nc.tensor.matmul(po[:, h, :], wf_stack[:, k, :], r[:, k, h * HALF:(h + 1) * HALF],
                                              start=k == 0 and r is xT_hi, stop=k == KT - 1 and r is xT_lo)
                    if k == KT - 1:
                        mm.then_inc(s_f, 1)
                for h in range(2):
                    k_steps(0, 0, h, k, k + 1, h)
            scores_ps = pj[:, 2:4, :].rearrange("p a b -> p (a b)")

            def scores(c, u):
                un, a, i = UNITS * c, u // NT % 2, u % NT
                if u % NT == 0:
                    pe.wait_ge(s_stkl, STK_PAIR * c + STK_HEAD * (u // NT + 1))
                if u > 0:
                    pe.wait_ge(s_sp, un + u)
                L = max(i + 1, 2) * P
                parts = [(0, min(L, HALF))] + ([(HALF, max(L, HALF + 2 * P))] if L > HALF else [])
                for k0, k1 in parts:
                    nc.tensor.matmul(scores_ps[:, k0:k1], q_stack[:, a, i * P:(i + 1) * P],
                                     k_stack_hi[:, a, k0:k1], start=True, stop=False)
                    mm = nc.tensor.matmul(scores_ps[:, k0:k1], q_stack[:, a, i * P:(i + 1) * P],
                                          k_stack_lo[:, a, k0:k1], start=False, stop=True)
                mm.then_inc(s_s, 1)

            def turn(c, u):
                i = u % NT
                top = 2 * (i // 2) + 1
                pe.wait_ge(s_pn, UNITS * c + u + 1)
                for n, slots in enumerate(batches(i)):
                    x_ = tb_before(u) + n
                    pe.wait_ge(s_tlo, TB_PAIR * c + x_ - 1)
                    for q, slot in enumerate(slots):
                        kt = top - slot
                        mm = nc.tensor.transpose(pt[:, x_ % 2, q * P:(q + 1) * P],
                                                 probs[:, u % 2, kt * P:(kt + 1) * P], ident[:, :])
                    mm.then_inc(s_tb, 1)

            def weigh(c, n):
                a, top = n // (NT // 2), 2 * (n % (NT // 2)) + 1
                u = 2 * n + 1
                pe.wait_ge(s_tlo, TB_PAIR * c + tb_before(u) + len(batches(u % NT)))
                if n >= 2:
                    pe.wait_ge(s_oadd, PV_PAIR * c + n - 1)
                for slot in range(top + 1):
                    for r in (pT_hi, pT_lo):
                        mm = nc.tensor.matmul(po[:, n % 2, 0:2 * P],
                                              v_stack[:, a, top - slot, :, :].rearrange("p a b -> p (a b)"),
                                              r[:, slot, :], start=slot == 0 and r is pT_hi,
                                              stop=slot == top and r is pT_lo)
                mm.then_inc(s_pv, 1)

            CUTS = [(2, 2)] * 15 + [(1, 1)]

            def pair(c, last):
                s = 4 * c
                pe.wait_ge(s_pjfree, 8 * c + 6)
                for b in range(2):
                    for k in range(4):
                        mm = nc.tensor.transpose(pt[:, b, k * P:(k + 1) * P],
                                                 v_raw[:, (4 * b + k) * P:(4 * b + k + 1) * P], ident[:, :])
                    mm.then_inc(s_tb, 1)
                for u in range(UNITS):
                    cut, cut2 = CUTS[u]
                    stream_part(s + S_C, S_C, 4 * u, 4 * u + cut)
                    turn(c, u)
                    stream_part(s + S_C, S_C, 4 * u + cut, 4 * u + cut2)
                    if u + 2 < UNITS or not last:
                        scores(c, u + 2)
                    stream_part(s + S_C, S_C, 4 * u + cut2, 4 * u + 4)
                    if u % 2 == 0 and u:
                        weigh(c, u // 2 - 1)
                weigh(c, UNITS // 2 - 1)

            stream_tile(1, 1, back=None, halves=range(0, 1))
            pe.wait_ge(s_cst, 2)
            n = 0
            for m in range(MT):
                pe.wait_ge(s_mn, m + 1)
                for kb in range(KT // 4):
                    if n >= 2:
                        pe.wait_ge(s_mte, n - 1)
                    for k in range(4):
                        mm = nc.tensor.transpose(pt[:, n % 2, k * P:(k + 1) * P],
                                                 mem_sb[:, m, (4 * kb + k) * P:(4 * kb + k + 1) * P], ident[:, :])
                    mm.then_inc(s_mt, 1)
                    n += 1
            stream_tile(1, 1, back=None, halves=range(1, 2))
            pe.wait_ge(s_mte, n)
            pe.wait_ge(s_wkv, 16)
            pe.wait_ge(s_fv, 1)
            for c in range(MP):
                for k in range(KT):
                    mm = nc.tensor.matmul(po[:, c, 0:MEM], wkv[:, k, c * P:(c + 1) * P], memT[:, k, :],
                                          start=k == 0, stop=k == KT - 1)
                mm.then_inc(s_kv, 1)
            for m in range(MT):
                for k in range(KT):
                    mm = nc.tensor.matmul(pt[:, m, 0:M_W], memT[:, k, m * P:(m + 1) * P], wkv[:, k, M_W:2 * M_W],
                                          start=k == 0, stop=k == KT - 1)
                mm.then_inc(s_kv, 1)

            stream_tile(2, 2)
            scores(0, 0)
            scores(0, 1)
            pe.wait_ge(s_kvl, 2 * MP + MT)
            pe.wait_ge(s_pjfree, 2 * S_C)
            with pe.Fori(0, CT - 1) as c:
                pair(c, False)
            pair(CT - 1, True)

            TB, PV, UN = TB_PAIR * CT, PV_PAIR * CT, UNITS * CT

            def mscores(w):
                m, i = w // NT, w % NT
                if i == 0:
                    pe.wait_ge(s_stkl, STK_PAIR * CT + 2 * (m + 1))
                if w >= 2:
                    pe.wait_ge(s_e, UN + w - 1)
                for a in range(2):
                    q = (q_stack, q_stack1)[m][:, a, i * P:(i + 1) * P]
                    o = pj[:, 2 + w % 2, a * MEM:(a + 1) * MEM]
                    nc.tensor.matmul(o, q, km_hi[:, 2 * m + a, :], start=True, stop=False)
                    mm = nc.tensor.matmul(o, q, km_lo[:, 2 * m + a, :], start=False, stop=True)
                mm.then_inc(s_s, 1)

            def mweigh(g):
                pe.wait_ge(s_tlo, TB + 2 * g + 2)
                for a in range(2):
                    pe.wait_ge(s_oadd, PV + 2 * g + a - 1)
                    for t in range(MT):
                        for r in (pT_hi, pT_lo):
                            mm = nc.tensor.matmul(
                                po[:, a, 0:2 * P],
                                vm_stack[:, t, 2 * (g // (NT // 2)) + a, :, :].rearrange("p a b -> p (a b)"),
                                r[:, MT * a + t, :], start=t == 0 and r is pT_hi, stop=t == MT - 1 and r is pT_lo)
                    mm.then_inc(s_pv, 1)

            pe.wait_ge(s_sp, UN)
            mscores(0)
            mscores(1)
            for w in range(2 * NT):
                s, n0, d = (S_M, 6 * w, 3) if w < NT else (S_M + 3, 8 * (w - NT), 4)
                stream_part(s, s, n0, n0 + d)
                pe.wait_ge(s_pn, UN + w + 1)
                pe.wait_ge(s_tlo, TB + w - 1)
                for q in range(2 * MT):
                    mm = nc.tensor.transpose(pt[:, w % 2, q * P:(q + 1) * P],
                                             probs[:, w % 2, q * P:(q + 1) * P], ident[:, :])
                mm.then_inc(s_tb, 1)
                stream_part(s, s, n0 + d, n0 + 2 * d)
                if w % 2 == 0 and w:
                    mweigh(w // 2 - 1)
                if w + 2 < 2 * NT:
                    mscores(w + 2)
            mweigh(NT - 1)
            for j in range(2):
                stream_tile(S_GC - 2 + j, j, back=0)

            def merge(s0, nk, r_hi, r_lo, z_count):
                with pe.Fori(0, DT) as dt:
                    stream_tile(s0 + 2 * dt, 0)
                    pe.wait_ge(s_zlo, z_count)
                    stream_tile(s0 + 2 * dt + 1, 1, nk, r_hi, r_lo)

            def channel_mean(bank, done):
                for h in range(2):
                    for ct in range(CT):
                        for r in (z_hi, z_lo):
                            mm = nc.tensor.matmul(bank[:, h, :], ones_ln[:, :], r[:, ct, h * HALF:(h + 1) * HALF],
                                                  start=ct == 0 and r is z_hi, stop=ct == CT - 1 and r is z_lo)
                    mm.then_inc(done, 1)

            merge(S_GC, CT, z_hi, z_lo, CT)
            merge(S_GM, MP, zm_hi, zm_lo, CT + MP)
            stream_tile(S_B, 0)
            pe.wait_ge(s_cst, 3)
            pe.wait_ge(s_al, CT)
            channel_mean(pt, s_lnm)
            for j in range(1, 3):
                stream_tile(S_B + j, j)
            pe.wait_ge(s_al, 2 * CT)
            channel_mean(po, s_lnv)
            stream_tile(S_B + 3, 3)
            with pe.Fori(1, CT) as ct:
                for j in range(4):
                    stream_tile(S_B + 4 * ct + j, j)
            merge(S_GB, CT, z_hi, z_lo, CT + MP + CT)
            with pe.Fori(0, CT // 2) as i:
                for j in range(2):
                    stream_tile(S_AG + 2 * i + j, j)
            merge(S_GA, CT, z_hi, z_lo, CT + MP + 2 * CT)

            def out_step(n, k, part):
                tk, c = slice(n // 2 * P, (n // 2 + 1) * P), slice(n % 2 * HALF, (n % 2 + 1) * HALF)
                m_hi = xT_hi[:, k, tk] if k else merged_hi0[:, tk]
                o_hi = wout_hi[:, k, c] if k else wout_hi0[:, c]
                m, o = ((m_hi, o_hi), (m_hi, wout_lo[:, k, c]), (xT_lo[:, k, tk], o_hi))[part]
                mm = nc.tensor.matmul(pj[:, n % 4, :], m, o, start=k == 0 and part == 0, stop=k == KT - 1 and part == 2)
                if k == KT - 1 and part == 2:
                    mm.then_inc(s_out_pj, 1)

            for k in range(KT - 1):
                pe.wait_ge(s_gh, k + 1)
                for part in range(3):
                    if part:
                        pe.wait_ge((s_wol, s_gl)[part - 1], k + 1)
                    for n in (0, 2, 1, 3):
                        if k == 0 and part == 0 and n == 0:
                            pe.wait_ge(s_pjfree, 2 * S_END - 2)
                        elif k == 0 and part == 0 and n == 1:
                            pe.wait_ge(s_pjfree, 2 * S_END)
                        out_step(n, k, part)
            pe.wait_ge(s_wol, KT)
            pe.wait_ge(s_gl, KT)
            for n in range(4):
                for part in range(3):
                    out_step(n, KT - 1, part)
            for n in range(4, 2 * NT):
                pe.wait_ge(s_yk, n - 3)
                for k in range(KT):
                    for part in range(3):
                        out_step(n, k, part)

        @block.scalar
        def _(act):
            def split_w(sh, j, nk=KT, free=True, part=slice(0, 2)):
                if part.start == 0:
                    act.wait_ge(s_wld[j % 2], raw_count(sh, j))
                    if free:
                        act.wait_ge(s_pj, 4 * sh + 2 * j - 2)
                for k in pieces(nk)[part]:
                    nc.scalar.activation(w_hi[:, j % 2, k, :], w_raw[:, j % 2, k, :], ACT.Copy).then_inc(s_whi, 1)

            def evac_half(s, bank, h, func, scale):
                act.wait_ge(s_pj, 2 * s + h + 1)
                if h == 0:
                    act.wait_ge(s_pjfree, 2 * s)
                nc.scalar.activation(xt[:, h * HALF:(h + 1) * HALF], pj[:, bank, :], func, scale=scale).then_inc(s_xt, 1)

            def evac(s, j, func, scale):
                for h in range(2):
                    evac_half(s, 2 * (j % 2) + h, h, func, scale)

            act.wait_ge(s_wf, 16)
            act.wait_ge(s_wfs, 1)
            nc.scalar.activation(wf_stack[:, :, 0:HEADS], wf_raw[:, :, :], ACT.Copy).then_inc(s_fa, 1)
            for k in range(KT):
                act.wait_ge(s_x[k], 16)
                nc.scalar.activation(xT_hi[:, k, :], x_raw[:, k, :], ACT.Copy).then_inc(s_xhi, 1)
                if k == 0:
                    split_w(0, 0, free=False)
            split_w(0, 1, free=False)
            act.wait_ge(s_ms, MT)
            act.wait_ge(s_fix, 1)
            nc.scalar.activation(rstd[:, 0:MT], mv[:, :, 1], ACT.Sqrt, bias=eps[:, 0:1]).then_inc(s_mr, 1)
            for h in range(2):
                act.wait_ge(s_f, h + 1)
                nc.scalar.activation(f_l[:, h * HALF:(h + 1) * HALF], po[32:32 + HEADS, h, :],
                                     ACT.Copy).then_inc(s_fa, 1)
            act.wait_ge(s_fv, 1)
            nc.scalar.activation(f_abs[:, :], f_z[:, :], ACT.Abs).then_inc(s_fa, 1)
            act.wait_ge(s_fa, 4)
            nc.scalar.activation(f_e[:, :], f_abs[:, :], ACT.Exp, scale=-1.0).then_inc(s_fa, 1)
            act.wait_ge(s_fv, 2)
            nc.scalar.activation(f_l[:, :], f_u[:, :], ACT.Ln).then_inc(s_fa, 1)
            split_w(1, 0)
            for c in range(MP):
                act.wait_ge(s_kv, c + 1)
                for a in range(2):
                    b, o = DH * a, DH * (1 - a)
                    for r in (b, o):
                        op = nc.scalar.activation(km_hi[r:r + DH, 2 * c + a, :], po[b:b + DH, c, 0:MEM], ACT.Copy)
                    op.then_inc(s_kvh, 1)
            for m in range(MT):
                act.wait_ge(s_kv, MP + m + 1)
                nc.scalar.activation(vm_stack[:, m, :, 0, :],
                                     pt[:, m, 0:M_W].rearrange("p (h d) -> p h d", d=DH), ACT.Copy).then_inc(s_kvh, 1)

            def raw_half(s, h, dst, scale):
                act.wait_ge(s_pj, 2 * s + h + 1)
                nc.scalar.activation(dst[:, h * HALF:(h + 1) * HALF], pj[:, h, :], ACT.Copy,
                                     scale=scale).then_inc(s_pjfree, 1)

            def out_shift(a, n, count, first=False):
                b, o = DH * a, DH * (1 - a)
                act.wait_ge(s_pv, count + 1)
                if not first:
                    act.wait_ge(s_oadd, count)
                nc.scalar.activation(otmp[b:b + DH, :], po[o:o + DH, n % 2, 0:2 * P], ACT.Copy).then_inc(s_osh, 1)

            def q_hi(a, src, dst):
                b = DH * a
                nc.scalar.activation(dst[b:b + DH, a, :], src[b:b + DH, :], ACT.Copy).then_inc(s_stkh, 1)

            def k_hi(a):
                b = DH * a
                for r in (b, DH - b):
                    nc.scalar.activation(k_stack_hi[r:r + DH, a, :], k_raw[b:b + DH, :], ACT.Copy).then_inc(s_stkh, 1)

            def exp(c, u):
                i = u % NT
                act.wait_ge(s_sp, UNITS * c + u + 1)
                nc.scalar.activation(probs[:, u % 2, 0:(i + 1) * P], probs[:, u % 2, 0:(i + 1) * P], ACT.Exp,
                                     scale=-1.0, bias=rmin[:, u % 2, 1:2],
                                     accum_out=rsum[:, u % 2, 0:1]).then_inc(s_e, 1)

            def turned_hi(c, u):
                i = u % NT
                for n, slots in enumerate(batches(i)):
                    act.wait_ge(s_tb, TB_PAIR * c + tb_before(u) + n + 1)
                    if i % 2 == 0 and n == 0 and u > 0:
                        act.wait_ge(s_pv, PV_PAIR * c + u // 2)
                    nc.scalar.activation(
                        pT_hi[:, slots[0]:slots[-1] + 1, (i % 2) * P:(i % 2 + 1) * P],
                        pt[:, (tb_before(u) + n) % 2, 0:len(slots) * P].rearrange("p (k q) -> p k q", q=P),
                        ACT.Copy).then_inc(s_thi, 1)

            def pair(c, last):
                s = 4 * c
                for b in range(2):
                    act.wait_ge(s_tb, TB_PAIR * c + b + 1)
                    nc.scalar.activation(v_stack[:, :, 4 * b:4 * b + 4, 0, :].rearrange("p a k d -> p k a d"),
                                         pt[:, b, :].rearrange("p (k a d) -> p k a d", k=4, a=2),
                                         ACT.Copy).then_inc(s_thi, 1)
                for k in range(UNITS):
                    if k:
                        turned_hi(c, k - 1)
                        if k + 1 < UNITS or not last:
                            exp(c, k + 1)
                    if k % 2 and k > 1:
                        n = k // 2 - 1
                        out_shift(n // (NT // 2), n, PV_PAIR * c + n, first=n == 0)
                    if k % 4 == 0:
                        split_w(2 * c, 4 + k // 4)
                    for a, kq, kk in ((0, 9, 10), (1, 14, 15)):
                        if k == kq:
                            act.wait_ge(s_s, UNITS * c + NT * (a + 1))
                            act.wait_ge(s_pjfree, 8 * c + 8)
                            q_hi(a, q_raw, q_stack)
                        if k == kk and not last:
                            act.wait_ge(s_pjfree, 8 * c + 10)
                            k_hi(a)
                    h = k // 2 % 2 ^ 1
                    if k in (2, 4):
                        raw_half(s + 3, h, q_raw, QSCALE)
                    if k in (6, 8):
                        raw_half(s + 4, h, k_raw, QSCALE if last else 1.0)
                    if k in (10, 12) and not last:
                        raw_half(s + 5, h, v_raw, 0.5)
                    if last and k in (10, 12):
                        evac_half(s + 5, k // 2 - 5, k // 2 - 5, ACT.Tanh, 0.5)
                    if k == 14:
                        evac_half(s + 6, 0, 0, ACT.Tanh, 0.5)
                turned_hi(c, UNITS - 1)
                if not last:
                    exp(c, UNITS + 1)
                evac_half(s + 6, 1, 1, ACT.Tanh, 0.5)
                out_shift(1, UNITS // 2 - 1, PV_PAIR * c + UNITS // 2 - 1)

            act.wait_ge(s_pjfree, 2)
            q_hi(0, q_raw, q_stack)
            act.wait_ge(s_pjfree, 4)
            k_hi(0)
            q_hi(1, q_raw, q_stack)
            k_hi(1)
            split_w(1, 1)
            exp(0, 0)
            exp(0, 1)
            with act.Fori(0, CT - 1) as c:
                pair(c, False)
            pair(CT - 1, True)

            TB, PV, UN = TB_PAIR * CT, PV_PAIR * CT, UNITS * CT

            def mexp(w):
                act.wait_ge(s_sp, UN + w + 1)
                if w >= 2:
                    act.wait_ge(s_tb, TB + w - 1)
                for a in range(2):
                    op = nc.scalar.activation(probs[:, w % 2, a * MEM:(a + 1) * MEM],
                                              pj[:, 2 + w % 2, a * MEM:(a + 1) * MEM], ACT.Exp,
                                              bias=rmin[:, w % 2, a:a + 1], accum_out=rsum[:, w % 2, a:a + 1])
                op.then_inc(s_e, 1)

            def mturned_hi(w):
                act.wait_ge(s_tb, TB + w + 1)
                if w % 2 == 0:
                    act.wait_ge(s_pv, PV + w)
                nc.scalar.activation(pT_hi[:, 0:2 * MT, (w % 2) * P:(w % 2 + 1) * P],
                                     pt[:, w % 2, :].rearrange("p (k q) -> p k q", q=P), ACT.Copy).then_inc(s_thi, 1)

            mexp(0)
            for w in range(2 * NT):
                if w:
                    mturned_hi(w - 1)
                if w + 1 < 2 * NT:
                    mexp(w + 1)
                for s, h in M_ENDS.get(w, ()):
                    if s == S_M or (s - S_A) % 2 == 0:
                        evac_half(s, h, h, ACT.Tanh, 0.5)
                if w % 2 == 0 and w:
                    for a in range(2):
                        out_shift(a, a, PV + w - 2 + a)
                for s in M_STARTS.get(w, ()):
                    split_w((s + 1) // 2, (s + 1) % 2)
                if w in (2, 3):
                    if w == 2:
                        act.wait_ge(s_dm, 1 + UNITS * CT)
                    q_hi(w - 2, k_raw, q_stack1)
            mturned_hi(2 * NT - 1)
            for s, h in M_ENDS[2 * NT]:
                if (s - S_A) % 2 == 0:
                    evac_half(s, h, h, ACT.Tanh, 0.5)
            for a in range(2):
                out_shift(a, a, PV + 2 * NT - 2 + a)
            split_w(S_GC // 2 - 1, 1)
            for ct in range(CT):
                if ct == 0:
                    act.wait_ge(s_zpre, CT + MP)
                nc.scalar.activation(z_hi[:, ct, :], z_raw[:, ct, :], ACT.Copy).then_inc(s_zhi, 1)
            evac(S_GC - 2, 0, ACT.Tanh, 0.5)
            for m in range(MP):
                nc.scalar.activation(zm_hi[:, m, :], zm_raw[:, m, :], ACT.Copy).then_inc(s_zhi, 1)
            split_w(S_GC // 2, 0)

            def merge_step(s0, dt, nk, last=False):
                sh = s0 // 2 + dt
                split_w(sh, 1, nk)
                evac_half(s0 + 2 * dt, 0, 0, ACT.Tanh, 0.5)
                if not last:
                    split_w(sh, 2, part=slice(0, 1))
                evac_half(s0 + 2 * dt, 1, 1, ACT.Tanh, 0.5)
                if not last:
                    split_w(sh, 2, part=slice(1, 2))

            with act.Fori(0, DT) as dt:
                merge_step(S_GC, dt, CT)
            with act.Fori(0, DT) as dt:
                merge_step(S_GM, dt, MP)
            def b_step(ct, squares=False):
                s = S_B + 4 * ct
                sh = S_B // 2 + 2 * ct
                split_w(sh, 1)
                evac(s, 0, ACT.Copy, 1.0)
                split_w(sh, 2)
                if squares:
                    for t in range(CT):
                        act.wait_ge(s_lnc, t + 1)
                        nc.scalar.activation(z_raw[:, t, :], glu[:, t, PAD_A:WA], ACT.Square).then_inc(s_sq, 1)
                        act.wait_ge(s_sq, t + 1)
                        nc.scalar.activation(z_hi[:, t, :], z_raw[:, t, :], ACT.Copy).then_inc(s_ah, 1)
                split_w(sh, 3)
                evac(s + 2, 2, ACT.Tanh, 0.5)
                split_w(sh, 4)
                act.wait_ge(s_zpre, CT + MP + ct + 1)
                nc.scalar.activation(z_hi[:, bass.ds(ct, 1), :].rearrange("p o t -> p (o t)"), bz[:, :],
                                     ACT.Copy).then_inc(s_zhi, 1)

            for ct in range(CT):
                act.wait_ge(s_ca, CONV_STEPS - UNIT_STEPS * (CT - 1 - ct))
                nc.scalar.activation(z_hi[:, ct, :], glu[:, ct, PAD_A:WA], ACT.Copy).then_inc(s_ah, 1)
            b_step(0, squares=True)
            with act.Fori(1, CT) as ct:
                b_step(ct)
            act.wait_ge(s_lnv, 2)
            for h in range(2):
                op = nc.scalar.activation(sg[:, h * HALF:(h + 1) * HALF], po[:, h, :], ACT.Sqrt, bias=eps[:, 0:1])
            op.then_inc(s_sd, 1)
            for dt in range(2):
                merge_step(S_GB, dt, CT)
            for ct in range(CT):
                act.wait_ge(s_an, ct + 1)
                nc.scalar.activation(glu[:, ct, PAD_A:WA], glu[:, ct, PAD_A:WA], ACT.Identity,
                                     scale=lag[:, ct:ct + 1], bias=lab[:, ct:ct + 1]).then_inc(s_ag, 1)
            for ct in range(CT):
                act.wait_ge(s_ag, ct + 1)
                if ct >= 1:
                    act.wait_ge(s_as, ct)
                nc.scalar.activation(an_rstd[:, :], glu[:, ct, PAD_A:WA], ACT.Tanh, scale=0.5).then_inc(s_at, 1)
            with act.Fori(2, DT) as dt:
                merge_step(S_GB, dt, CT)
            act.wait_ge(s_as, CT)
            with act.Fori(0, CT // 2) as i:
                sh = S_AG // 2 + i
                for j in range(2):
                    split_w(sh, j + 1)
                    evac(S_AG + 2 * i + j, j, ACT.Tanh, 0.5)
                    act.wait_ge(s_zpre, 2 * CT + MP + 2 * i + j + 1)
                    nc.scalar.activation(z_hi[:, bass.ds(2 * i + j, 1), :].rearrange("p o t -> p (o t)"), sg[:, :],
                                         ACT.Copy).then_inc(s_zhi, 1)
            with act.Fori(0, DT - 1) as dt:
                merge_step(S_GA, dt, CT)
            merge_step(S_GA, DT - 1, CT, last=True)
            for k in range(KT):
                act.wait_ge(s_wo[k], 16)
                if k == 1:
                    act.wait_ge(s_pj, 2 * S_END)
                nc.scalar.activation(wout_hi[:, k, :] if k else wout_hi0[:, :], wout_raw[:, k, :],
                                     ACT.Copy).then_inc(s_woh, 1)
                act.wait_ge(s_add, 3 * DT if k == KT - 1 else 2 * DT + k + 1)
                nc.scalar.activation(xT_hi[:, k, :] if k else merged_hi0[:, :], merged[:, k, :], ACT.Copy,
                                     scale=0.5).then_inc(s_gh, 1)
            for t in range(NT):
                act.wait_ge(s_mvr, t + 1)
                nc.scalar.activation(rstd[:, t % 2:t % 2 + 1], mv[:, t % 2, 1:2], ACT.Sqrt,
                                     bias=eps[:, 0:1]).then_inc(s_osd, 1)

        @block.gpsimd
        def _(pool):
            def split_w(s, j, nk=KT):
                for e, k in enumerate(pieces(nk)):
                    pool.wait_ge(s_whi, 2 * s + e + 1)
                    nc.gpsimd.tensor_tensor(w_lo[:, j % 2, k, :], w_raw[:, j % 2, k, :], w_hi[:, j % 2, k, :],
                                            ALU.subtract).then_inc(s_wlo, 1)

            nc.gpsimd.memset(ident[:, :], 0.0).then_inc(s_cst, 1)
            pool.wait_ge(s_cst, 1)
            nc.gpsimd.affine_select(out=ident[:, :], in_=ident[:, :], compare_op=ALU.not_equal, fill=1.0, base=0,
                                    pattern=[[-1, P]], channel_multiplier=1).then_inc(s_cst, 1)
            nc.gpsimd.memset(maskc[:, :], 0.0).then_inc(s_bd, 1)
            pool.wait_ge(s_bd, 1)
            nc.gpsimd.affine_select(out=maskc[:, :], in_=maskc[:, :], compare_op=ALU.is_ge, fill=-BIG, base=0,
                                    pattern=[[-1, P]], channel_multiplier=1).then_inc(s_bd, 1)
            split_w(0, 0)
            split_w(1, 1)
            pool.wait_ge(s_bd, 2)

            def diag_bias(c, u):
                a, i = u // NT % 2, u % NT
                if i == 0:
                    pool.wait_ge(s_bias[a], 16 * (c + 1 + u // UNITS))
                pool.wait_ge(s_dm, UNITS * c + u)
                nc.gpsimd.tensor_tensor(bdiag[:, u % 2, :], bias[:, a, i * P:(i + 1) * P], maskc[:, :],
                                        ALU.add).then_inc(s_bd, 1)

            split_w(2, 2)
            pool.wait_ge(s_bias[0], 16)
            for u in range(2):
                nc.gpsimd.tensor_tensor(bdiag[:, u, :], bias[:, 0, u * P:(u + 1) * P], maskc[:, :],
                                        ALU.add).then_inc(s_bd, 1)
            split_w(3, 3)

            def pair(c, last):
                for k in range(UNITS):
                    if k + 2 < UNITS or not last:
                        diag_bias(c, k + 2)
                    if k % 4 == 0:
                        split_w(4 * c + 4 + k // 4, 4 + k // 4)
                pool.wait_ge(s_oadd, PV_PAIR * (c + 1))
                pool.wait_ge(s_pjfree, 8 * c + 14)
                z = z_raw[:, bass.ds(c, 1), :].rearrange("p o t -> p (o t)")
                nc.gpsimd.tensor_tensor(z, z, sg[:, :], ALU.mult).then_inc(s_zpre, 1)

            with pool.Fori(0, CT - 1) as c:
                pair(c, False)
            pair(CT - 1, True)
            for s in range(S_M + 1, S_GC + 1):
                split_w(s, s)
            with pool.Fori(0, DT) as dt:
                split_w(S_GC + 2 * dt + 1, 1, CT)
                split_w(S_GC + 2 * dt + 2, 2)

            def merge_step(s0, nk, d2, last=False):
                for e in range(2):
                    dt = 2 * d2 + e
                    split_w(s0 + 2 * dt + 1, 1, nk)
                    if not (last and e == 1):
                        split_w(s0 + 2 * dt + 2, 2)
                    else:
                        pool.wait_ge(s_woh, 1)
                        nc.gpsimd.tensor_tensor(wout_lo[:, 0, :], wout_raw[:, 0, :], wout_hi0[:, :],
                                                ALU.subtract).then_inc(s_wol, 1)
                    pool.wait_ge(s_pjfree, 2 * (s0 + 2 * dt + 2))
                    md = merged[:, bass.ds(dt, 1), :].rearrange("p o t -> p (o t)")
                    nc.gpsimd.tensor_tensor(md, md, ytmp[:, e, :], ALU.add).then_inc(s_add, 1)

            with pool.Fori(0, DT // 2) as d2:
                merge_step(S_GM, MP, d2)
            nc.gpsimd.memset(ones_ln[:, :].bitcast(mybir.dt.uint32), (127 - (A_W.bit_length() - 1)) << 23
                             ).then_inc(s_cst, 1)
            with pool.Fori(0, CT) as ct:
                for j in range(1, 5):
                    split_w(S_B + 4 * ct + j, j)
            with pool.Fori(0, DT // 2) as d2:
                merge_step(S_GB, CT, d2)
            with pool.Fori(0, CT // 2) as i:
                for j in range(1, 3):
                    split_w(S_AG + 2 * i + j, j)
            with pool.Fori(0, DT // 2 - 1) as d2:
                merge_step(S_GA, CT, d2)
            merge_step(S_GA, CT, DT // 2 - 1, last=True)

        @block.vector
        def _(dve):
            def hs(h):
                return slice(h * HALF, (h + 1) * HALF)

            def raw_evac(s, j, dst, scale=None):
                for h in range(2):
                    dve.wait_ge(s_pj, 2 * s + h + 1)
                    if scale is None:
                        nc.vector.tensor_copy(dst[:, hs(h)], pj[:, 2 * (j % 2) + h, :]).then_inc(s_pjfree, 1)
                    else:
                        nc.vector.tensor_scalar(dst[:, hs(h)], pj[:, 2 * (j % 2) + h, :], scale, None,
                                                ALU.mult).then_inc(s_pjfree, 1)

            def gate_evac(s, j, xt_count):
                for h in range(2):
                    dve.wait_ge(s_xt, xt_count + h + 1)
                    nc.vector.scalar_tensor_tensor(out=sg[:, hs(h)], in0=xt[:, hs(h)], scalar=1.0,
                                                   in1=pj[:, 2 * (j % 2) + h, :], op0=ALU.add,
                                                   op1=ALU.mult).then_inc(s_pjfree, 1)

            nc.vector.memset(wf_stack[:, :, :].bitcast(mybir.dt.uint32), 0).then_inc(s_wfs, 1)
            nc.vector.memset(eps[:, :], EPS).then_inc(s_fix, 1)
            dve.wait_ge(s_fa, 1)
            nc.vector.tensor_tensor(wf_stack[:, :, 32:32 + HEADS], wf_raw[:, :, :], wf_stack[:, :, 0:HEADS],
                                    ALU.subtract).then_inc(s_wfs, 1)
            for k in range(KT):
                dve.wait_ge(s_xhi, k + 1)
                nc.vector.tensor_tensor(xT_lo[:, k, :], x_raw[:, k, :], xT_hi[:, k, :], ALU.subtract).then_inc(s_xlo, 1)
            dve.wait_ge(s_mem, 16)
            for m in range(MT):
                for h in range(2):
                    op = nc.vector.bn_stats(stats[:, m, h, :], mem_sb[:, m, hs(h)])
            op.then_inc(s_st, 1)
            dve.wait_ge(s_st, 1)
            for m in range(MT):
                nc.vector.bn_aggr(mv[:, m, :], stats[:, m, :, :]).then_inc(s_ms, 1)
            dve.wait_ge(s_mr, 1)
            nc.vector.reciprocal(rinv[:, 0, :], rstd[:, 0:MT]).then_inc(s_mr, 1)
            dve.wait_ge(s_mr, 2)
            for m in range(MT):
                nc.vector.tensor_scalar(mem_sb[:, m, :], mem_sb[:, m, :], mv[:, m, 0:1], rinv[:, 0, m:m + 1],
                                        ALU.subtract, ALU.mult).then_inc(s_mn, 1)
            dve.wait_ge(s_par, 16 * 8)
            dve.wait_ge(s_fa, 3)
            for h in range(2):
                op = nc.vector.scalar_tensor_tensor(out=f_z[:, hs(h)], in0=po[0:HEADS, h, :], scalar=bf[:, 0:1],
                                                    in1=f_l[:, hs(h)], op0=ALU.add, op1=ALU.add)
            op.then_inc(s_fv, 1)
            n = 0
            for m in range(MT):
                for kb in range(KT // 4):
                    dve.wait_ge(s_mt, n + 1)
                    for k in range(4):
                        kk = 4 * kb + k
                        op = nc.vector.tensor_scalar(memT[:, kk, m * P:(m + 1) * P], pt[:, n % 2, k * P:(k + 1) * P],
                                                     memg[:, kk:kk + 1], memb[:, kk:kk + 1], ALU.mult, ALU.add)
                    op.then_inc(s_mte, 1)
                    n += 1
            raw_evac(0, 0, q_raw, QSCALE)
            dve.wait_ge(s_fa, 5)
            nc.vector.tensor_scalar(f_u[:, :], f_e[:, :], 1.0, None, ALU.add).then_inc(s_fv, 1)
            dve.wait_ge(s_fv, 2)
            nc.vector.scalar_tensor_tensor(out=f_e[:, :], in0=f_u[:, :], scalar=1.0, in1=f_e[:, :],
                                           op0=ALU.subtract, op1=ALU.subtract).then_inc(s_fv, 1)
            nc.vector.reciprocal(f_r[:, :], f_u[:, :]).then_inc(s_fv, 1)
            dve.wait_ge(s_fv, 4)
            nc.vector.scalar_tensor_tensor(out=f_e[:, :], in0=f_e[:, :], scalar=-1.0, in1=f_r[:, :],
                                           op0=ALU.mult, op1=ALU.mult).then_inc(s_fv, 1)
            dve.wait_ge(s_fa, 6)
            dve.wait_ge(s_fv, 5)
            nc.vector.tensor_tensor(f_l[:, :], f_l[:, :], f_e[:, :], ALU.add).then_inc(s_fv, 1)
            nc.vector.tensor_scalar(f_z[:, :], f_z[:, :], -1.0, 0.0, ALU.mult, ALU.max).then_inc(s_fv, 1)
            dve.wait_ge(s_fv, 7)
            nc.vector.tensor_tensor(f_l[:, :], f_l[:, :], f_z[:, :], ALU.add).then_inc(s_fv, 1)
            nc.vector.memset(f_abs[:, :], 1.0).then_inc(s_fv, 1)
            dve.wait_ge(s_fv, 9)
            nc.vector.tensor_tensor_scan(negcum[:, :], f_abs[:, :], f_l[:, :], 0.0, ALU.mult,
                                         ALU.add).then_inc(s_fv, 1)
            raw_evac(1, 1, k_raw)
            for c in range(MP):
                for a in range(2):
                    b, o = DH * a, DH * (1 - a)
                    dve.wait_ge(s_kvh, 2 * c + a + 1)
                    for r in (b, o):
                        op = nc.vector.tensor_tensor(km_lo[r:r + DH, 2 * c + a, :], po[b:b + DH, c, 0:MEM],
                                                     km_hi[b:b + DH, 2 * c + a, :], ALU.subtract)
                    op.then_inc(s_kvl, 1)
            for m in range(MT):
                dve.wait_ge(s_kvh, 2 * MP + m + 1)
                nc.vector.tensor_tensor(vm_stack[:, m, :, 1, :], pt[:, m, 0:M_W].rearrange("p (h d) -> p h d", d=DH),
                                        vm_stack[:, m, :, 0, :], ALU.subtract).then_inc(s_kvl, 1)
            dve.wait_ge(s_fv, F_STEPS)
            for t in (pT_hi, pT_lo):
                op = nc.vector.memset(t[:, 0, 0:P].bitcast(mybir.dt.uint32), 0)
            op.then_inc(s_dm, 1)

            def out_add(a, n, dst, count):
                b = DH * a
                dve.wait_ge(s_osh, count + 1)
                nc.vector.tensor_tensor(dst[b:b + DH], po[b:b + DH, n % 2, 0:2 * P], otmp[b:b + DH, :],
                                        ALU.add).then_inc(s_oadd, 1)

            def gate_half(h, dst, xt_count):
                dve.wait_ge(s_xt, xt_count + h + 1)
                nc.vector.scalar_tensor_tensor(out=dst[:, hs(h)], in0=xt[:, hs(h)], scalar=1.0, in1=pj[:, h, :],
                                               op0=ALU.add, op1=ALU.mult).then_inc(s_pjfree, 1)

            def q_lo(a, src, dst, count):
                b, o = DH * a, DH * (1 - a)
                dve.wait_ge(s_stkh, count)
                nc.vector.tensor_tensor(dst[o:o + DH, a, :], src[b:b + DH, :], dst[b:b + DH, a, :],
                                        ALU.subtract).then_inc(s_stkl, 1)

            def k_lo(a, half, count):
                b, r = DH * a, DH * (a ^ half)
                dve.wait_ge(s_stkh, count)
                nc.vector.tensor_tensor(k_stack_lo[r:r + DH, a, :], k_raw[b:b + DH, :],
                                        k_stack_hi[b:b + DH, a, :], ALU.subtract).then_inc(s_stkl, 1)

            def biased(c, u):
                a, i = u // NT % 2, u % NT
                un, tb = UNITS * c, TB_PAIR * c
                dve.wait_ge(s_s, un + u + 1)
                dve.wait_ge(s_bd, 2 + un + u + 1)
                if i == 0:
                    dve.wait_ge(s_bias[a], 16 * (c + 1 + u // UNITS))
                if u >= 2:
                    dve.wait_ge(s_tb, tb + tb_before(u - 1))
                sc = pj[:, 2:4, :].rearrange("p a b -> p (a b)")
                d = slice(i * P, (i + 1) * P)
                mn = rmin[:, u % 2, 0:1] if i else rmin[:, u % 2, 1:2]
                dve.sem_inc(s_passed[0], 1)
                nc.vector.tensor_tensor_reduce(probs[:, u % 2, d], sc[:, d], bdiag[:, u % 2, :], -1.0, BIG,
                                               ALU.add, ALU.min, mn).then_inc(s_dm, 1)
                dve.wait_ge(s_dm, 1 + un + u + 1)
                if i:
                    dve.sem_inc(s_passed[0], 1)
                    nc.vector.tensor_tensor_reduce(probs[:, u % 2, 0:i * P], sc[:, 0:i * P], bias[:, a, 0:i * P],
                                                   -1.0, rmin[:, u % 2, 0:1], ALU.add, ALU.min,
                                                   rmin[:, u % 2, 1:2]).then_inc(s_sp, 1)
                else:
                    nc.vector.tensor_copy(rmin[:, u % 2, 0:1], rmin[:, u % 2, 1:2]).then_inc(s_sp, 1)

            def normalise(c, u):
                un, i = UNITS * c, u % NT
                dve.wait_ge(s_e, un + u + 1)
                nc.vector.reciprocal(rinv[:, u % 2, 0:1], rsum[:, u % 2, 0:1]).then_inc(s_ri, 1)
                dve.wait_ge(s_ri, un + u + 1)
                nc.vector.tensor_scalar(probs[:, u % 2, 0:(i + 1) * P], probs[:, u % 2, 0:(i + 1) * P],
                                        rinv[:, u % 2, 0:1], None, ALU.mult).then_inc(s_pn, 1)

            def turned_lo(c, u):
                i = u % NT
                for n, slots in enumerate(batches(i)):
                    dve.wait_ge(s_thi, TB_PAIR * c + tb_before(u) + n + 1)
                    q = slice((i % 2) * P, (i % 2 + 1) * P)
                    nc.vector.tensor_tensor(
                        pT_lo[:, slots[0]:slots[-1] + 1, q],
                        pt[:, (tb_before(u) + n) % 2, 0:len(slots) * P].rearrange("p (k q) -> p k q", q=P),
                        pT_hi[:, slots[0]:slots[-1] + 1, q], ALU.subtract).then_inc(s_tlo, 1)

            def pair(c, last):
                s, stk = 4 * c, STK_PAIR * (c + 1)
                for b in range(2):
                    dve.wait_ge(s_thi, TB_PAIR * c + b + 1)
                    nc.vector.tensor_tensor(v_stack[:, :, 4 * b:4 * b + 4, 1, :].rearrange("p a k d -> p k a d"),
                                            pt[:, b, :].rearrange("p (k a d) -> p k a d", k=4, a=2),
                                            v_stack[:, :, 4 * b:4 * b + 4, 0, :].rearrange("p a k d -> p k a d"),
                                            ALU.subtract).then_inc(s_tlo, 1)

                def zc(n):
                    g = n % (NT // 2)
                    return z_raw[:, bass.ds(c, 1), g * 2 * P:(g + 1) * 2 * P].rearrange("p o t -> p (o t)")

                for k in range(1, UNITS):
                    if k + 1 < UNITS or not last:
                        biased(c, k + 1)
                    turned_lo(c, k - 1)
                    if k + 1 < UNITS or not last:
                        normalise(c, k + 1)
                    if k == 1:
                        q_lo(1, q_raw, q_stack, STK_PAIR * c + 4)
                    if k in (2, 3):
                        k_lo(1, k - 2, STK_PAIR * c + 3 + k)
                    if k == 10:
                        q_lo(0, q_raw, q_stack, stk + 1)
                    if k in (11, 12) and not last:
                        k_lo(0, k - 11, stk + k - 9)
                    if k == 15 and last:
                        q_lo(1, q_raw, q_stack, stk + 2)
                    h = k // 2 % 2 ^ 1
                    if k in (10, 12) and last:
                        gate_half(h, v_raw, 2 * c)
                    if k == 14:
                        gate_half(0, sg, 2 * c + 2 * last)
                    if k % 2 and k > 1:
                        n = k // 2 - 1
                        out_add(n // (NT // 2), n, zc(n), PV_PAIR * c + n)
                if not last:
                    biased(c, UNITS + 1)
                turned_lo(c, UNITS - 1)
                gate_half(1, sg, 2 * c + 2 * last)
                if not last:
                    normalise(c, UNITS + 1)
                n = UNITS // 2 - 1
                out_add(1, n, zc(n), PV_PAIR * c + n)

            q_lo(0, q_raw, q_stack, 1)
            for half in range(2):
                k_lo(0, half, 2 + half)
            raw_evac(2, 2, v_raw, 0.5)
            for u in range(2):
                biased(0, u)
                normalise(0, u)
            with dve.Fori(0, CT - 1) as c:
                pair(c, False)
            pair(CT - 1, True)

            TB, PV, UN = TB_PAIR * CT, PV_PAIR * CT, UNITS * CT

            def mmax(w):
                dve.wait_ge(s_s, UN + w + 1)
                nc.vector.tensor_reduce(rmin[:, w % 2, :], pj[:, 2 + w % 2, :].rearrange("p (a k) -> p a k", a=2),
                                        AX.X, ALU.max).then_inc(s_dm, 1)
                dve.wait_ge(s_dm, 1 + UN + w + 1)
                nc.vector.tensor_scalar(rmin[:, w % 2, :], rmin[:, w % 2, :], -1.0, None, ALU.mult).then_inc(s_sp, 1)

            def mnormalise(w):
                dve.wait_ge(s_e, UN + w + 1)
                nc.vector.reciprocal(rinv[:, w % 2, :], rsum[:, w % 2, :]).then_inc(s_ri, 1)
                dve.wait_ge(s_ri, UN + w + 1)
                for a in range(2):
                    op = nc.vector.tensor_scalar(probs[:, w % 2, a * MEM:(a + 1) * MEM],
                                                 probs[:, w % 2, a * MEM:(a + 1) * MEM],
                                                 rinv[:, w % 2, a:a + 1], None, ALU.mult)
                op.then_inc(s_pn, 1)

            def mturned_lo(w):
                dve.wait_ge(s_thi, TB + w + 1)
                q = slice((w % 2) * P, (w % 2 + 1) * P)
                nc.vector.tensor_tensor(pT_lo[:, 0:2 * MT, q], pt[:, w % 2, :].rearrange("p (k q) -> p k q", q=P),
                                        pT_hi[:, 0:2 * MT, q], ALU.subtract).then_inc(s_tlo, 1)

            def mout(g):
                m, g2 = g // (NT // 2), g % (NT // 2)
                for a in range(2):
                    out_add(a, a, zm_raw[:, m, g2 * 2 * P:(g2 + 1) * 2 * P], PV + 2 * g + a)

            def mgate(m, gate):
                dve.wait_ge(s_oadd, PV + NT * (m + 1))
                nc.vector.scalar_tensor_tensor(out=zm_raw[:, m, :], in0=zm_raw[:, m, :], scalar=0.5, in1=gate[:, :],
                                               op0=ALU.mult, op1=ALU.mult).then_inc(s_zpre, 1)

            def a_half(ct, h, bank):
                s = S_A + 2 * ct
                dve.wait_ge(s_pj, 2 * s + 2 + h + 1)
                dve.wait_ge(s_xt, X_A + 2 * ct + h + 1)
                nc.vector.scalar_tensor_tensor(out=glu[:, ct, PAD_A + h * HALF:PAD_A + (h + 1) * HALF],
                                               in0=xt[:, hs(h)], scalar=1.0, in1=pj[:, bank, :],
                                               op0=ALU.add, op1=ALU.mult).then_inc(s_pjfree, 1)

            for ct in range(CT):
                op = nc.vector.memset(glu[:, ct, 0:PAD_A], 0.0)
            op.then_inc(s_ca, 1)
            nc.vector.tensor_scalar(cwa[:, :, :], cwa[:, :, :], 0.5, None, ALU.mult).then_inc(s_cw, 1)
            mmax(0)
            mnormalise(0)
            for w in range(2 * NT + 1):
                if w + 1 < 2 * NT:
                    mmax(w + 1)
                if w:
                    mturned_lo(w - 1)
                if w + 1 < 2 * NT:
                    mnormalise(w + 1)
                if w in (4, 5):
                    q_lo(w - 4, k_raw, q_stack1, STK_PAIR * CT + 2 + w - 4 + 1)
                for s, h in M_ENDS.get(w, ()):
                    if s == S_M:
                        gate_half(h, g_raw, X_M)
                    elif (s - S_A) % 2 == 0:
                        dve.wait_ge(s_xt, X_A + (s - S_A) + h + 1)
                        dve.sem_inc(s_pjfree, 1)
                    else:
                        a_half((s - S_A) // 2, h, h)
                if w % 2 == 0 and w:
                    mout(w // 2 - 1)
                if w == NT + 1:
                    mgate(0, v_raw)
            mgate(1, g_raw)
            for ct in range(CT):
                dve.wait_ge(s_zhi, ct + 1)
                nc.vector.tensor_tensor(z_lo[:, ct, :], z_raw[:, ct, :], z_hi[:, ct, :], ALU.subtract).then_inc(s_zlo, 1)
            for h in range(2):
                dve.wait_ge(s_xt, X_A + 2 * (CT - 1) + h + 1)
                dve.sem_inc(s_pjfree, 1)
            for m in range(MP):
                dve.wait_ge(s_zhi, CT + m + 1)
                nc.vector.tensor_tensor(zm_lo[:, m, :], zm_raw[:, m, :], zm_hi[:, m, :], ALU.subtract).then_inc(s_zlo, 1)
            for h in range(2):
                a_half(CT - 1, h, 2 + h)

            def conv_taps(ct, h, taps, unit):
                for n in taps:
                    src = glu[:, bass.ds(ct, 1), h * HALF + n:(h + 1) * HALF + n].rearrange("p o t -> p (o t)")
                    acc = sg[:, (n % 2) * HALF:(n % 2 + 1) * HALF]
                    if n == 0:
                        dve.wait_ge(s_ca, 1 + UNIT_STEPS * unit)
                        dve.wait_ge(s_cw, 1 + 2 * unit)
                        nc.vector.tensor_copy(cwk[:, 0:CONV_A], cwa[:, bass.ds(ct, 1), :].rearrange("p o t -> p (o t)")
                                              ).then_inc(s_cw, 1)
                        nc.vector.tensor_copy(cwk[:, CONV_A:CONV_A + 1], cab[:, bass.ds(ct, 1)]).then_inc(s_cw, 1)
                        dve.wait_ge(s_cw, 1 + 2 * unit + 2)
                        op = nc.vector.tensor_scalar(acc, src, cwk[:, 0:1], cwk[:, CONV_A:CONV_A + 1],
                                                     ALU.mult, ALU.add)
                    elif n == 1:
                        op = nc.vector.tensor_scalar(acc, src, cwk[:, 1:2], None, ALU.mult)
                    else:
                        dve.wait_ge(s_ca, 1 + UNIT_STEPS * unit + n - 1)
                        op = nc.vector.scalar_tensor_tensor(out=acc, in0=src, scalar=cwk[:, n:n + 1], in1=acc,
                                                            op0=ALU.mult, op1=ALU.add)
                    op.then_inc(s_ca, 1)

            def conv_sum(ct, h, unit):
                dst = glu[:, bass.ds(ct, 1), PAD_A + h * HALF:PAD_A + (h + 1) * HALF].rearrange("p o t -> p (o t)")
                dve.wait_ge(s_ca, 1 + UNIT_STEPS * unit + CONV_A)
                nc.vector.tensor_tensor(dst, sg[:, 0:HALF], sg[:, HALF:T], ALU.add).then_inc(s_ca, 1)

            def merge_step(s0, x0, d2, first=False, fresh=False, adds=0, conv=None):
                cuts = [range(0, CONV_A // 2), range(CONV_A // 2, CONV_A)]
                for e in range(2):
                    dt = 2 * d2 + e
                    if conv is not None:
                        conv_taps(d2, conv[0], cuts[e], conv[1] + d2)
                    for h in range(2):
                        if h == 0:
                            dve.wait_ge(s_xt, x0 + 2 * dt + 2)
                            if not first and not fresh:
                                dve.wait_ge(s_add, adds + dt - 1)
                        dve.wait_ge(s_pj, 2 * (s0 + 2 * dt + 1) + h + 1)
                        dst = merged[:, bass.ds(dt, 1), hs(h)].rearrange("p o t -> p (o t)") if first else ytmp[:, e, hs(h)]
                        nc.vector.scalar_tensor_tensor(out=dst, in0=xt[:, hs(h)], scalar=1.0, in1=pj[:, 2 + h, :],
                                                       op0=ALU.add, op1=ALU.mult).then_inc(s_pjfree, 2)
                if conv is not None:
                    conv_sum(d2, conv[0], conv[1] + d2)

            dve.wait_ge(s_pjfree, 2 * S_GC)
            with dve.Fori(0, DT // 2) as d2:
                merge_step(S_GC, X_GC, d2, first=True, conv=(1, 0))
            merge_step(S_GM, X_GM, 0, fresh=True, conv=(0, CT))
            with dve.Fori(1, DT // 2) as d2:
                merge_step(S_GM, X_GM, d2, conv=(0, CT))

            for ct in range(CT):
                dve.wait_ge(s_ah, ct + 1)
                nc.vector.tensor_tensor(z_lo[:, ct, :], glu[:, ct, PAD_A:WA], z_hi[:, ct, :],
                                        ALU.subtract).then_inc(s_al, 1)
            dve.wait_ge(s_lnm, 2)
            for ct in range(CT):
                for h in range(2):
                    v = glu[:, ct, PAD_A + h * HALF:PAD_A + (h + 1) * HALF]
                    op = nc.vector.tensor_tensor(v, v, pt[:, h, :], ALU.subtract)
                op.then_inc(s_lnc, 1)

            for ct in range(CT):
                dve.wait_ge(s_ah, CT + ct + 1)
                nc.vector.tensor_tensor(z_lo[:, ct, :], z_raw[:, ct, :], z_hi[:, ct, :], ALU.subtract).then_inc(s_al, 1)

            nc.vector.memset(prod[:, 0:PAD_B], 0.0).then_inc(s_cb, 1)
            with dve.Fori(0, CT) as ct:
                s = S_B + 4 * ct
                x0 = X_B + 4 * ct
                dve.wait_ge(s_xt, x0 + 2)
                for h in range(2):
                    dve.wait_ge(s_pj, 2 * (s + 1) + h + 1)
                    nc.vector.tensor_tensor(prod[:, PAD_B + h * HALF:PAD_B + (h + 1) * HALF], pj[:, 2 + h, :],
                                            xt[:, hs(h)], ALU.mult).then_inc(s_pjfree, 2)
                nc.vector.tensor_copy(cwk[:, 0:CONV_B], cwb[:, bass.ds(ct, 1), :].rearrange("p o t -> p (o t)")
                                      ).then_inc(s_cb, 1)
                dve.wait_ge(s_pjfree, 2 * s + 4)
                for n in range(CONV_B):
                    dve.wait_ge(s_cb, 1 + (CONV_B + 1) * ct + 1 + n)
                    if n == 0:
                        op = nc.vector.tensor_scalar(cv[:, :], prod[:, 0:T], cwk[:, 0:1], None, ALU.mult)
                    else:
                        op = nc.vector.scalar_tensor_tensor(out=cv[:, :], in0=prod[:, n:n + T], scalar=cwk[:, n:n + 1],
                                                            in1=cv[:, :], op0=ALU.mult, op1=ALU.add)
                    op.then_inc(s_cb, 1)
                gate_evac(s + 2, 2, x0 + 2)
                dve.wait_ge(s_cb, 1 + (CONV_B + 1) * (ct + 1))
                for h in range(2):
                    dve.wait_ge(s_pj, 2 * (s + 3) + h + 1)
                    nc.vector.tensor_tensor(bz[:, hs(h)], pj[:, 2 + h, :], cv[:, hs(h)], ALU.mult).then_inc(s_pjfree, 1)
                dve.wait_ge(s_pjfree, 2 * s + 8)
                nc.vector.scalar_tensor_tensor(out=bz[:, :], in0=bz[:, :], scalar=0.5, in1=sg[:, :],
                                               op0=ALU.mult, op1=ALU.mult).then_inc(s_zpre, 1)
                dve.wait_ge(s_zhi, CT + MP + ct + 1)
                nc.vector.tensor_tensor(z_lo[:, bass.ds(ct, 1), :].rearrange("p o t -> p (o t)"), bz[:, :],
                                        z_hi[:, bass.ds(ct, 1), :].rearrange("p o t -> p (o t)"),
                                        ALU.subtract).then_inc(s_zlo, 1)
            dve.wait_ge(s_sd, 1)
            nc.vector.reciprocal(an_rstd[:, :], sg[:, :]).then_inc(s_rs, 1)
            dve.wait_ge(s_rs, 1)
            dve.wait_ge(s_lnc, CT)
            for ct in range(CT):
                v = glu[:, ct, PAD_A:WA]
                nc.vector.tensor_tensor(v, v, an_rstd[:, :], ALU.mult).then_inc(s_an, 1)
            merge_step(S_GB, X_GB, 0, adds=DT)
            for ct in range(CT):
                v = glu[:, ct, PAD_A:WA]
                dve.wait_ge(s_at, ct + 1)
                nc.vector.scalar_tensor_tensor(out=v, in0=an_rstd[:, :], scalar=1.0, in1=v, op0=ALU.add,
                                               op1=ALU.mult).then_inc(s_as, 1)
            with dve.Fori(1, DT // 2) as d2:
                merge_step(S_GB, X_GB, d2, adds=DT)

            dve.wait_ge(s_as, CT)
            with dve.Fori(0, CT // 2) as i:
                for j in range(2):
                    ct = 2 * i + j
                    dve.wait_ge(s_zlo, 2 * CT + MP + ct)
                    gate_evac(S_AG + ct, j, X_AG + 2 * ct)
                    dve.wait_ge(s_pjfree, 2 * (S_AG + ct + 1))
                    v = glu[:, bass.ds(ct, 1), PAD_A:WA].rearrange("p o t -> p (o t)")
                    nc.vector.scalar_tensor_tensor(out=sg[:, :], in0=sg[:, :], scalar=0.25, in1=v,
                                                   op0=ALU.mult, op1=ALU.mult).then_inc(s_zpre, 1)
                    dve.wait_ge(s_zhi, 2 * CT + MP + ct + 1)
                    nc.vector.tensor_tensor(z_lo[:, bass.ds(ct, 1), :].rearrange("p o t -> p (o t)"), sg[:, :],
                                            z_hi[:, bass.ds(ct, 1), :].rearrange("p o t -> p (o t)"),
                                            ALU.subtract).then_inc(s_zlo, 1)
            with dve.Fori(0, DT // 2) as d2:
                merge_step(S_GA, X_GA, d2, adds=2 * DT)

            for k in range(KT):
                if k:
                    dve.wait_ge(s_woh, k + 1)
                    dve.wait_ge(s_wol, k)
                    nc.vector.tensor_tensor(wout_lo[:, k, :], wout_raw[:, k, :], wout_hi[:, k, :],
                                            ALU.subtract).then_inc(s_wol, 1)
                else:
                    dve.wait_ge(s_pj, 2 * S_END)
                dve.wait_ge(s_gh, k + 1)
                nc.vector.scalar_tensor_tensor(out=xT_lo[:, k, :], in0=merged[:, k, :], scalar=0.5,
                                               in1=xT_hi[:, k, :] if k else merged_hi0[:, :],
                                               op0=ALU.mult, op1=ALU.subtract).then_inc(s_gl, 1)
            dve.wait_ge(s_lnp, 32)
            for t in range(NT):
                q = t % 2
                if t >= 2:
                    dve.wait_ge(s_store[q], 16 * (t // 2))
                dve.wait_ge(s_xtk[q], 16 * (t // 2 + 1))
                for h in range(2):
                    dve.wait_ge(s_out_pj, 2 * t + h + 1)
                    nc.vector.scalar_tensor_tensor(out=y_tok[:, q, hs(h)], in0=x_tok[:, q, hs(h)], scalar=ALPHA,
                                                   in1=pj[:, (2 * t + h) % 4, :], op0=ALU.mult,
                                                   op1=ALU.add).then_inc(s_yk, 1)
                dve.wait_ge(s_yk, 2 * t + 2)
                for h in range(2):
                    op = nc.vector.bn_stats(stats[:, q, h, :], y_tok[:, q, hs(h)])
                op.then_inc(s_st, 1)
                dve.wait_ge(s_st, 1 + t + 1)
                nc.vector.bn_aggr(mv[:, q, :], stats[:, q, :, :]).then_inc(s_mvr, 1)
                dve.wait_ge(s_osd, t + 1)
                nc.vector.reciprocal(rinv[:, q, 0:1], rstd[:, q:q + 1]).then_inc(s_ors, 1)
                nc.vector.scalar_tensor_tensor(out=y_tok[:, q, :], in0=y_tok[:, q, :], scalar=mv[:, q, 0:1],
                                               in1=lng_b[:, :], op0=ALU.subtract, op1=ALU.mult).then_inc(s_t1, 1)
                dve.wait_ge(s_ors, t + 1)
                dve.wait_ge(s_t1, t + 1)
                nc.vector.scalar_tensor_tensor(out=y_tok[:, q, :], in0=y_tok[:, q, :], scalar=rinv[:, q, 0:1],
                                               in1=lnb_b[:, :], op0=ALU.mult, op1=ALU.add).then_inc(s_yo, 1)


def kernel(**inputs):
    import numpy as np
    import concourse.bacc as bacc
    from concourse.bass_utils import run_bass_kernel_spmd

    def one(name):
        return np.ascontiguousarray(np.asarray(inputs[name])[0])

    def columns(v):
        return np.ascontiguousarray(v.reshape(-1, P).T)

    x = one("x")
    arrays = {
        "xT": np.ascontiguousarray(x.T), "x": x, "mem": one("mem"), "w_in": one("w_in"),
        "b_forget": one("b_forget"), "conv_a_wT": np.ascontiguousarray(one("conv_a_w").T),
        "conv_a_b": columns(one("conv_a_b")), "ln_a_g": columns(one("ln_a_g")), "ln_a_b": columns(one("ln_a_b")),
        "conv_b_wT": np.ascontiguousarray(one("conv_b_w").T), "w_kv_mem": one("w_kv_mem"),
        "mem_ln_g": columns(np.asarray(inputs["mem_ln_g"])), "mem_ln_b": columns(np.asarray(inputs["mem_ln_b"])),
        "p_a": one("p_a"), "p_b": one("p_b"), "p_c": one("p_c"), "p_m": one("p_m"), "w_out": one("w_out"),
        "ln_g": one("ln_g"), "ln_b": one("ln_b"),
    }
    nc = bacc.Bacc("TRN2", target_bir_lowering=False, num_devices=1)
    args = {name: nc.dram_tensor(f"in_{name}", a.shape, F32, kind="ExternalInput").ap() for name, a in arrays.items()}
    out = nc.dram_tensor("out_y", x.shape, F32, kind="ExternalOutput").ap()
    hybrid_mixer(nc, out=out, **args)
    r = run_bass_kernel_spmd(nc, [{f"in_{name}": a for name, a in arrays.items()}], core_ids=[0])
    return r.results[0]["out_y"].reshape(inputs["x"].shape)
```
